# Optimizing a Trainium2 kernel written in Bass

```python
import jax, jax.numpy as jnp
from jax import lax
import numpy as np
import math

D_MODEL = 1024
BATCH = 1
SEQ = 256
DEPTH = 2

NORM_EPS = 1e-6
ROPE_THETA = 10000.0
Q_BLOCK = 128

A_HEADS = 8
A_HEAD_DIM = 64
IDX_HEADS = 8
IDX_DIM = 64
DSA_TOPK_MAX = 256

B_HEADS = 8
B_HEAD_DIM = 64
MOBA_BLOCK = 256
MOBA_TOPK = 3
MOBA_Q_CHUNK = 16

EVEN_COLS = (A_HEADS * A_HEAD_DIM,
             A_HEAD_DIM,
             A_HEAD_DIM,
             IDX_HEADS * IDX_DIM,
             IDX_DIM,
             IDX_HEADS,
             B_HEADS * B_HEAD_DIM,
             B_HEADS * B_HEAD_DIM,
             B_HEADS * B_HEAD_DIM)
EVEN_IN_COLS = int(sum(EVEN_COLS))
EVEN_SPLITS = tuple(int(c) for c in np.cumsum(EVEN_COLS)[:-1])
EVEN_OUT_COLS = A_HEADS * A_HEAD_DIM + B_HEADS * B_HEAD_DIM

C_HEADS = 16
C_NOPE = 64
C_ROPE = 32
C_V = 64
C_Q_RANK = 768
C_KV_RANK = 256
C_IN_COLS = C_Q_RANK + C_KV_RANK + C_ROPE

PEER_HEADS = 8
PEER_NKEYS = 128
PEER_N_EXPERTS = PEER_NKEYS * PEER_NKEYS
PEER_QDIM = 256
PEER_TOPK_HALF = 16
PEER_TOPK = 16
PEER_CHUNK = 128

N_EVEN = (DEPTH + 1) // 2
N_ODD = DEPTH // 2


def rms_norm(x, g):
    xf = x.astype(jnp.float32)
    y = xf * lax.rsqrt(jnp.mean(xf * xf, axis=-1, keepdims=True) + NORM_EPS)
    return (y * g.astype(jnp.float32)).astype(x.dtype)

def rope_tables(positions, dim):
    inv = 1.0 / (ROPE_THETA ** (jnp.arange(0, dim, 2, dtype=jnp.float32) / dim))
    ang = positions.astype(jnp.float32)[..., None] * inv
    return jnp.cos(ang)[:, :, None, :], jnp.sin(ang)[:, :, None, :]

def apply_rope(x, cos, sin):
    x1, x2 = jnp.split(x, 2, axis=-1)
    c = cos.astype(x.dtype)
    s = sin.astype(x.dtype)
    return jnp.concatenate([x1 * c - x2 * s, x1 * s + x2 * c], axis=-1)

def to_blocks(a, blk):
    b, s = a.shape[:2]
    return jnp.moveaxis(a.reshape((b, s // blk, blk) + a.shape[2:]), 1, 0)

def from_blocks(a):
    a = jnp.moveaxis(a, 0, 1)
    return a.reshape((a.shape[0], a.shape[1] * a.shape[2]) + a.shape[3:])

def dsa_attention(q, k, v, iq, ik, iw):
    b, s = q.shape[:2]
    n_sel = min(DSA_TOPK_MAX, s // 4)
    key_pos = jnp.arange(s)
    w_scale = (IDX_HEADS ** -0.5) * (IDX_DIM ** -0.5)
    a_scale = A_HEAD_DIM ** -0.5
    gather = jax.vmap(lambda t, i: t[i])

    def one_block(args):
        blk, qb, iqb, iwb = args
        q_pos = blk * Q_BLOCK + jnp.arange(Q_BLOCK)
        causal = key_pos[None, :] <= q_pos[:, None]
        logits = jnp.einsum('bqhd,bsd->bqhs', iqb, ik).astype(jnp.float32)
        score = jnp.einsum('bqhs,bqh->bqs', jax.nn.relu(logits), iwb.astype(jnp.float32)) * w_scale
        score = jnp.where(causal[None], score, -jnp.inf)
        _, sel = lax.top_k(score, n_sel)
        k_sel = gather(k, sel)
        v_sel = gather(v, sel)
        valid = sel <= q_pos[None, :, None]
        sc = jnp.einsum('bqhd,bqnd->bqhn', qb, k_sel).astype(jnp.float32) * a_scale
        sc = jnp.where(valid[:, :, None, :], sc, -jnp.inf)
        p = jax.nn.softmax(sc, axis=-1).astype(v.dtype)
        return jnp.einsum('bqhn,bqnd->bqhd', p, v_sel)

    nblk = s // Q_BLOCK
    out = lax.map(one_block, (jnp.arange(nblk), to_blocks(q, Q_BLOCK),
                              to_blocks(iq, Q_BLOCK), to_blocks(iw, Q_BLOCK)))
    return from_blocks(out)

def moba_attention(q, k, v):
    b, s, h, d = q.shape
    nb = -(-s // MOBA_BLOCK)
    pad = nb * MOBA_BLOCK - s

    def blocks(a):
        a = jnp.pad(a, ((0, 0), (0, pad), (0, 0), (0, 0)))
        return a.reshape(b, nb, MOBA_BLOCK, h, d).transpose(0, 3, 1, 2, 4)

    kb = blocks(k)
    vb = blocks(v)
    k_mean = jnp.mean(kb.astype(jnp.float32), axis=3).astype(k.dtype)
    n_top = min(MOBA_TOPK, nb - 1)
    scale = d ** -0.5
    blk_ids = jnp.arange(nb)
    key_in_blk = jnp.arange(MOBA_BLOCK)
    gather = jax.vmap(jax.vmap(lambda t, i: t[i]))

    def one_chunk(args):
        c, qc = args
        q_pos = c * MOBA_Q_CHUNK + jnp.arange(MOBA_Q_CHUNK)
        own = (c * MOBA_Q_CHUNK) // MOBA_BLOCK
        k_own = lax.dynamic_index_in_dim(kb, own, axis=2, keepdims=False)
        v_own = lax.dynamic_index_in_dim(vb, own, axis=2, keepdims=False)
        s_own = jnp.einsum('bqhd,bhkd->bhqk', qc, k_own).astype(jnp.float32) * scale
        s_own = jnp.where((own * MOBA_BLOCK + key_in_blk)[None, :] <= q_pos[:, None], s_own, -jnp.inf)
        if n_top == 0:
            p = jax.nn.softmax(s_own, axis=-1).astype(v.dtype)
            return jnp.einsum('bhqk,bhkd->bqhd', p, v_own)
        gate = jnp.einsum('bqhd,bhnd->bhqn', qc, k_mean).astype(jnp.float32)
        gate = jnp.where(blk_ids < own, gate, -jnp.inf)
        _, sel = lax.top_k(gate, n_top)
        k_sel = gather(kb, sel)
        v_sel = gather(vb, sel)
        s_past = jnp.einsum('bqhd,bhqnkd->bhqnk', qc, k_sel).astype(jnp.float32) * scale
        s_past = jnp.where((sel < own)[..., None], s_past, -jnp.inf)
        s_past = s_past.reshape(b, h, MOBA_Q_CHUNK, n_top * MOBA_BLOCK)
        p = jax.nn.softmax(jnp.concatenate([s_past, s_own], axis=-1), axis=-1).astype(v.dtype)
        p_past = p[..., :n_top * MOBA_BLOCK].reshape(b, h, MOBA_Q_CHUNK, n_top, MOBA_BLOCK)
        p_own = p[..., n_top * MOBA_BLOCK:]
        return (jnp.einsum('bhqnk,bhqnkd->bqhd', p_past, v_sel)
                + jnp.einsum('bhqk,bhkd->bqhd', p_own, v_own))

    nchunk = s // MOBA_Q_CHUNK
    out = lax.map(one_chunk, (jnp.arange(nchunk), to_blocks(q, MOBA_Q_CHUNK)))
    return from_blocks(out)

def even_mixer(h, cos64, sin64, w_in, w_out):
    b, s, _ = h.shape
    qa, ka, va, iq, ik, iw, qb, kb, vb = jnp.split(h @ w_in, EVEN_SPLITS, axis=-1)
    qa = apply_rope(qa.reshape(b, s, A_HEADS, A_HEAD_DIM), cos64, sin64)
    ka = apply_rope(ka[:, :, None, :], cos64, sin64)[:, :, 0]
    iq = apply_rope(iq.reshape(b, s, IDX_HEADS, IDX_DIM), cos64, sin64)
    ik = apply_rope(ik[:, :, None, :], cos64, sin64)[:, :, 0]
    out_a = dsa_attention(qa, ka, va, iq, ik, iw)
    qb = apply_rope(qb.reshape(b, s, B_HEADS, B_HEAD_DIM), cos64, sin64)
    kb = apply_rope(kb.reshape(b, s, B_HEADS, B_HEAD_DIM), cos64, sin64)
    vb = vb.reshape(b, s, B_HEADS, B_HEAD_DIM)
    out_b = moba_attention(qb, kb, vb)
    o = jnp.concatenate([out_a.reshape(b, s, A_HEADS * A_HEAD_DIM),
                         out_b.reshape(b, s, B_HEADS * B_HEAD_DIM)], axis=-1)
    return o @ w_out

def mla_attention(q_nope, q_rope, k_nope, k_rope, v):
    s = q_nope.shape[1]
    key_pos = jnp.arange(s)
    scale = (C_NOPE + C_ROPE) ** -0.5

    def one_block(args):
        blk, qn, qr = args
        q_pos = blk * Q_BLOCK + jnp.arange(Q_BLOCK)
        sc = (jnp.einsum('bqhd,bshd->bhqs', qn, k_nope)
              + jnp.einsum('bqhd,bsd->bhqs', qr, k_rope)).astype(jnp.float32) * scale
        sc = jnp.where(key_pos[None, :] <= q_pos[:, None], sc, -jnp.inf)
        p = jax.nn.softmax(sc, axis=-1).astype(v.dtype)
        return jnp.einsum('bhqs,bshd->bqhd', p, v)

    nblk = s // Q_BLOCK
    out = lax.map(one_block, (jnp.arange(nblk), to_blocks(q_nope, Q_BLOCK), to_blocks(q_rope, Q_BLOCK)))
    return from_blocks(out)

def mla_mixer(h, cos32, sin32, w_in, q_norm, kv_norm, w_uq, w_ukv, w_out):
    b, s, _ = h.shape
    cq, ckv, kr = jnp.split(h @ w_in, [C_Q_RANK, C_Q_RANK + C_KV_RANK], axis=-1)
    q = (rms_norm(cq, q_norm) @ w_uq).reshape(b, s, C_HEADS, C_NOPE + C_ROPE)
    q_nope, q_rope = jnp.split(q, [C_NOPE], axis=-1)
    q_rope = apply_rope(q_rope, cos32, sin32)
    kv = (rms_norm(ckv, kv_norm) @ w_ukv).reshape(b, s, C_HEADS, C_NOPE + C_V)
    k_nope, v = jnp.split(kv, [C_NOPE], axis=-1)
    k_rope = apply_rope(kr[:, :, None, :], cos32, sin32)[:, :, 0]
    o = mla_attention(q_nope, q_rope, k_nope, k_rope, v)
    return o.reshape(b, s, C_HEADS * C_V) @ w_out

def peer_ffn(h, w_q, sub_keys, u_tab, v_tab):
    b, s, d = h.shape
    tokens = h.reshape(b * s // PEER_CHUNK, PEER_CHUNK, d)

    def one_chunk(xc):
        t = xc.shape[0]
        q = (xc @ w_q).reshape(t, PEER_HEADS, 2, PEER_QDIM // 2)
        sc = jnp.einsum('thpc,hpnc->thpn', q, sub_keys).astype(jnp.float32)
        v_half, i_half = lax.top_k(sc, PEER_TOPK_HALF)
        cand = (v_half[:, :, 0, :, None] + v_half[:, :, 1, None, :]).reshape(t, PEER_HEADS, -1)
        cand_idx = (i_half[:, :, 0, :, None] * PEER_NKEYS + i_half[:, :, 1, None, :]).reshape(t, PEER_HEADS, -1)
        top_s, pos = lax.top_k(cand, PEER_TOPK)
        expert = jnp.take_along_axis(cand_idx, pos, axis=-1)
        g = jax.nn.softmax(top_s, axis=-1)
        u = u_tab[expert]
        act = jax.nn.gelu(jnp.einsum('thkd,td->thk', u, xc).astype(jnp.float32), approximate=False)
        w = (g * act).astype(xc.dtype)
        return jnp.einsum('thk,thkd->td', w, v_tab[expert])

    return lax.map(one_chunk, tokens).reshape(b, s, d)

def first_inputs(seed: int = 0) -> dict:
    key = jax.random.key(seed)
    ks = jax.random.split(key, 20)
    f32 = jnp.float32

    def nrm(k, shape, scale):
        return jax.random.normal(k, shape, f32) * scale

    def gain(k, shape):
        return 1.0 + 0.02 * jax.random.normal(k, shape, f32)

    return {
        'x': jax.random.normal(ks[0], (BATCH, SEQ, D_MODEL), f32),
        'positions': jnp.broadcast_to(jnp.arange(SEQ, dtype=jnp.int32)[None, :], (BATCH, SEQ)),
        'attn_norm': gain(ks[1], (DEPTH, D_MODEL)),
        'ffn_norm': gain(ks[2], (DEPTH, D_MODEL)),
        'final_norm': gain(ks[3], (D_MODEL,)),
        'hyb_w_in': nrm(ks[4], (N_EVEN, D_MODEL, EVEN_IN_COLS), D_MODEL ** -0.5),
        'hyb_w_out': nrm(ks[5], (N_EVEN, EVEN_OUT_COLS, D_MODEL), EVEN_OUT_COLS ** -0.5),
        'mla_w_in': nrm(ks[6], (N_ODD, D_MODEL, C_IN_COLS), D_MODEL ** -0.5),
        'mla_q_norm': gain(ks[7], (N_ODD, C_Q_RANK)),
        'mla_kv_norm': gain(ks[8], (N_ODD, C_KV_RANK)),
        'mla_w_uq': nrm(ks[9], (N_ODD, C_Q_RANK, C_HEADS * (C_NOPE + C_ROPE)), C_Q_RANK ** -0.5),
        'mla_w_ukv': nrm(ks[10], (N_ODD, C_KV_RANK, C_HEADS * (C_NOPE + C_V)), C_KV_RANK ** -0.5),
        'mla_w_out': nrm(ks[11], (N_ODD, C_HEADS * C_V, D_MODEL), (C_HEADS * C_V) ** -0.5),
        'peer_w_q': nrm(ks[12], (DEPTH, D_MODEL, PEER_HEADS * PEER_QDIM), D_MODEL ** -0.5),
        'peer_sub_keys': nrm(ks[13], (DEPTH, PEER_HEADS, 2, PEER_NKEYS, PEER_QDIM // 2), (PEER_QDIM // 2) ** -0.5),
        'peer_u': nrm(ks[14], (DEPTH, PEER_N_EXPERTS, D_MODEL), D_MODEL ** -0.5),
        'peer_v': nrm(ks[15], (DEPTH, PEER_N_EXPERTS, D_MODEL), D_MODEL ** -0.5),
    }

def first_block(x, positions, attn_norm, ffn_norm, final_norm, hyb_w_in, hyb_w_out,
              mla_w_in, mla_q_norm, mla_kv_norm, mla_w_uq, mla_w_ukv, mla_w_out,
              peer_w_q, peer_sub_keys, peer_u, peer_v):
    cos64, sin64 = rope_tables(positions, A_HEAD_DIM)
    cos32, sin32 = rope_tables(positions, C_ROPE)
    for i in range(DEPTH):
        h = rms_norm(x, attn_norm[i])
        j = i // 2
        if i % 2 == 0:
            x = x + even_mixer(h, cos64, sin64, hyb_w_in[j], hyb_w_out[j])
        else:
            x = x + mla_mixer(h, cos32, sin32, mla_w_in[j], mla_q_norm[j], mla_kv_norm[j],
                              mla_w_uq[j], mla_w_ukv[j], mla_w_out[j])
        h = rms_norm(x, ffn_norm[i])
        x = x + peer_ffn(h, peer_w_q[i], peer_sub_keys[i], peer_u[i], peer_v[i])
    return rms_norm(x, final_norm)


DEPTH_2 = 1

HEAD_DIM = 64
BLOCK_Q = 128
N_SB_HEADS = 4
DIL_PATTERNS = ((128, 1), (512, 4), (2048, 16))
N_DIL_GROUPS = len(DIL_PATTERNS)
N_DIL_HEADS = 4
N_FOX_HEADS = 4
N_DIFF_HEADS = 4
DIFF_QK_DIM = HEAD_DIM // 2
N_BRANCH = 4
BRANCH_WIDTH = 4 * HEAD_DIM
D_FF = 4 * D_MODEL
RMS_EPS = 1e-6
N_ALIBI = N_DIL_GROUPS * N_DIL_HEADS + N_DIFF_HEADS

SB_W = N_SB_HEADS * HEAD_DIM
DIL_W = N_DIL_GROUPS * N_DIL_HEADS * HEAD_DIM
FOX_W = N_FOX_HEADS * HEAD_DIM
DIFF_QK_W = N_DIFF_HEADS * 2 * DIFF_QK_DIM
DIFF_V_W = N_DIFF_HEADS * HEAD_DIM
GATE_W = N_BRANCH * D_MODEL
SPLIT_SIZES = (SB_W,) * 3 + (DIL_W,) * 3 + (FOX_W,) * 3 + (N_FOX_HEADS,) + (DIFF_QK_W, DIFF_QK_W, DIFF_V_W) + (GATE_W,)
D_IN = sum(SPLIT_SIZES)
SPLIT_OFFSETS = tuple(sum(SPLIT_SIZES[:i + 1]) for i in range(len(SPLIT_SIZES) - 1))


def rms_norm_2(x, g):
    xf = x.astype(jnp.float32)
    y = xf * lax.rsqrt(jnp.mean(xf * xf, axis=-1, keepdims=True) + RMS_EPS)
    return (y * g.astype(jnp.float32)).astype(x.dtype)

def alibi_slopes():
    return jnp.asarray(2.0 ** (-8.0 * np.arange(1, N_ALIBI + 1) / N_ALIBI), dtype=jnp.float32)

def _stick_breaking(q_blk, k, v, dist):
    z = jnp.einsum('bqhd,bshd->bhqs', q_blk, k).astype(jnp.float32) * (HEAD_DIM ** -0.5)
    strict = dist > 0
    log_keep = jnp.where(strict, jax.nn.log_sigmoid(-z), 0.0)
    log_between = lax.cumsum(log_keep, axis=3, reverse=True) - log_keep
    a = jnp.where(strict, jnp.exp(jax.nn.log_sigmoid(z) + log_between), 0.0)
    return jnp.einsum('bhqs,bshd->bqhd', a.astype(v.dtype), v)

def _dilated(q_blk, k, v, t_idx, slopes):
    outs, lses = [], []
    for g, (window, dil) in enumerate(DIL_PATTERNS):
        dists = dil * jnp.arange(window // dil + 1)
        idx = t_idx[:, None] - dists[None, :]
        valid = idx >= 0
        idx = jnp.maximum(idx, 0)
        kg = jnp.take(k[:, :, g], idx, axis=1)
        vg = jnp.take(v[:, :, g], idx, axis=1)
        s = jnp.einsum('bqhd,bqnhd->bhqn', q_blk[:, :, g], kg).astype(jnp.float32) * (HEAD_DIM ** -0.5)
        s = s - slopes[g][:, None, None] * dists.astype(jnp.float32)
        s = jnp.where(valid, s, -jnp.inf)
        lse = jax.nn.logsumexp(s, axis=-1)
        p = jnp.exp(s - lse[..., None])
        outs.append(jnp.einsum('bhqn,bqnhd->bqhd', p.astype(v.dtype), vg))
        lses.append(lse)
    alpha = jax.nn.softmax(jnp.stack(lses, axis=0), axis=0)
    alpha = jnp.transpose(alpha, (0, 1, 3, 2))[..., None]
    return jnp.sum(alpha.astype(v.dtype) * jnp.stack(outs, axis=0), axis=0)

def _forgetting(q_blk, k, v, cum_blk, cum, dist):
    s = jnp.einsum('bqhd,bshd->bhqs', q_blk, k).astype(jnp.float32) * (HEAD_DIM ** -0.5)
    s = s + jnp.transpose(cum_blk, (0, 2, 1))[..., None] - jnp.transpose(cum, (0, 2, 1))[:, :, None, :]
    p = jax.nn.softmax(jnp.where(dist >= 0, s, -jnp.inf), axis=-1)
    return jnp.einsum('bhqs,bshd->bqhd', p.astype(v.dtype), v)

def _differential(q_blk, k, v, dist, slopes, lam):
    s = jnp.einsum('bqhcd,bshcd->bchqs', q_blk, k).astype(jnp.float32) * (DIFF_QK_DIM ** -0.5)
    s = s - slopes[:, None, None] * dist.astype(jnp.float32)
    p = jax.nn.softmax(jnp.where(dist >= 0, s, -jnp.inf), axis=-1)
    w = p[:, 0] - lam * p[:, 1]
    return jnp.einsum('bhqs,bshd->bqhd', w.astype(v.dtype), v)

def _token_mixers(h, w_in, b_forget, lam, diff_g, diff_out_scale, slopes_dil, slopes_diff):
    bsz, seq, _ = h.shape
    proj = h @ w_in
    (qa, ka, va, qb, kb, vb, qc, kc, vc, f_logit, qd, kd, vd, gate_logit) = jnp.split(proj, SPLIT_OFFSETS, axis=-1)
    qa, ka, va = (a.reshape(bsz, seq, N_SB_HEADS, HEAD_DIM) for a in (qa, ka, va))
    qb, kb, vb = (a.reshape(bsz, seq, N_DIL_GROUPS, N_DIL_HEADS, HEAD_DIM) for a in (qb, kb, vb))
    qc, kc, vc = (a.reshape(bsz, seq, N_FOX_HEADS, HEAD_DIM) for a in (qc, kc, vc))
    qd, kd = (a.reshape(bsz, seq, N_DIFF_HEADS, 2, DIFF_QK_DIM) for a in (qd, kd))
    vd = vd.reshape(bsz, seq, N_DIFF_HEADS, HEAD_DIM)
    log_f = jax.nn.log_sigmoid(f_logit.astype(jnp.float32) + b_forget.astype(jnp.float32))
    cum = jnp.cumsum(log_f, axis=1)
    s_idx = jnp.arange(seq)

    def block(q0):
        t_idx = q0 + jnp.arange(BLOCK_Q)
        dist = t_idx[:, None] - s_idx[None, :]
        sl = lambda a: lax.dynamic_slice_in_dim(a, q0, BLOCK_Q, axis=1)
        return (_stick_breaking(sl(qa), ka, va, dist),
                _dilated(sl(qb), kb, vb, t_idx, slopes_dil),
                _forgetting(sl(qc), kc, vc, sl(cum), cum, dist),
                _differential(sl(qd), kd, vd, dist, slopes_diff, lam))

    o_a, o_b, o_c, o_d = lax.map(block, jnp.arange(seq // BLOCK_Q) * BLOCK_Q)
    unblock = lambda o: jnp.moveaxis(o, 0, 1).reshape(bsz, seq, o.shape[3], o.shape[4])
    o_d = rms_norm_2(unblock(o_d), diff_g) * diff_out_scale
    ys = jnp.stack([unblock(o_a), unblock(o_b), unblock(o_c), o_d], axis=2)
    return ys.reshape(bsz, seq, N_BRANCH, BRANCH_WIDTH), gate_logit

def second_inputs(seed: int = 0) -> dict:
    key = jax.random.key(seed)
    ks = jax.random.split(key, 16)
    nrm = lambda k, shape, scale: jax.random.normal(k, shape, jnp.float32) * scale
    return {
        'x': nrm(ks[0], (BATCH, SEQ, D_MODEL), 1.0),
        'mix_norm_g': 1.0 + nrm(ks[1], (DEPTH_2, D_MODEL), 0.05),
        'w_in': nrm(ks[2], (DEPTH_2, D_MODEL, D_IN), D_MODEL ** -0.5),
        'b_forget': jax.random.uniform(ks[3], (DEPTH_2, N_FOX_HEADS), jnp.float32, 1.0, 4.0),
        'lambda_q1': nrm(ks[4], (DEPTH_2, DIFF_QK_DIM), 0.1),
        'lambda_k1': nrm(ks[5], (DEPTH_2, DIFF_QK_DIM), 0.1),
        'lambda_q2': nrm(ks[6], (DEPTH_2, DIFF_QK_DIM), 0.1),
        'lambda_k2': nrm(ks[7], (DEPTH_2, DIFF_QK_DIM), 0.1),
        'diff_norm_g': 1.0 + nrm(ks[8], (DEPTH_2, HEAD_DIM), 0.05),
        'w_branch': nrm(ks[9], (DEPTH_2, N_BRANCH, BRANCH_WIDTH, D_MODEL), BRANCH_WIDTH ** -0.5),
        'w_out': nrm(ks[10], (DEPTH_2, D_MODEL, D_MODEL), D_MODEL ** -0.5),
        'mlp_norm_g': 1.0 + nrm(ks[11], (DEPTH_2, D_MODEL), 0.05),
        'w_up': nrm(ks[12], (DEPTH_2, D_MODEL, D_FF), D_MODEL ** -0.5),
        'w_down': nrm(ks[13], (DEPTH_2, D_FF, D_MODEL), D_FF ** -0.5),
        'final_norm_g': 1.0 + nrm(ks[14], (D_MODEL,), 0.05),
    }

def second_block(x, mix_norm_g, w_in, b_forget, lambda_q1, lambda_k1, lambda_q2, lambda_k2, diff_norm_g, w_branch, w_out, mlp_norm_g, w_up, w_down, final_norm_g):
    bsz, seq, _ = x.shape
    slopes = alibi_slopes()
    n0, n1 = N_DIL_HEADS, N_DIL_HEADS + N_DIFF_HEADS
    slopes_dil = jnp.stack([slopes[:n0], slopes[n1:n1 + N_DIL_HEADS], slopes[n1 + N_DIL_HEADS:]], axis=0)
    slopes_diff = slopes[n0:n1]
    for l in range(DEPTH_2):
        lambda_init = 0.8 - 0.6 * math.exp(-0.3 * l)
        lam = (jnp.exp(jnp.sum(lambda_q1[l].astype(jnp.float32) * lambda_k1[l].astype(jnp.float32)))
               - jnp.exp(jnp.sum(lambda_q2[l].astype(jnp.float32) * lambda_k2[l].astype(jnp.float32))) + lambda_init)
        h = rms_norm_2(x, mix_norm_g[l])
        ys, gate_logit = _token_mixers(h, w_in[l], b_forget[l], lam, diff_norm_g[l], 1.0 - lambda_init, slopes_dil, slopes_diff)
        branch = jnp.einsum('bsnc,ncd->bsnd', ys, w_branch[l])
        gates = jax.nn.sigmoid(gate_logit.reshape(bsz, seq, N_BRANCH, D_MODEL))
        x = x + jnp.sum(gates * branch, axis=2) @ w_out[l]
        h = rms_norm_2(x, mlp_norm_g[l])
        x = x + jnp.square(jax.nn.relu(h @ w_up[l])) @ w_down[l]
    return rms_norm_2(x, final_norm_g)


def setup_inputs(seed=0):
    out = dict(first_inputs(seed))
    for name, value in second_inputs(seed + 1).items():
        if name != "x":
            out[name + "_2"] = value
    return out


def reference(
    x, positions, attn_norm, ffn_norm, final_norm, hyb_w_in, hyb_w_out, mla_w_in, mla_q_norm,
    mla_kv_norm, mla_w_uq, mla_w_ukv, mla_w_out, peer_w_q, peer_sub_keys, peer_u, peer_v,
    mix_norm_g_2, w_in_2, b_forget_2, lambda_q1_2, lambda_k1_2, lambda_q2_2, lambda_k2_2,
    diff_norm_g_2, w_branch_2, w_out_2, mlp_norm_g_2, w_up_2, w_down_2, final_norm_g_2,
):
    x = first_block(
        x, positions, attn_norm, ffn_norm, final_norm, hyb_w_in, hyb_w_out, mla_w_in,
        mla_q_norm, mla_kv_norm, mla_w_uq, mla_w_ukv, mla_w_out, peer_w_q, peer_sub_keys,
        peer_u, peer_v,
    )
    return second_block(
        x, mix_norm_g_2, w_in_2, b_forget_2, lambda_q1_2, lambda_k1_2, lambda_q2_2, lambda_k2_2,
        diff_norm_g_2, w_branch_2, w_out_2, mlp_norm_g_2, w_up_2, w_down_2, final_norm_g_2,
    )


_drawn_inputs = setup_inputs


def setup_inputs(seed=0):
    import zlib

    import numpy as np

    out = dict(_drawn_inputs(seed))
    spreads = {}
    factors = {'ffn_norm': 8.0,
     'mla_q_norm': 8.0,
     'mla_kv_norm': 7.363,
     'lambda_k1_2': 26.528,
     'lambda_q2_2': 2.801,
     'lambda_k2_2': 3.693,
     'diff_norm_g_2': 2.895}
    for name, (base, spread) in spreads.items():
        noise = np.random.default_rng([zlib.crc32(name.encode()), seed]).standard_normal(out[name].shape)
        drawn = base * np.exp(spread * noise) if base else spread * noise
        out[name] = __import__('jax').numpy.asarray(drawn.astype(out[name].dtype))
    for name, factor in factors.items():
        out[name] = (out[name] * factor).astype(out[name].dtype)
    return out
```

```python
from contextlib import ExitStack

import numpy as np

import concourse.bass as bass
from concourse import mybir

ALU = mybir.AluOpType
ACT = mybir.ActivationFunctionType
F32 = mybir.dt.float32
I32 = mybir.dt.int32
U32 = mybir.dt.uint32
AX = mybir.AxisListType

P = 128
SEQ = 256
TILES = SEQ // P
D = 1024
DC = D // P
EPS = 1e-6
NEG = -1.0e30
TAKEN = -3.0e38
SLOT = 2048
SLOTS = 5
U_SLOTS = 4
V_SLOTS = 4
DIAGS = 4

HD = 64
QA, KA, VA, IQ, IK, IW, QB, KB, VB = (int(c) for c in np.cumsum([0, 512, 64, 64, 512, 64, 8, 512, 512]))
EVEN_COLS = VB + 512
DSA_KEEP = 64
KV_RANK, Q_RANK, ROPE = 256, 768, 32
MLA_HEADS, NOPE = 16, 64
MLA_D = NOPE + ROPE
EH, NK, TOP = 8, 128, 16
MIX = 4612
SLOPES = [float(np.float32(2.0 ** (-8.0 * n / 16))) for n in range(1, 17)]
DIL = ((128, 1), (512, 4), (2048, 16))
SLOPES_DIL = [SLOPES[0:4], SLOPES[8:12], SLOPES[12:16]]
SLOPES_DIFF = SLOPES[4:8]
LAMBDA_INIT = 0.2
TWO_PI = 2 * np.pi
C1 = 6.28125
C2 = float(np.float32(np.round((TWO_PI - C1) * 2 ** 21) / 2 ** 21))
C3 = float(TWO_PI - C1 - C2)
ROUND = 12582912.0


class Banks:

    def __init__(self, views, full, free):
        self.views, self.full, self.free, self.n = views, full, free, 0

    def take(self):
        b, use = self.n % len(self.views), self.n // len(self.views)
        self.n += 1
        return Unit(self, b, use)


class Unit:

    def __init__(self, banks, b, use):
        self.ap, self.b, self.use = banks.views[b], b, use
        self.full, self.free = banks.full[b], banks.free[b]

    def wait_free(self, pe):
        if self.use:
            pe.wait_ge(self.free, self.use)

    def wait_full(self, eng):
        eng.wait_ge(self.full, self.use + 1)

    def wait_emptied(self, eng):
        eng.wait_ge(self.free, self.use + 1)

    def full_at(self):
        return self.full, self.use + 1


class Signal:

    def __init__(self, sem):
        self.sem, self.n = sem, 0

    def plan(self, k=1):
        self.n += k
        return self.n


class Chain:

    def __init__(self, eng, sem):
        self.eng, self.sem, self.n = eng, sem, 0

    def __call__(self, ins):
        self.n += 1
        ins.then_inc(self.sem, 1)
        self.eng.wait_ge(self.sem, self.n)

    def add(self, ins):
        self.n += 1
        ins.then_inc(self.sem, 1)

    def wait(self):
        self.eng.wait_ge(self.sem, self.n)


def build(nc, a, out):
    with ExitStack() as ctx:
        def sb(name, shape, dt=F32):
            return ctx.enter_context(nc.sbuf_tensor("sb_" + name, shape, dt))

        def sem(name):
            return ctx.enter_context(nc.semaphore(name))

        psum = [ctx.enter_context(nc.psum_tensor(f"bank{i}", [P, 512], F32)) for i in range(2)]
        ps_scores = ctx.enter_context(nc.psum_tensor("ps_scores", [P, 4, SEQ], F32))
        ps_turn = [ctx.enter_context(nc.psum_tensor(f"ps_turn{i}", [P, 512], F32)) for i in range(2)]
        ps_acc = ctx.enter_context(nc.psum_tensor("ps_acc", [P, D], F32))

        x = sb("x", [P, TILES, D])
        h = sb("h", [P, TILES, D])
        hT = sb("hT", [P, DC, SEQ])
        mixed = sb("mixed", [P, TILES, 1056])
        probs = sb("probs", [P, 2, 4, SEQ])
        probsT = sb("probsT", [P, 2, 2, 4, P])
        wring = sb("wring", [P, SLOTS, SLOT])
        rows = sb("rows", [P, U_SLOTS + V_SLOTS, D])
        tok = sb("tok", [P, 10496])
        turned = sb("turned", [P, 32 * SEQ])
        gain = sb("gain", [P, D])
        ident = sb("ident", [P, P])
        causal = sb("causal", [P, TILES, SEQ])
        cos = sb("cos", [P, TILES, 32])
        sin = sb("sin", [P, TILES, 32])
        small = sb("small", [P, 256])
        stat = sb("stat", [P, 64])
        expert = sb("expert", [P, TILES, P], I32)
        share = sb("share", [P, TILES, P])
        dots = sb("dots", [P, P])
        gelu = sb("gelu", [P, 2, TOP])
        weight = sb("weight", [P, P])
        diag = sb("diag", [P, DIAGS, P])

        w_landed = [sem(f"w_landed{i}") for i in range(SLOTS)]
        w_used = Signal(sem("w_used"))
        gain_landed = Signal(sem("gain_landed"))
        gain_used = Signal(sem("gain_used"))
        x_landed = sem("x_landed")
        consts_landed = sem("consts_landed")
        pool_made = sem("pool_made")
        pool_step = sem("pool_step")
        dve_step = sem("dve_step")
        act_step = sem("act_step")
        done = {e: sem(f"stage_done_{e}") for e in ("pe", "act", "dve")}
        var_ready = Signal(sem("var_ready"))
        root_ready = Signal(sem("root_ready"))
        maxes_ready = Signal(sem("maxes_ready"))
        probs_ready = Signal(sem("probs_ready"))
        relu_used = Signal(sem("relu_used"))
        to_act = Signal(sem("to_act"))
        from_act = Signal(sem("from_act"))
        experts_ready = Signal(sem("experts_ready"))
        u_landed = [sem(f"u_landed{i}") for i in range(U_SLOTS)]
        v_landed = [sem(f"v_landed{i}") for i in range(V_SLOTS)]
        u_used = Signal(sem("u_used"))
        v_used = Signal(sem("v_used"))
        gelu_ready = Signal(sem("gelu_ready"))
        weights_ready = Signal(sem("weights_ready"))
        diag_ready = Signal(sem("diag_ready"))
        out_landed = sem("out_landed")

        pair = [sem(f"product_full{i}") for i in range(2)], [sem(f"product_free{i}") for i in range(2)]
        products = Banks([b[:, :] for b in psum], *pair)
        pair = [sem(f"turn_full{i}") for i in range(2)], [sem(f"turn_free{i}") for i in range(2)]
        turns = Banks([b[:, :] for b in ps_turn], *pair)
        scores = Banks([ps_scores[:, :, :]], [sem("scores_full")], [sem("scores_free")])

        stages = []
        stream = []
        given_back = {}
        ends = {"pe": 0, "act": 0, "dve": 0}
        chains = {}

        def stage(pe=None, act=None, dve=None):
            stages.append({"pe": pe, "act": act, "dve": dve})

        def run_stages(name, eng):
            others = [n for n in ("pe", "act", "dve") if n != name]
            for k, s in enumerate(stages):
                if s[name] is not None:
                    s[name](eng)
                eng.drain().then_inc(done[name], 1)
                for n in others:
                    eng.wait_ge(done[n], k + 1)

        def weights(view, chunks, cols):
            stream.append((view, chunks, cols))
            return len(stream) - 1

        def slot_ap(n):
            _, chunks, cols = stream[n]
            return wring[:, n % SLOTS, 0:chunks * cols].rearrange("p (c n) -> p c n", c=chunks)

        def slot_wait(pe, n):
            pe.wait_ge(w_landed[n % SLOTS], 16 * (n // SLOTS + 1))

        def rows_of(w):
            return w.rearrange("(c p) n -> p c n", p=P)

        gains = []
        squares = [probs[:, i].rearrange("p a b -> p (a b)") for i in range(2)]

        def norm(src, dst, width, g, tiles=range(TILES)):
            gains.append((g, width))
            number = len(gains)
            g_value = gain_landed.plan(16)
            n = len(tiles)
            v_value, r_value = var_ready.plan(), root_ready.plan()
            gain_used.plan()
            var, root, y, t1 = (stat[:, 4 * i:4 * i + n] for i in range(4))

            def dve(e):
                link = chains["dve"]
                for i, t in enumerate(tiles):
                    link.add(e.tensor_tensor_reduce(squares[t][:, 0:width], src(t), src(t), 1.0 / width, 0.0, ALU.mult, ALU.add,
                                                    stat[:, i:i + 1]))
                link.wait()
                e.tensor_scalar(var, var, EPS, None, ALU.add).then_inc(var_ready.sem, 1)
                e.wait_ge(root_ready.sem, r_value)
                link(e.reciprocal(y, root))
                link(e.tensor_tensor(t1, y, y, ALU.mult))
                link(e.tensor_tensor(t1, t1, var, ALU.mult))
                link(e.tensor_scalar(t1, t1, -0.5, 1.5, ALU.mult, ALU.add))
                link(e.tensor_tensor(y, y, t1, ALU.mult))
                e.wait_ge(gain_landed.sem, g_value)
                for i, t in enumerate(tiles):
                    last = e.scalar_tensor_tensor(dst(t), src(t), stat[:, 8 + i:9 + i], gain[:, 0:width],
                                                  ALU.mult, ALU.mult)
                last.then_inc(gain_used.sem, 1)

            def act(e):
                e.wait_ge(var_ready.sem, v_value)
                e.activation(root, var, ACT.Sqrt).then_inc(root_ready.sem, 1)
                if number < len(gains):
                    e.wait_ge(gain_used.sem, number)
                    load_gain(e, number)

            stage(act=act, dve=dve)

        def load_gain(e, n):
            g, width = gains[n]
            e.dma_start(gain[:, 0:width], g.to_broadcast([P, width])).then_inc(gain_landed.sem, 16)

        def turn(blocks):
            plan = [(srcs, dst, turns.take()) for srcs, dst in blocks]

            def pe(e):
                for srcs, dst, u in plan:
                    w = dst.shape[0]
                    u.wait_free(e)
                    for i, s in enumerate(srcs):
                        last = e.transpose(u.ap[0:w, i * P:(i + 1) * P], s, ident[:, :])
                    last.then_inc(u.full, 1)

            def empty(e, b):
                for srcs, dst, u in plan:
                    if u.b == b:
                        u.wait_full(e)
                        w, n = dst.shape[0], len(srcs)
                        src = u.ap[0:w, 0:n * P].rearrange("p (n t) -> p n t", n=n)
                        copy = e.copy if b == 0 else e.tensor_copy
                        copy(dst, src).then_inc(u.free, 1)

            stage(pe=pe, act=lambda e: empty(e, 0), dve=lambda e: empty(e, 1))

        def turn_wide(src, dst, chunks, tiles=range(TILES)):
            blocks = []
            for t in tiles:
                for c0 in range(0, chunks, 4):
                    n = min(4, chunks - c0)
                    blocks.append(([src(t)[:, c * P:(c + 1) * P] for c in range(c0, c0 + n)],
                                   dst[:, c0:c0 + n, t * P:(t + 1) * P]))
            turn(blocks)

        def project(xT, w, chunks, cols, empty, engine, tiles=range(TILES)):
            per = min(chunks, 4) if chunks != 6 else 3
            wide = SLOT // per // 512 * 512 if per < 4 else 512
            plan = []
            wv = rows_of(w)
            for n0 in range(0, cols, wide):
                wn = min(wide, cols - n0)
                slots = [(weights(wv[:, k:k + per, n0:n0 + wn], per, wn), k) for k in range(0, chunks, per)]
                blocks = range(0, wn, 512)
                for b0 in blocks:
                    bn = min(512, wn - b0)
                    units = [products.take() for _ in tiles]
                    plan.append((slots, b0, bn, n0 + b0, units, b0 == blocks[-1]))
                for s, k0 in slots:
                    last_use = units[-1].full_at() if k0 + per == chunks else (w_used.sem, w_used.plan())
                    given_back[s] = last_use

            def pe(e):
                for slots, b0, bn, _, units, ends_slot in plan:
                    for u in units:
                        u.wait_free(e)
                    for s, k0 in slots:
                        slot_wait(e, s)
                        sl = slot_ap(s)
                        for t, u in zip(tiles, units):
                            for k in range(per):
                                last = e.matmul(u.ap[:, 0:bn], xT[:, k0 + k, t * P:(t + 1) * P],
                                                sl[:, k, b0:b0 + bn], start=k0 + k == 0, stop=k0 + k == chunks - 1)
                            if k0 + per == chunks:
                                last.then_inc(u.full, 1)
                        if ends_slot and k0 + per < chunks:
                            last.then_inc(w_used.sem, 1)

            def other(e):
                for _, _, bn, c0, units, _ in plan:
                    for t, u in zip(tiles, units):
                        u.wait_full(e)
                        empty(e, u.ap[:, 0:bn], t, c0, bn).then_inc(u.free, 1)

            stage(pe=pe, **{engine: other})

        def rotate(src, dst, heads, half, t, stride=1):
            c = cos[:, t, 0:32:stride].unsqueeze(1).to_broadcast([P, heads, half])
            s = sin[:, t, 0:32:stride].unsqueeze(1).to_broadcast([P, heads, half])
            x1, x2 = src[:, :, 0, :], src[:, :, 1, :]
            n = heads * half
            flat_probs = probs[:, :, :, :].rearrange("p a b c -> p (a b c)")
            tmp = [flat_probs[:, i * n:(i + 1) * n].rearrange("p (a b) -> p a b", a=heads) for i in range(4)]

            def dve(e):
                link = chains["dve"]
                link.add(e.tensor_tensor(tmp[0], x1, c, ALU.mult))
                link.add(e.tensor_tensor(tmp[1], x2, s, ALU.mult))
                link.add(e.tensor_tensor(tmp[2], x1, s, ALU.mult))
                link(e.tensor_tensor(tmp[3], x2, c, ALU.mult))
                link.add(e.tensor_tensor(dst[:, :, 0, :], tmp[0], tmp[1], ALU.subtract))
                link(e.tensor_tensor(dst[:, :, 1, :], tmp[2], tmp[3], ALU.add))
            return dve

        def dve_stage(steps):
            def dve(e):
                for s in steps:
                    s(e)
            stage(dve=dve)

        def attend(groups):
            plan = []
            for g in groups:
                n_out = {"joint": 1, "diff": 2}.get(g["kind"], len(g["maps"]))
                n_turned = 2 if g["kind"] == "diff" else len(g["maps"])
                chunks = g["tile"] + 1
                value = {"s": scores.take(), "turns": [turns.take() for _ in range(chunks)], "out": products.take(),
                         "n_out": n_out, "n_turned": n_turned, "chunks": chunks, "w": P * chunks,
                         "m": maxes_ready.plan(), "p": probs_ready.plan()}
                if g["kind"] == "stick":
                    value["m2"] = maxes_ready.plan()
                    value["a1"] = from_act.plan()
                if g["kind"] == "diff":
                    value["a2"] = from_act.plan()
                plan.append(g | value)

            def place(i):
                return (i % 2) * 2 + i // 2

            def places(g):
                n = len(g["maps"])
                return [place(i) for i in range(n)] if g["kind"] != "joint" else list(range(n))

            def pe(e):
                def score(g):
                    g["s"].wait_free(e)
                    for i, (q, k) in enumerate(g["maps"]):
                        last = e.matmul(g["s"].ap[:, places(g)[i], 0:g["w"]], q, k, start=True, stop=True)
                    last.then_inc(g["s"].full, 1)

                def apply(n, g):
                    e.wait_ge(probs_ready.sem, g["p"])
                    for c, u in enumerate(g["turns"]):
                        u.wait_free(e)
                        for i in range(g["n_turned"]):
                            at = i if g["kind"] == "diff" else places(g)[i]
                            last = e.transpose(u.ap[:, i * P:(i + 1) * P], probs[:, n % 2, at, c * P:(c + 1) * P],
                                               ident[:, :])
                        last.then_inc(u.full, 1)
                    u = g["out"]
                    for turned_unit in g["turns"]:
                        turned_unit.wait_emptied(e)
                    u.wait_free(e)
                    for i in range(g["n_turned"]):
                        o = 0 if g["kind"] == "joint" else i
                        for c in range(g["chunks"]):
                            first = c == 0 and (i == 0 or g["kind"] != "joint")
                            final = c == g["chunks"] - 1 and (i == g["n_turned"] - 1 or g["kind"] != "joint")
                            last = e.matmul(u.ap[:, o * HD:(o + 1) * HD], probsT[:, n % 2, c, i, :], g["values"][i](c),
                                            start=first, stop=final)
                    last.then_inc(u.full, 1)

                for n, g in enumerate(plan):
                    score(g)
                    if n:
                        apply(n - 1, plan[n - 1])
                apply(len(plan) - 1, plan[-1])

            def empty_turns(e, b, n, g):
                for c, u in enumerate(g["turns"]):
                    if u.b == b:
                        u.wait_full(e)
                        k = g["n_turned"]
                        copy = e.copy if b == 0 else e.tensor_copy
                        copy(probsT[:, n % 2, c, 0:k, :], u.ap[:, 0:k * P].rearrange("p (n t) -> p n t", n=k)
                             ).then_inc(u.free, 1)

            def act(e):
                link = chains["act"]
                for n, g in enumerate(plan):
                    w, k = g["w"], len(g["maps"])
                    pr = probs[:, n % 2]
                    sums = stat[:, 16 + 8 * (n % 2):24 + 8 * (n % 2)]
                    neg = stat[:, 32 + 8 * (n % 2):40 + 8 * (n % 2)]
                    if g["kind"] == "stick":
                        az = stick_tmp[:, :, 0:w]
                        g["s"].wait_full(e)
                        link(e.activation(az, g["s"].ap[:, :, 0:w], ACT.Abs, scale=g["scale"]))
                        link(e.activation(az, az, ACT.Exp, scale=-1.0))
                        e.activation(az, az, ACT.Ln, bias=1.0).then_inc(from_act.sem, 1)
                        e.wait_ge(maxes_ready.sem, g["m2"])
                        e.activation(pr[:, :, 0:w], pr[:, :, 0:w], ACT.Exp).then_inc(probs_ready.sem, 1)
                    else:
                        e.wait_ge(maxes_ready.sem, g["m"])
                        if g["kind"] == "joint":
                            last = e.activation(pr[:, 0:k, 0:w], pr[:, 0:k, 0:w], ACT.Exp, bias=neg[:, 0:1],
                                                accum_out=sums[:, 0:1])
                        else:
                            for i in sorted(places(g)):
                                last = e.activation(pr[:, i, 0:w], pr[:, i, 0:w], ACT.Exp, bias=neg[:, i:i + 1],
                                                    accum_out=sums[:, i:i + 1])
                        last.then_inc(from_act.sem if g["kind"] == "diff" else probs_ready.sem, 1)
                    if n:
                        empty_turns(e, 0, n - 1, plan[n - 1])
                empty_turns(e, 0, len(plan) - 1, plan[-1])

            def dve(e):
                link = chains["dve"]

                def soften(n, g):
                    w, k = g["w"], len(g["maps"])
                    pr = probs[:, n % 2]
                    neg = stat[:, 32 + 8 * (n % 2):40 + 8 * (n % 2)]
                    sums = stat[:, 16 + 8 * (n % 2):24 + 8 * (n % 2)]
                    s = g["s"].ap
                    if g["kind"] == "stick":
                        e.wait_ge(from_act.sem, g["a1"])
                        az = stick_tmp[:, :, 0:w]
                        z = pr[:, :, 0:w]
                        e.tensor_scalar(z, s[:, :, 0:w], g["scale"], None, ALU.mult).then_inc(g["s"].free, 1)
                        e.wait_ge(g["s"].free, g["s"].use + 1)
                        link(e.scalar_tensor_tensor(az, z, 0.0, az, ALU.max, ALU.add))
                        link(e.tensor_tensor(az, az, g["strict"].unsqueeze(1).to_broadcast([P, 4, w]), ALU.mult))
                        for i in range(4):
                            link.add(e.tensor_tensor_scan(az[:, i, ::-1], zero[:, 0:w], az[:, i, ::-1], 0.0,
                                                          ALU.add, ALU.add))
                        link.wait()
                        link(e.tensor_tensor(z, z, az, ALU.subtract))
                        e.tensor_tensor(z, z, g["bias"].unsqueeze(1).to_broadcast([P, 4, w]), ALU.add
                                        ).then_inc(maxes_ready.sem, 2)
                        return
                    g["s"].wait_full(e)
                    if isinstance(g["bias"], list):
                        for i in range(k):
                            at = places(g)[i]
                            last = e.scalar_tensor_tensor(pr[:, at, 0:w], s[:, at, 0:w], g["scale"], g["bias"][i],
                                                          ALU.mult, ALU.add)
                    else:
                        last = e.scalar_tensor_tensor(pr[:, 0:k, 0:w], s[:, 0:k, 0:w], g["scale"],
                                                      g["bias"].unsqueeze(1).to_broadcast([P, k, w]), ALU.mult, ALU.add)
                    last.then_inc(g["s"].free, 1)
                    e.wait_ge(g["s"].free, g["s"].use + 1)
                    if g["kind"] == "joint":
                        link(e.tensor_reduce(neg[:, 0:1], pr[:, 0:k, 0:w], AX.XY, ALU.max))
                        k = 1
                    else:
                        link(e.tensor_reduce(neg[:, 0:k], pr[:, 0:k, 0:w], AX.X, ALU.max))
                    e.tensor_scalar(neg[:, 0:k], neg[:, 0:k], -1.0, None, ALU.mult).then_inc(maxes_ready.sem, 1)

                def combine(n, g):
                    w = g["w"]
                    pr = probs[:, n % 2]
                    sums = stat[:, 16 + 8 * (n % 2):24 + 8 * (n % 2)]
                    e.wait_ge(from_act.sem, g["a2"])
                    link(e.reciprocal(sums[:, 0:4], sums[:, 0:4]))
                    link(e.tensor_scalar(sums[:, 2:4], sums[:, 2:4], lam, None, ALU.mult))
                    for i in range(2):
                        link(e.tensor_scalar(pr[:, 2 + i, 0:w], pr[:, 2 + i, 0:w], sums[:, 2 + i:3 + i], None, ALU.mult))
                        last = e.scalar_tensor_tensor(pr[:, i, 0:w], pr[:, i, 0:w], sums[:, i:i + 1], pr[:, 2 + i, 0:w],
                                                      ALU.mult, ALU.subtract)
                        if i == 0:
                            link(last)
                    last.then_inc(probs_ready.sem, 1)

                def take_out(n, g):
                    sums = stat[:, 16 + 8 * (n % 2):24 + 8 * (n % 2)]
                    k = g["n_out"]
                    if g["kind"] in ("softmax", "joint"):
                        e.wait_ge(probs_ready.sem, g["p"])
                        link(e.reciprocal(sums[:, 0:max(k, 1)], sums[:, 0:max(k, 1)]))
                    g["out"].wait_full(e)
                    src = g["out"].ap[:, 0:k * HD].rearrange("p (n d) -> p n d", n=k)
                    if g["kind"] == "softmax":
                        for par in range(2):
                            r = sums[:, 2 * par:2 * par + 2].unsqueeze(2).to_broadcast([P, 2, HD])
                            last = e.tensor_tensor(g["out_ap"][:, par::2, :], src[:, par::2, :], r, ALU.mult)
                            if par == 0:
                                link(last)
                    elif g["kind"] == "joint":
                        last = e.tensor_scalar(g["out_ap"], src, sums[:, 0:1], None, ALU.mult)
                    else:
                        last = e.tensor_copy(g["out_ap"], src)
                    last.then_inc(g["out"].free, 1)

                for n, g in enumerate(plan):
                    if g.get("before"):
                        g["before"](e)
                    soften(n, g)
                    if n:
                        empty_turns(e, 1, n - 1, plan[n - 1])
                        take_out(n - 1, plan[n - 1])
                    if g["kind"] == "diff":
                        combine(n, g)
                empty_turns(e, 1, len(plan) - 1, plan[-1])
                take_out(len(plan) - 1, plan[-1])

            stage(pe=pe, act=act, dve=dve)

        raw = sb("raw", [P, 8])
        lam = small[:, 250:251]
        flat = rows[:, :, :].rearrange("p a b -> p (a b)")

        def carve(at, shape):
            n = int(np.prod(shape))
            v = flat[:, at:at + n]
            return v.rearrange("p (a b) -> p a b", a=shape[0]) if len(shape) == 2 else v

        stick_tmp = carve(0, (4, SEQ))
        dist = carve(1024, (TILES, SEQ))
        strict = carve(1536, (TILES, SEQ))
        strict_bias = carve(2048, (TILES, SEQ))
        zero = carve(2560, (SEQ,))
        dil_bias = [causal] + [carve(2816 + 512 * i, (TILES, SEQ)) for i in range(2)]
        window = carve(3840, (TILES, SEQ))
        head_bias = carve(4352, (4, SEQ))
        gates = carve(5376, (TILES, 512))
        upper = carve(6400, (TILES, SEQ))
        forget = carve(6912, (TILES, 4))
        cum_keys = carve(6920, (4, SEQ))

        inv = small[:, 0:32]
        ang = small[:, 32:96].rearrange("p (t f) -> p t f", t=TILES)
        turns_n = small[:, 96:160].rearrange("p (t f) -> p t f", t=TILES)
        pos = raw[:, 0:2]
        pos_i = raw[:, 2:4]
        ang_v, sin_v = to_act.plan(), from_act.plan()

        def angles_dve(e):
            link = chains["dve"]
            e.wait_ge(consts_landed, 32)
            link(e.tensor_copy(pos, pos_i.bitcast(I32)))
            for t in range(TILES):
                link.add(e.tensor_scalar(ang[:, t, :], inv, pos[:, t:t + 1], None, ALU.mult))
            link.wait()
            link(e.tensor_scalar(turns_n, ang, float(1 / TWO_PI), ROUND, ALU.mult, ALU.add))
            link(e.tensor_scalar(turns_n, turns_n, ROUND, None, ALU.subtract))
            for c in (C1, C2, C3):
                link(e.scalar_tensor_tensor(ang, turns_n, -c, ang, ALU.mult, ALU.add))
            link(e.tensor_scalar(ang, ang, 3.1415925, -3.1415925, ALU.min, ALU.max))
            link(e.scalar_tensor_tensor(turns_n, ang, -1.0, ang, ALU.mult, ALU.max))
            e.tensor_scalar(turns_n, turns_n, -1.0, float(np.pi / 2), ALU.mult, ALU.add).then_inc(to_act.sem, 1)

        def angles_act(e):
            e.wait_ge(to_act.sem, ang_v)
            e.activation(sin[:, :, :], ang, ACT.Sin)
            e.activation(cos[:, :, :], turns_n, ACT.Sin).then_inc(from_act.sem, 1)

        def wait_pool_pe(e):
            e.wait_ge(pool_made, 1)

        def wait_pool_dve(e):
            e.wait_ge(pool_made, 1)
            e.wait_ge(x_landed, 16)
            angles_dve(e)

        stage(pe=wait_pool_pe, act=angles_act, dve=wait_pool_dve)

        X = lambda t: x[:, t, :]
        H = lambda t: h[:, t, :]
        M = lambda t: mixed[:, t, 0:D]
        T = turned[:, :].rearrange("p (c s) -> p c s", s=SEQ)

        def add_residual(e, ps, t, c0, n):
            return e.tensor_tensor(x[:, t, c0:c0 + n], x[:, t, c0:c0 + n], ps, ALU.add)

        def copy_to(buf):
            return lambda e, ps, t, c0, n: e.copy(buf[:, t, c0:c0 + n], ps)

        norm(X, H, D, a["attn_norm"][0:1, :])
        turn_wide(H, hT, DC)
        proj = tok[:, 0:TILES * EVEN_COLS].rearrange("p (t n) -> p t n", t=TILES)
        project(hT, a["hyb_w_in"][0], DC, EVEN_COLS, copy_to(proj), "act")
        R_QA, R_KA, R_IQ, R_IK, R_QB, R_KB = 0, 512, 640, 1152, 1280, 1792
        rot = tok[:, TILES * EVEN_COLS:TILES * (EVEN_COLS + 2304)].rearrange("p (t n) -> p t n", t=TILES)
        steps = []
        for t in range(TILES):
            for src, dst, heads in ((QA, R_QA, 8), (KA, R_KA, 1), (KA, R_KA + HD, 1), (IQ, R_IQ, 8), (IK, R_IK, 1),
                                    (IK, R_IK + HD, 1), (QB, R_QB, 16)):
                sv, dv = (b[:, t, o:o + heads * HD].rearrange("p (a b c) -> p a b c", a=heads, b=2)
                          for b, o in ((proj, src), (rot, dst)))
                steps.append(rotate(sv, dv, heads, HD // 2, t))
        dve_stage(steps)
        turn_wide(lambda t: rot[:, t, :], T, 18)

        def head_T(first, i, t, n=1, shared=False):
            c = first // P + (0 if shared else i // 2)
            r = (i % 2) * HD
            return T[r:r + HD, c, t * P:t * P + n * P]

        keep_bias = carve(0, (TILES, SEQ))
        rank = carve(512, (TILES, SEQ))
        relu = carve(1024, (4, SEQ))
        iws = stat[:, 56:64]

        def index(t):
            w = P * (t + 1)
            w_scale = 8 ** -0.5 * 64 ** -0.5
            units = [scores.take() for _ in range(2)]
            used_values = [relu_used.plan() for _ in range(2)]
            rk = rank[:, t, 0:w]

            def pe(e):
                for j, u in enumerate(units):
                    u.wait_free(e)
                    for i in range(4):
                        last = e.matmul(u.ap[:, (i % 2) * 2 + i // 2, 0:w], head_T(R_IQ, 4 * j + i, t),
                                        head_T(R_IK, i, 0, t + 1, True), start=True, stop=True)
                    last.then_inc(u.full, 1)

            def act(e):
                for u, used in zip(units, used_values):
                    u.wait_full(e)
                    if used > 1:
                        e.wait_ge(relu_used.sem, used - 1)
                    e.activation(relu[:, :, 0:w], u.ap[:, :, 0:w], ACT.Relu).then_inc(u.free, 1)

            def dve(e):
                link = chains["dve"]
                link(e.tensor_scalar(iws, proj[:, t, IW:IW + 8], w_scale, None, ALU.mult))
                for j, (u, used) in enumerate(zip(units, used_values)):
                    u.wait_emptied(e)
                    for i in range(4):
                        src = relu[:, (i % 2) * 2 + i // 2, 0:w]
                        s = iws[:, 4 * j + i:4 * j + i + 1]
                        if j == 0 and i == 0:
                            link(e.tensor_scalar(rk, src, s, None, ALU.mult))
                        elif i < 3:
                            link(e.scalar_tensor_tensor(rk, src, s, rk, ALU.mult, ALU.add))
                        else:
                            e.scalar_tensor_tensor(rk, src, s, rk, ALU.mult, ALU.add).then_inc(relu_used.sem, 1)
                            e.wait_ge(relu_used.sem, used)
                link(e.tensor_tensor(rk, rk, causal[:, t, 0:w], ALU.add))
                m8 = stat[:, 48:56]
                for _ in range(DSA_KEEP // 8):
                    link(e.max(m8, rk))
                    link(e.match_replace(rk, m8, rk, TAKEN))
                kb = keep_bias[:, t, 0:w]
                link(e.tensor_scalar(kb, rk, TAKEN / 2, NEG, ALU.is_gt, ALU.mult))
                link(e.tensor_tensor(kb, kb, causal[:, t, 0:w], ALU.add))

            stage(pe=pe, act=act, dve=dve)

        for t in range(TILES):
            index(t)

        groups = []
        for t in range(TILES):
            for j in range(2):
                hs = range(4 * j, 4 * j + 4)
                groups.append(dict(
                    kind="softmax", tile=t, scale=HD ** -0.5, bias=keep_bias[:, t, 0:P * (t + 1)],
                    maps=[(head_T(R_QA, i, t), head_T(R_KA, i, 0, t + 1, True)) for i in hs],
                    values=[lambda c: proj[:, c, VA:VA + HD]] * 4,
                    out_ap=mixed[:, t, 256 * j:256 * j + 256].rearrange("p (n d) -> p n d", d=HD)))
            for j in range(2):
                hs = range(4 * j, 4 * j + 4)
                groups.append(dict(
                    kind="softmax", tile=t, scale=HD ** -0.5, bias=causal[:, t, 0:P * (t + 1)],
                    maps=[(head_T(R_QB, i, t), head_T(R_KB, i, 0, t + 1)) for i in hs],
                    values=[(lambda c, i=i: proj[:, c, VB + i * HD:VB + (i + 1) * HD]) for i in hs],
                    out_ap=mixed[:, t, 512 + 256 * j:768 + 256 * j].rearrange("p (n d) -> p n d", d=HD)))
        attend(groups)
        turn_wide(M, T, DC)
        project(T, a["hyb_w_out"][0], DC, D, add_residual, "dve")

        qT = turned[:, 0:16 * P].rearrange("p (n t) -> p n t", n=16)
        key_scores = turned[:, 16 * P:32 * P].rearrange("p (n k) -> p n k", n=16)
        onehot = turned[:, 32 * P:48 * P]
        best = turned[:, 6144:6400].rearrange("p (n k) -> p n k", n=16)
        best_at = turned[:, 6400:6656].rearrange("p (n k) -> p n k", n=16)
        best_f = turned[:, 6656:6912].rearrange("p (n k) -> p n k", n=16)
        top = turned[:, 6912:7040].rearrange("p (n k) -> p n k", n=EH)
        top_at = turned[:, 7040:7168].rearrange("p (n k) -> p n k", n=EH)
        hi = turned[:, 7168:7296]
        lo = turned[:, 7296:7424]
        pick = [turned[:, 7424:7552], turned[:, 7552:7680]]
        iota16 = sb("iota16", [P, TOP])

        routed = {}

        def route(layer, t):
            wq = rows_of(a["peer_w_q"][layer])
            plan = []
            for b in range(4):
                slots = [(weights(wq[:, k:k + 4, b * 512:(b + 1) * 512], 4, 512), k) for k in (0, 4)]
                plan.append((slots, products.take()))
                for s, _ in slots:
                    given_back[s] = plan[-1][1].full_at()
            keys = weights(a["peer_keys"][layer].rearrange("(o p) n -> p o n", o=1), 1, SLOT)
            key_units = [products.take() for _ in range(4)]
            given_back[keys] = key_units[-1].full_at()
            e_in, e_out = to_act.plan(), from_act.plan()
            routed[layer, t] = experts_ready.plan()

            def pe(e):
                for slots, u in plan:
                    u.wait_free(e)
                    for s, _ in slots:
                        slot_wait(e, s)
                    for j in range(4):
                        for s, k0 in slots:
                            for k in range(4):
                                last = e.matmul(u.ap[:, j * P:(j + 1) * P], slot_ap(s)[:, k, j * P:(j + 1) * P],
                                                hT[:, k0 + k, t * P:(t + 1) * P], start=k0 + k == 0,
                                                stop=k0 + k == DC - 1)
                    last.then_inc(u.full, 1)
                slot_wait(e, keys)
                for b, u in enumerate(key_units):
                    plan[b][1].wait_emptied(e)
                    u.wait_free(e)
                    for j in range(4 * b, 4 * b + 4):
                        last = e.matmul(u.ap[:, (j % 4) * P:(j % 4 + 1) * P], qT[:, j, :],
                                        slot_ap(keys)[:, 0, j * P:(j + 1) * P], start=True, stop=True)
                    last.then_inc(u.full, 1)

            def act(e):
                for b, (_, u) in enumerate(plan):
                    u.wait_full(e)
                    e.copy(qT[:, 4 * b:4 * b + 4, :], u.ap.rearrange("p (n t) -> p n t", n=4)).then_inc(u.free, 1)
                for b, u in enumerate(key_units):
                    u.wait_full(e)
                    e.copy(key_scores[:, 4 * b:4 * b + 4, :], u.ap.rearrange("p (n t) -> p n t", n=4)
                           ).then_inc(u.free, 1)
                e.wait_ge(to_act.sem, e_in)
                e.activation(share[:, t, :], share[:, t, :], ACT.Exp).then_inc(from_act.sem, 1)

            def dve(e):
                link = chains["dve"]
                halves = [(key_scores[:, j, :], best[:, j, :], best_at[:, j, :].bitcast(U32)) for j in range(16)]

                def top16(items, ready):
                    for j, (v, m, at) in enumerate(items):
                        if ready:
                            key_units[j // 4].wait_emptied(e)
                        link.add(e.max(m[:, 0:8], v))
                    link.wait()
                    for v, m, at in items:
                        link.add(e.max_index(at[:, 0:8], m[:, 0:8], v))
                    link.wait()
                    for v, m, at in items:
                        link.add(e.match_replace(v, m[:, 0:8], v, TAKEN))
                    link.wait()
                    for v, m, at in items:
                        link.add(e.max(m[:, 8:16], v))
                    link.wait()
                    for v, m, at in items:
                        link.add(e.max_index(at[:, 8:16], m[:, 8:16], v))
                    link.wait()

                top16(halves, True)
                link(e.tensor_copy(best_f, best_at.bitcast(U32)))
                cand = key_scores.rearrange("p n k -> p (n k)").rearrange("p (h i j) -> p h i j", h=EH, i=TOP)
                b4 = best.rearrange("p (h s) k -> p h s k", s=2)
                link(e.tensor_tensor(cand, b4[:, :, 0, :].unsqueeze(3).to_broadcast([P, EH, TOP, TOP]),
                                     b4[:, :, 1, :].unsqueeze(2).to_broadcast([P, EH, TOP, TOP]), ALU.add))
                cf = key_scores.rearrange("p n k -> p (n k)").rearrange("p (h m) -> p h m", h=EH)
                top16([(cf[:, j, :], top[:, j, :], top_at[:, j, :].bitcast(U32)) for j in range(EH)], False)
                at = top_at.rearrange("p n k -> p (n k)").bitcast(I32)
                link.add(e.tensor_scalar(pick[0].bitcast(I32), at, 4, None, ALU.arith_shift_right))
                link(e.tensor_scalar(pick[1].bitcast(I32), at, 15, None, ALU.bitwise_and))
                link.add(e.tensor_copy(hi, pick[0].bitcast(I32)))
                link(e.tensor_copy(lo, pick[1].bitcast(I32)))
                f4 = best_f.rearrange("p (h s) k -> p h s k", s=2)
                oh3 = onehot.rearrange("p (a i) -> p a i", i=TOP)
                oh4 = onehot.rearrange("p (h k i) -> p h k i", h=EH, k=TOP)
                for s, where in enumerate((hi, lo)):
                    link(e.tensor_tensor(oh3, where.unsqueeze(2).to_broadcast([P, P, TOP]),
                                         iota16[:, :].unsqueeze(1).to_broadcast([P, P, TOP]), ALU.is_equal))
                    link(e.tensor_tensor(oh4, oh4, f4[:, :, s, :].unsqueeze(2).to_broadcast([P, EH, TOP, TOP]),
                                         ALU.mult))
                    link(e.tensor_reduce(pick[s], oh3, AX.X, ALU.add))
                if layer:
                    link(e.tensor_scalar(pick[1], pick[1], float(layer * NK * NK), None, ALU.add))
                e.scalar_tensor_tensor(expert[:, t, :], pick[0], float(NK), pick[1], ALU.mult, ALU.add
                                       ).then_inc(experts_ready.sem, 1)
                sh = share[:, t, :].rearrange("p (h k) -> p h k", h=EH)
                e.tensor_tensor(sh, top, top[:, :, 0:1].to_broadcast([P, EH, TOP]), ALU.subtract
                                ).then_inc(to_act.sem, 1)
                e.wait_ge(from_act.sem, e_out)
                link(e.tensor_reduce(small[:, 240:248], sh, AX.X, ALU.add))
                link(e.reciprocal(small[:, 240:248], small[:, 240:248]))
                link(e.tensor_tensor(sh, sh, small[:, 240:248].unsqueeze(2).to_broadcast([P, EH, TOP]), ALU.mult))

            stage(pe=pe, act=act, dve=dve)

        gathers = []

        def experts(layer, t):
            n0 = len(gathers) * P
            gathers.append((layer, t, routed[layer, t]))
            gelu_v = [gelu_ready.plan() for _ in range(EH)]
            weights_v = [weights_ready.plan() for _ in range(EH)]

            def dve(e):
                link = chains["dve"]

                def weigh(j):
                    e.wait_ge(gelu_ready.sem, gelu_v[j])
                    e.tensor_tensor(weight[:, j * TOP:(j + 1) * TOP], gelu[:, j % 2, :],
                                    share[:, t, j * TOP:(j + 1) * TOP], ALU.mult).then_inc(weights_ready.sem, 1)

                for j in range(EH):
                    for k in range(TOP):
                        if k == 2 and j:
                            weigh(j - 1)
                        n = n0 + j * TOP + k
                        e.wait_ge(u_landed[n % U_SLOTS], 16 * (n // U_SLOTS + 1))
                        r = rows[:, n % U_SLOTS, :]
                        e.tensor_tensor_reduce(r, r, h[:, t, :], 1.0, 0.0, ALU.mult, ALU.add,
                                               dots[:, j * TOP + k:j * TOP + k + 1]).then_inc(u_used.sem, 1)
                weigh(EH - 1)
                e.wait_ge(v_used.sem, n0 + P)
                for b in range(2):
                    link(e.tensor_tensor(x[:, t, b * 512:(b + 1) * 512], x[:, t, b * 512:(b + 1) * 512],
                                         ps_acc[:, b * 512:(b + 1) * 512], ALU.add))

            def act(e):
                def spread(j):
                    e.wait_ge(weights_ready.sem, weights_v[j])
                    for k in range(TOP):
                        n = n0 + j * TOP + k
                        if n >= DIAGS:
                            e.wait_ge(v_used.sem, n - DIAGS + 1)
                        e.activation(diag[:, n % DIAGS, :], ident[:, :], ACT.Copy,
                                     scale=weight[:, j * TOP + k:j * TOP + k + 1]).then_inc(diag_ready.sem, 1)

                for j in range(EH):
                    e.wait_ge(u_used.sem, n0 + (j + 1) * TOP)
                    e.activation(gelu[:, j % 2, :], dots[:, j * TOP:(j + 1) * TOP], ACT.Gelu
                                 ).then_inc(gelu_ready.sem, 1)
                    spread(j)

            def pe(e):
                for i in range(P):
                    n = n0 + i
                    e.wait_ge(v_landed[n % V_SLOTS], 16 * (n // V_SLOTS + 1))
                    e.wait_ge(diag_ready.sem, n + 1)
                    for b in range(2):
                        last = e.matmul(ps_acc[:, b * 512:(b + 1) * 512], diag[:, n % DIAGS, :],
                                        rows[:, U_SLOTS + n % V_SLOTS, b * 512:(b + 1) * 512],
                                        start=i == 0, stop=i == P - 1)
                    last.then_inc(v_used.sem, 1)

            stage(pe=pe, act=act, dve=dve)

        def peer(layer):
            norm(X, H, D, a["ffn_norm"][layer:layer + 1, :])
            turn_wide(H, hT, DC)
            for t in range(TILES):
                route(layer, t)
            for t in range(TILES):
                experts(layer, t)

        peer(0)

        norm(X, H, D, a["attn_norm"][1:2, :])
        turn_wide(H, hT, DC)
        project(hT, a["mla_w_in"][0], DC, Q_RANK + KV_RANK + ROPE, copy_to(mixed), "act")
        norm(lambda t: mixed[:, t, 0:Q_RANK], lambda t: h[:, t, 0:Q_RANK], Q_RANK, a["mla_q_norm"])
        norm(lambda t: mixed[:, t, Q_RANK:D], lambda t: h[:, t, Q_RANK:D], KV_RANK, a["mla_kv_norm"])
        turn_wide(H, hT, DC)
        n_q, n_kv = MLA_HEADS * MLA_D, MLA_HEADS * P
        q_tok = tok[:, 0:TILES * n_q].rearrange("p (t n) -> p t n", t=TILES)
        kv_tok = tok[:, TILES * n_q:TILES * (n_q + n_kv)].rearrange("p (t n) -> p t n", t=TILES)
        k_tok = tok[:, TILES * (n_q + n_kv):TILES * (2 * n_q + n_kv)].rearrange("p (t n) -> p t n", t=TILES)
        project(hT[:, 0:6, :], a["mla_w_uq"][0], 6, n_q, copy_to(q_tok), "act")
        project(hT[:, 6:8, :], a["mla_w_ukv"][0], 2, n_kv, copy_to(kv_tok), "act")
        steps = []
        for t in range(TILES):
            q3 = q_tok[:, t, :].rearrange("p (n d) -> p n d", n=MLA_HEADS)
            k3 = k_tok[:, t, :].rearrange("p (n d) -> p n d", n=MLA_HEADS)
            kv3 = kv_tok[:, t, :].rearrange("p (n d) -> p n d", n=MLA_HEADS)
            qr = q3[:, :, NOPE:MLA_D].rearrange("p n (b c) -> p n b c", b=2)
            kr = mixed[:, t, D:D + ROPE].rearrange("p (n b c) -> p n b c", n=1, b=2)
            steps.append(rotate(qr, qr, MLA_HEADS, ROPE // 2, t, 2))
            steps.append(rotate(kr, kr, 1, ROPE // 2, t, 2))

            def keys(e, k3=k3, kv3=kv3, t=t):
                chains["dve"].add(e.tensor_copy(k3[:, :, 0:NOPE], kv3[:, :, 0:NOPE]))
                chains["dve"].add(e.tensor_copy(k3[:, :, NOPE:MLA_D], mixed[:, t, D:D + ROPE].unsqueeze(1)
                                                .to_broadcast([P, MLA_HEADS, ROPE])))
            steps.append(keys)
        dve_stage(steps)
        qh = turned[:, 0:16 * SEQ].rearrange("p (n s) -> p n s", s=SEQ)
        kh = turned[:, 16 * SEQ:32 * SEQ].rearrange("p (n s) -> p n s", s=SEQ)
        blocks = []
        for t in range(TILES):
            for src, dst in ((q_tok, qh), (k_tok, kh)):
                for n0 in range(0, MLA_HEADS, 4):
                    blocks.append(([src[:, t, n * MLA_D:(n + 1) * MLA_D] for n in range(n0, n0 + 4)],
                                   dst[0:MLA_D, n0:n0 + 4, t * P:(t + 1) * P]))
        turn(blocks)
        groups = []
        for t in range(TILES):
            for n0 in range(0, MLA_HEADS, 4):
                groups.append(dict(
                    kind="softmax", tile=t, scale=MLA_D ** -0.5, bias=causal[:, t, 0:P * (t + 1)],
                    maps=[(qh[0:MLA_D, n, t * P:(t + 1) * P], kh[0:MLA_D, n, 0:P * (t + 1)]) for n in range(n0, n0 + 4)],
                    values=[(lambda c, n=n: kv_tok[:, c, n * P + NOPE:(n + 1) * P]) for n in range(n0, n0 + 4)],
                    out_ap=mixed[:, t, n0 * HD:(n0 + 4) * HD].rearrange("p (n d) -> p n d", d=HD)))
        attend(groups)
        turn_wide(M, T, DC)
        project(T, a["mla_w_out"][0], DC, D, add_residual, "dve")
        peer(1)

        norm(X, M, D, a["final_norm"])
        dve_stage([lambda e, t=t: e.tensor_copy(X(t), M(t)) for t in range(TILES)])

        norm(X, H, D, a["mix_norm_g_2"])
        turn_wide(H, hT, DC)
        mix = tok[:, 0:TILES * MIX].rearrange("p (t n) -> p t n", t=TILES)
        project(hT, a["w_in_2"][0][:, 0:MIX], DC, MIX, copy_to(mix), "act")
        (S_Q, S_K, S_V, D_Q, D_K, D_V, F_Q, F_K, F_V, F_F, E_Q, E_K, E_V) = (
            int(c) for c in np.cumsum([0, 256, 256, 256, 768, 768, 768, 256, 256, 256, 4, 256, 256]))
        T_SQ, T_SK, T_DQ, T_DK, T_FQ, T_FK, T_EQ, T_EK = 0, 2, 4, 10, 16, 18, 20, 24
        blocks = []
        for t in range(TILES):
            for col, first, n in ((S_Q, T_SQ, 4), (D_Q, T_DQ, 4), (D_Q + 512, T_DQ + 4, 4), (D_K + 256, T_DK + 2, 4),
                                  (F_Q, T_FQ, 4)):
                blocks.append(([mix[:, t, col + c * P:col + (c + 1) * P] for c in range(n)],
                               T[:, first:first + n, t * P:(t + 1) * P]))
            for col, first in ((E_Q, T_EQ), (E_K, T_EK)):
                blocks.append(([mix[:, t, col + c * HD:col + (c + 1) * HD] for c in range(4)],
                               T[0:HD, first:first + 4, t * P:(t + 1) * P]))
        turn(blocks)

        fl_in, fl_out = to_act.plan(), from_act.plan()
        l_in, l_out = to_act.plan(), from_act.plan()
        col_unit = products.take()
        key_units = [products.take() for _ in range(2)]
        bf = small[:, 0:4]
        lams = small[:, 8:136].rearrange("p (n d) -> p n d", n=4)
        lf_b = stick_tmp[:, :, :].rearrange("p a b -> p (a b)").rearrange("p (r h q) -> p r h q", r=TILES, h=4)
        cum_q = small[:, 140:148].rearrange("p (t h) -> p t h", t=TILES)
        cum_pe = var_ready.plan()
        causal_in = [causal[:, t, 0:P * (t + 1)] for t in range(TILES)]
        diff_gain = small[:, 150:214]
        last_landed = sem("last_landed")
        masks_made = sem("masks_made")

        def masks_dve(e):
            link = chains["dve"]
            e.wait_ge(masks_made, 1)
            e.wait_ge(last_landed, 48)
            fv = mix[:, :, F_F:F_F + 4]
            f0 = forget[:, :, :]
            f1 = stat[:, 0:8].rearrange("p (t h) -> p t h", t=TILES)
            link(e.tensor_tensor(f0, fv, bf.unsqueeze(1).to_broadcast([P, TILES, 4]), ALU.add))
            link(e.scalar_tensor_tensor(f1, f0, -1.0, f0, ALU.mult, ALU.max))
            e.tensor_scalar(f1, f1, -1.0, None, ALU.mult).then_inc(to_act.sem, 1)
            e.wait_ge(from_act.sem, fl_out)
            link(e.scalar_tensor_tensor(f0, f0, 0.0, f1, ALU.min, ALU.subtract))
            for r in range(TILES):
                last = e.tensor_copy(lf_b[:, r], f0[:, r, :].unsqueeze(2).to_broadcast([P, 4, P]))
            last.then_inc(var_ready.sem, 1)
            for i in range(2):
                last = e.tensor_tensor_reduce(lams[:, 2 * i, :], lams[:, 2 * i, :], lams[:, 2 * i + 1, :], 1.0, 0.0,
                                              ALU.mult, ALU.add, stat[:, 8 + i:9 + i])
            last.then_inc(to_act.sem, 1)
            e.wait_ge(from_act.sem, l_out)
            link(e.tensor_tensor(lam, stat[:, 8:9], stat[:, 9:10], ALU.subtract))
            link(e.tensor_scalar(lam, lam, LAMBDA_INIT, None, ALU.add))
            link(e.tensor_scalar(diff_gain, diff_gain, 1.0 - LAMBDA_INIT, None, ALU.mult))
            link.add(e.memset(zero, 0.0))
            link.add(e.tensor_scalar(strict, dist, 0.0, None, ALU.is_gt))
            link.add(e.tensor_scalar(strict_bias, dist, 0.0, NEG, ALU.is_le, ALU.mult))
            di = window.bitcast(I32)
            for g in (1, 2):
                link(e.tensor_copy(di, dist))
                link(e.tensor_scalar(di, di, DIL[g][1] - 1, None, ALU.bitwise_and))
                link(e.tensor_copy(dil_bias[g], di))
                link(e.tensor_scalar(dil_bias[g], dil_bias[g], 0.0, NEG, ALU.not_equal, ALU.mult))
                link(e.tensor_tensor(dil_bias[g], dil_bias[g], causal[:, :, :], ALU.add))
            link(e.tensor_scalar(window, dist, float(DIL[0][0]), NEG, ALU.is_gt, ALU.mult))
            link(e.tensor_tensor(window, window, causal[:, :, :], ALU.add))
            col_unit.wait_full(e)
            e.tensor_copy(cum_q, col_unit.ap[:, 0:8].rearrange("p (t h) -> p t h", t=TILES)
                          ).then_inc(col_unit.free, 1)
            for j, u in enumerate(key_units):
                u.wait_full(e)
                e.tensor_copy(cum_keys[:, 2 * j:2 * j + 2, :], u.ap.rearrange("p (n s) -> p n s", n=2)
                              ).then_inc(u.free, 1)

        def masks_act(e):
            link = chains["act"]
            f1 = stat[:, 0:8]
            e.wait_ge(to_act.sem, fl_in)
            link(e.activation(f1, f1, ACT.Exp))
            e.activation(f1, f1, ACT.Ln, bias=1.0).then_inc(from_act.sem, 1)
            e.wait_ge(to_act.sem, l_in)
            e.activation(stat[:, 8:10], stat[:, 8:10], ACT.Exp).then_inc(from_act.sem, 1)

        def masks_pe(e):
            e.wait_ge(masks_made, 1)
            e.wait_ge(var_ready.sem, cum_pe)
            col_unit.wait_free(e)
            for t in range(TILES):
                for r in range(t + 1):
                    last = e.matmul(col_unit.ap[:, 4 * t:4 * t + 4], upper[:, r, t * P:(t + 1) * P], forget[:, r, :],
                                    start=r == 0, stop=r == t)
            last.then_inc(col_unit.full, 1)
            for j, u in enumerate(key_units):
                u.wait_free(e)
                for i in range(2):
                    for r in range(TILES):
                        last = e.matmul(u.ap[:, i * SEQ:(i + 1) * SEQ], lf_b[:, r, 2 * j + i, :], upper[:, r, :],
                                        start=r == 0, stop=r == TILES - 1)
                last.then_inc(u.full, 1)

        masks_stage = len(stages)
        stage(pe=masks_pe, act=masks_act, dve=masks_dve)

        def bias_of(t, make):
            def before(e):
                for i in range(4):
                    make(e, i)
                chains["dve"].wait()
            return before

        def masked_slope(t, masks, slopes):
            w = P * (t + 1)

            def before(e):
                link = chains["dve"]
                link.wait()
                for i, (m, s) in enumerate(zip(masks, slopes)):
                    link.add(e.scalar_tensor_tensor(head_bias[:, i, 0:w], dist[:, t, 0:w], -s, m[:, t, 0:w],
                                                    ALU.mult, ALU.add))
                link.wait()
            return before

        def forget_bias(t):
            w = P * (t + 1)

            def before(e):
                link = chains["dve"]
                for i in range(4):
                    link.add(e.scalar_tensor_tensor(head_bias[:, i, 0:w], causal[:, t, 0:w], cum_q[:, t, i:i + 1],
                                                    cum_keys[:, i, 0:w], ALU.add, ALU.subtract))
                link.wait()
            return before

        def two_T(first, i, t, n=1):
            return T[(i % 2) * HD:(i % 2) * HD + HD, first + i // 2, t * P:t * P + n * P]

        groups = []
        for t in range(TILES):
            w = P * (t + 1)
            groups.append(dict(
                kind="stick", tile=t, scale=HD ** -0.5, bias=strict_bias[:, t, 0:w], strict=strict[:, t, 0:w],
                maps=[(two_T(T_SQ, i, t), two_T(T_SK, i, 0, t + 1)) for i in range(4)],
                values=[(lambda c, i=i: mix[:, c, S_V + i * HD:S_V + (i + 1) * HD]) for i in range(4)],
                out_ap=mixed[:, t, 0:256].rearrange("p (n d) -> p n d", d=HD)))
            for i in range(4):
                groups.append(dict(
                    kind="joint", tile=t, scale=HD ** -0.5, bias=[head_bias[:, g, 0:w] for g in range(3)],
                    before=masked_slope(t, [window] + dil_bias[1:], [SLOPES_DIL[g][i] for g in range(3)]),
                    maps=[(two_T(T_DQ, 4 * g + i, t), two_T(T_DK, 4 * g + i, 0, t + 1)) for g in range(3)],
                    values=[(lambda c, n=4 * g + i: mix[:, c, D_V + n * HD:D_V + (n + 1) * HD]) for g in range(3)],
                    out_ap=mixed[:, t, 256 + i * HD:256 + (i + 1) * HD].rearrange("p (n d) -> p n d", n=1)))
            groups.append(dict(
                kind="softmax", tile=t, scale=HD ** -0.5, bias=[head_bias[:, i, 0:w] for i in range(4)],
                before=forget_bias(t),
                maps=[(two_T(T_FQ, i, t), two_T(T_FK, i, 0, t + 1)) for i in range(4)],
                values=[(lambda c, i=i: mix[:, c, F_V + i * HD:F_V + (i + 1) * HD]) for i in range(4)],
                out_ap=mixed[:, t, 512:768].rearrange("p (n d) -> p n d", d=HD)))
            for j in range(2):
                hs = (2 * j, 2 * j + 1)
                order = [(n, c) for n in hs for c in range(2)]
                groups.append(dict(
                    kind="diff", tile=t, scale=32 ** -0.5, bias=[head_bias[:, i // 2, 0:w] for i in range(4)],
                    before=masked_slope(t, [causal, causal], [SLOPES_DIFF[n] for n in hs]),
                    maps=[(T[32 * c:32 * c + 32, T_EQ + n, t * P:(t + 1) * P], T[32 * c:32 * c + 32, T_EK + n, 0:w])
                          for n, c in order],
                    values=[(lambda c, n=n: mix[:, c, E_V + n * HD:E_V + (n + 1) * HD]) for n in hs],
                    out_ap=mixed[:, t, 768 + 128 * j:896 + 128 * j].rearrange("p (n d) -> p n d", d=HD)))
        attend(groups)

        heads = mixed[:, :, 768:1024].rearrange("p t (n d) -> p t n d", d=HD)
        v_value, r_value = var_ready.plan(), root_ready.plan()

        def diff_norm_dve(e):
            link = chains["dve"]
            sq = probs[:, 0, :, :].rearrange("p a b -> p (a b)")[:, 0:512].rearrange("p (t n d) -> p t n d", t=TILES, n=4)
            var, root, y, t1 = (stat[:, 8 * i:8 * i + 8] for i in range(4))
            for t in range(TILES):
                link.add(e.tensor_tensor(sq[:, t], heads[:, t], heads[:, t], ALU.mult))
            link.wait()
            link(e.tensor_reduce(var, sq.rearrange("p t n d -> p (t n) d"), AX.X, ALU.add))
            e.tensor_scalar(var, var, 1.0 / HD, EPS, ALU.mult, ALU.add).then_inc(var_ready.sem, 1)
            e.wait_ge(root_ready.sem, r_value)
            link(e.reciprocal(y, root))
            link(e.tensor_tensor(t1, y, y, ALU.mult))
            link(e.tensor_tensor(t1, t1, var, ALU.mult))
            link(e.tensor_scalar(t1, t1, -0.5, 1.5, ALU.mult, ALU.add))
            link(e.tensor_tensor(y, y, t1, ALU.mult))
            for t in range(TILES):
                link(e.tensor_tensor(heads[:, t], heads[:, t],
                                     y[:, 4 * t:4 * t + 4].unsqueeze(2).to_broadcast([P, 4, HD]), ALU.mult))
                link(e.tensor_tensor(heads[:, t], heads[:, t],
                                     diff_gain.unsqueeze(1).to_broadcast([P, 4, HD]), ALU.mult))

        def diff_norm_act(e):
            e.wait_ge(var_ready.sem, v_value)
            e.activation(stat[:, 8:16], stat[:, 0:8], ACT.Sqrt).then_inc(root_ready.sem, 1)

        stage(act=diff_norm_act, dve=diff_norm_dve)
        turn_wide(M, T, DC)

        w_in = rows_of(a["w_in_2"][0])
        w_branch = a["w_branch_2"][0]
        plan = []
        for n in range(4):
            branch = None
            for half in range(2):
                c0 = MIX + n * D + half * 512
                slots = [(weights(w_in[:, k:k + 4, c0:c0 + 512], 4, 512), k) for k in (0, 4)]
                if half == 0:
                    branch = weights(rows_of(w_branch[n]), 2, D)
                for t in range(TILES):
                    plan.append((n, half, t, slots, branch, products.take(), products.take(),
                                 relu_used.plan() if n else None))
                for s, _ in slots:
                    given_back[s] = plan[-1][5].full_at()
                given_back[branch] = plan[-1][6].full_at()
        gated = mixed

        def gate_pe(e):
            for n, half, t, slots, branch, ug, ub, _ in plan:
                for s, _ in slots:
                    slot_wait(e, s)
                ug.wait_free(e)
                for s, k0 in slots:
                    for k in range(4):
                        last = e.matmul(ug.ap, hT[:, k0 + k, t * P:(t + 1) * P], slot_ap(s)[:, k, :],
                                        start=k0 + k == 0, stop=k0 + k == DC - 1)
                last.then_inc(ug.full, 1)
                slot_wait(e, branch)
                ub.wait_free(e)
                for k in range(2):
                    last = e.matmul(ub.ap, T[:, 2 * n + k, t * P:(t + 1) * P],
                                    slot_ap(branch)[:, k, half * 512:half * 512 + 512], start=k == 0, stop=k == 1)
                last.then_inc(ub.full, 1)

        def gate_act(e):
            for i, (_, _, _, _, _, ug, _, _) in enumerate(plan):
                if i >= 2:
                    before, used = plan[i - 2][6], plan[i - 2][7]
                    if used is None:
                        before.wait_emptied(e)
                    else:
                        e.wait_ge(relu_used.sem, used)
                ug.wait_full(e)
                e.activation(gates[:, i % 2, :], ug.ap, ACT.Sigmoid).then_inc(ug.free, 1)

        def gate_dve(e):
            link = chains["dve"]
            for i, (n, half, t, _, _, ug, ub, _) in enumerate(plan):
                ug.wait_emptied(e)
                ub.wait_full(e)
                g = gates[:, i % 2, :]
                y = gated[:, t, half * 512:half * 512 + 512]
                if n == 0:
                    e.tensor_tensor(y, g, ub.ap, ALU.mult).then_inc(ub.free, 1)
                else:
                    e.tensor_tensor(g, g, ub.ap, ALU.mult).then_inc(ub.free, 1)
                    e.wait_ge(ub.free, ub.use + 1)
                    e.tensor_tensor(y, y, g, ALU.add).then_inc(relu_used.sem, 1)

        stage(pe=gate_pe, act=gate_act, dve=gate_dve)
        turn_wide(M, hT, DC)
        project(hT, a["w_out_2"][0], DC, D, add_residual, "dve")

        norm(X, H, D, a["mlp_norm_g_2"])
        turn_wide(H, hT, DC)
        w_up = rows_of(a["w_up_2"][0])
        up_plan = []
        for b in range(8):
            slots = [(weights(w_up[:, k:k + 4, b * 512:(b + 1) * 512], 4, 512), k) for k in (0, 4)]
            up_plan.append((b, slots, [products.take() for _ in range(2)]))
            for s, _ in slots:
                given_back[s] = up_plan[-1][2][-1].full_at()

        def up_pe(e):
            for b, slots, units in up_plan:
                for s, _ in slots:
                    slot_wait(e, s)
                for j, u in enumerate(units):
                    u.wait_free(e)
                    for i in range(2):
                        f = (2 * j + i) * P
                        for s, k0 in slots:
                            for k in range(4):
                                last = e.matmul(u.ap[:, i * SEQ:(i + 1) * SEQ], slot_ap(s)[:, k, f:f + P],
                                                hT[:, k0 + k, :], start=k0 + k == 0, stop=k0 + k == DC - 1)
                    last.then_inc(u.full, 1)

        def up_act(e):
            for b, _, units in up_plan:
                for j, u in enumerate(units):
                    u.wait_full(e)
                    e.activation(T[:, 4 * b + 2 * j:4 * b + 2 * j + 2, :], u.ap.rearrange("p (n s) -> p n s", n=2),
                                 ACT.Relu).then_inc(u.free, 1)

        def up_dve(e):
            for b, _, units in up_plan:
                for j, u in enumerate(units):
                    u.wait_emptied(e)
                    v = T[:, 4 * b + 2 * j:4 * b + 2 * j + 2, :]
                    e.tensor_tensor(v, v, v, ALU.mult)

        stage(pe=up_pe, act=up_act, dve=up_dve)
        project(T, a["w_down_2"][0], 32, D, add_residual, "dve")
        norm(X, H, D, a["final_norm_g_2"])

        block = ctx.enter_context(nc.Block())

        @block.sync
        def _(sp):
            sp.dma_start(raw[:, 2:4].bitcast(I32), a["positions"]).then_inc(consts_landed, 16)
            sp.dma_start(small[:, 0:32], a["inv_freq"].to_broadcast([P, 32])).then_inc(consts_landed, 16)
            load_gain(sp, 0)
            sp.dma_start(x[:, :, :], a["x"].rearrange("(t p) d -> p t d", p=P)).then_inc(x_landed, 16)
            for n, (view, chunks, cols) in enumerate(stream):
                if n >= SLOTS:
                    sp.wait_ge(*given_back[n - SLOTS])
                sp.dma_start(slot_ap(n), view).then_inc(w_landed[n % SLOTS], 16)
            for t in range(TILES):
                sp.wait_ge(done["dve"], len(stages))
                sp.dma_start(out.rearrange("(t p) d -> p t d", p=P)[:, t, :], h[:, t, :]).then_inc(out_landed, 16)
            sp.wait_ge(out_landed, 16 * TILES)

        @block.gpsimd
        def _(pool):
            step = Chain(pool, pool_step)
            step.add(pool.memset(ident[:, :], 0.0))
            step(pool.memset(causal[:, :, :], 0.0))
            step.add(pool.affine_select(ident[:, :], ident[:, :], pattern=[[-1, P]], compare_op=ALU.not_equal,
                                        fill=1.0, base=0, channel_multiplier=1))
            step.add(pool.affine_select(causal[:, :, :], causal[:, :, :], pattern=[[P, TILES], [-1, SEQ]],
                                        compare_op=ALU.is_ge, fill=NEG, base=0, channel_multiplier=1))
            step(pool.iota(iota16[:, :], pattern=[[1, TOP]], base=0, channel_multiplier=0,
                           allow_small_or_imprecise_dtypes=True))
            pool.drain().then_inc(pool_made, 1)
            g = 0
            for layer, t, ready in gathers:
                pool.wait_ge(experts_ready.sem, ready)
                n0 = g * P
                for i in range(P + TOP):
                    if i < P:
                        n = n0 + i
                        if n >= U_SLOTS:
                            pool.wait_ge(u_used.sem, n - U_SLOTS + 1)
                        pool.indirect_dma_start(
                            rows[:, n % U_SLOTS, :], None, a["peer_u"],
                            bass.IndirectOffsetOnAxis(ap=expert[:, t, i:i + 1], axis=0)).then_inc(u_landed[n % U_SLOTS], 16)
                    if i >= TOP:
                        n = n0 + i - TOP
                        if n >= V_SLOTS:
                            pool.wait_ge(v_used.sem, n - V_SLOTS + 1)
                        pool.indirect_dma_start(
                            rows[:, U_SLOTS + n % V_SLOTS, :], None, a["peer_v"],
                            bass.IndirectOffsetOnAxis(ap=expert[:, t, i - TOP:i - TOP + 1], axis=0)
                        ).then_inc(v_landed[n % V_SLOTS], 16)
                g += 1
            for e in ("dve", "act", "pe"):
                pool.wait_ge(done[e], masks_stage)
            step.add(pool.iota(dist, pattern=[[P, TILES], [-1, SEQ]], base=0, channel_multiplier=1,
                               allow_small_or_imprecise_dtypes=True))
            step(pool.memset(upper, 1.0))
            step(pool.affine_select(upper, upper, pattern=[[-P, TILES], [1, SEQ]], compare_op=ALU.is_ge, fill=0.0,
                                    base=0, channel_multiplier=-1))
            pool.dma_start(small[:, 0:4], a["b_forget_2"].to_broadcast([P, 4])).then_inc(last_landed, 16)
            pool.dma_start(small[:, 8:136], a["lambdas"].to_broadcast([P, 128])).then_inc(last_landed, 16)
            pool.dma_start(diff_gain, a["diff_norm_g_2"].to_broadcast([P, HD])).then_inc(last_landed, 16)
            pool.drain().then_inc(masks_made, 1)

        @block.scalar
        def _(act):
            chains["act"] = Chain(act, act_step)
            run_stages("act", act)

        @block.vector
        def _(dve):
            chains["dve"] = Chain(dve, dve_step)
            run_stages("dve", dve)

        @block.tensor
        def _(pe):
            run_stages("pe", pe)


INPUTS = ["x", "positions", "attn_norm", "ffn_norm", "final_norm", "hyb_w_in", "hyb_w_out", "mla_w_in", "mla_q_norm",
          "mla_kv_norm", "mla_w_uq", "mla_w_ukv", "mla_w_out", "peer_w_q", "peer_keys", "peer_u", "peer_v",
          "mix_norm_g_2", "w_in_2", "b_forget_2", "lambdas", "diff_norm_g_2", "w_branch_2", "w_out_2",
          "mlp_norm_g_2", "w_up_2", "w_down_2", "final_norm_g_2", "inv_freq"]


def kernel(**inputs):
    import concourse.bacc as bacc
    from concourse.bass_utils import run_bass_kernel_spmd

    got = {k: np.asarray(v) for k, v in inputs.items()}
    lambdas = [got.pop(f"lambda_{n}_2") for n in ("q1", "k1", "q2", "k2")]
    keys = got.pop("peer_sub_keys")
    layers = keys.shape[0]
    laid = got | {
        "x": got["x"].reshape(SEQ, D),
        "positions": got["positions"].reshape(TILES, P).T,
        "final_norm": got["final_norm"].reshape(1, D),
        "final_norm_g_2": got["final_norm_g_2"].reshape(1, D),
        "peer_u": got["peer_u"].reshape(-1, D),
        "peer_v": got["peer_v"].reshape(-1, D),
        "peer_keys": keys.transpose(0, 4, 1, 2, 3).reshape(layers, P, EH * 2 * NK),
        "lambdas": np.concatenate(lambdas, axis=1),
        "inv_freq": (1.0 / 10000.0 ** (np.arange(0, HD, 2, dtype=np.float32) / HD)).astype(np.float32).reshape(1, 32),
    }
    nc = bacc.Bacc("TRN2", target_bir_lowering=False, num_devices=1)
    arrays, a = {}, {}
    for name in INPUTS:
        v = np.ascontiguousarray(laid[name])
        arrays[f"in_{name}"] = v
        a[name] = nc.dram_tensor(f"in_{name}", v.shape, mybir.dt.from_np(v.dtype), kind="ExternalInput").ap()
    out = nc.dram_tensor("out_0", (SEQ, D), F32, kind="ExternalOutput").ap()
    build(nc, a, out)
    r = run_bass_kernel_spmd(nc, [arrays], core_ids=[0])
    return r.results[0]["out_0"].reshape(1, SEQ, D)
```

```python
from contextlib import ExitStack

import numpy as np

import concourse.bass as bass
from concourse import mybir

ALU = mybir.AluOpType
ACT = mybir.ActivationFunctionType
F32 = mybir.dt.float32
I32 = mybir.dt.int32
U32 = mybir.dt.uint32
AX = mybir.AxisListType

P = 128
SEQ = 256
TILES = SEQ // P
D = 1024
DC = D // P
EPS = 1e-6
NEG = -1.0e30
TAKEN = -3.0e38
SLOT = 2048
SLOTS = 5
U_SLOTS = 4
V_SLOTS = 4
DIAGS = 4

HD = 64
QA, KA, VA, IQ, IK, IW, QB, KB, VB = (int(c) for c in np.cumsum([0, 512, 64, 64, 512, 64, 8, 512, 512]))
EVEN_COLS = VB + 512
DSA_KEEP = 64
KV_RANK, Q_RANK, ROPE = 256, 768, 32
MLA_HEADS, NOPE = 16, 64
MLA_D = NOPE + ROPE
EH, NK, TOP = 8, 128, 16
LAG = TOP + 2
ITEMS = EH * TOP + LAG
RATE = 0.6
MIX = 4612
SLOPES = [float(np.float32(2.0 ** (-8.0 * n / 16))) for n in range(1, 17)]
DIL = ((128, 1), (512, 4), (2048, 16))
SLOPES_DIL = [SLOPES[0:4], SLOPES[8:12], SLOPES[12:16]]
SLOPES_DIFF = SLOPES[4:8]
LAMBDA_INIT = 0.2
TWO_PI = 2 * np.pi
C1 = 6.28125
C2 = float(np.float32(np.round((TWO_PI - C1) * 2 ** 21) / 2 ** 21))
C3 = float(TWO_PI - C1 - C2)
ROUND = 12582912.0


class Banks:

    def __init__(self, views, full, free):
        self.views, self.full, self.free, self.n = views, full, free, 0

    def take(self):
        b, use = self.n % len(self.views), self.n // len(self.views)
        self.n += 1
        return Unit(self, b, use)


class Unit:

    def __init__(self, banks, b, use):
        self.ap, self.b, self.use = banks.views[b], b, use
        self.full, self.free = banks.full[b], banks.free[b]

    def wait_free(self, pe):
        if self.use:
            pe.wait_ge(self.free, self.use)

    def wait_full(self, eng):
        eng.wait_ge(self.full, self.use + 1)

    def wait_emptied(self, eng):
        eng.wait_ge(self.free, self.use + 1)

    def full_at(self):
        return self.full, self.use + 1


class Signal:

    def __init__(self, sem):
        self.sem, self.n = sem, 0

    def plan(self, k=1):
        self.n += k
        return self.n


class Chain:

    def __init__(self, eng, sem):
        self.eng, self.sem, self.n = eng, sem, 0

    def __call__(self, ins):
        self.n += 1
        ins.then_inc(self.sem, 1)
        self.eng.wait_ge(self.sem, self.n)

    def add(self, ins):
        self.n += 1
        ins.then_inc(self.sem, 1)

    def wait(self):
        self.eng.wait_ge(self.sem, self.n)


def build(nc, a, out):
    with ExitStack() as ctx:
        def sb(name, shape, dt=F32):
            return ctx.enter_context(nc.sbuf_tensor("sb_" + name, shape, dt))

        def sem(name):
            return ctx.enter_context(nc.semaphore(name))

        psum = [ctx.enter_context(nc.psum_tensor(f"bank{i}", [P, 512], F32)) for i in range(2)]
        ps_scores = ctx.enter_context(nc.psum_tensor("ps_scores", [P, 4, SEQ], F32))
        ps_turn = [ctx.enter_context(nc.psum_tensor(f"ps_turn{i}", [P, 512], F32)) for i in range(2)]
        ps_acc = ctx.enter_context(nc.psum_tensor("ps_acc", [P, D], F32))

        x = sb("x", [P, TILES, D])
        h = sb("h", [P, TILES, D])
        hT = sb("hT", [P, DC, SEQ])
        mixed = sb("mixed", [P, TILES, 1056])
        probs = sb("probs", [P, 2, 4, SEQ])
        probsT = sb("probsT", [P, 2, 2, 4, P])
        wring = sb("wring", [P, SLOTS, SLOT])
        rows = sb("rows", [P, U_SLOTS + V_SLOTS, D])
        tok = sb("tok", [P, 10496])
        turned = sb("turned", [P, 32 * SEQ])
        gain = sb("gain", [P, D])
        ident = sb("ident", [P, P])
        causal = sb("causal", [P, TILES, SEQ])
        cos = sb("cos", [P, TILES, 32])
        sin = sb("sin", [P, TILES, 32])
        small = sb("small", [P, 256])
        stat = sb("stat", [P, 64])
        expert = sb("expert", [P, TILES, P], I32)
        share = sb("share", [P, TILES, P])
        dots = sb("dots", [P, P])
        gelu = sb("gelu", [P, 2, TOP])
        weight = sb("weight", [P, P])
        diag = sb("diag", [P, DIAGS, P])

        w_landed = [sem(f"w_landed{i}") for i in range(SLOTS)]
        w_used = Signal(sem("w_used"))
        gain_landed = Signal(sem("gain_landed"))
        gain_used = Signal(sem("gain_used"))
        x_landed = sem("x_landed")
        consts_landed = sem("consts_landed")
        pool_made = sem("pool_made")
        pool_step = sem("pool_step")
        dve_step = sem("dve_step")
        act_step = sem("act_step")
        done = {e: sem(f"stage_done_{e}") for e in ("pe", "act", "dve")}
        var_ready = Signal(sem("var_ready"))
        root_ready = Signal(sem("root_ready"))
        maxes_ready = Signal(sem("maxes_ready"))
        probs_ready = Signal(sem("probs_ready"))
        relu_used = Signal(sem("relu_used"))
        to_act = Signal(sem("to_act"))
        from_act = Signal(sem("from_act"))
        experts_ready = Signal(sem("experts_ready"))
        u_landed = [sem(f"u_landed{i}") for i in range(U_SLOTS)]
        v_landed = [sem(f"v_landed{i}") for i in range(V_SLOTS)]
        u_used = Signal(sem("u_used"))
        v_used = Signal(sem("v_used"))
        gelu_ready = Signal(sem("gelu_ready"))
        weights_ready = Signal(sem("weights_ready"))
        diag_ready = Signal(sem("diag_ready"))
        out_landed = sem("out_landed")

        pair = [sem(f"product_full{i}") for i in range(2)], [sem(f"product_free{i}") for i in range(2)]
        products = Banks([b[:, :] for b in psum], *pair)
        pair = [sem(f"turn_full{i}") for i in range(2)], [sem(f"turn_free{i}") for i in range(2)]
        turns = Banks([b[:, :] for b in ps_turn], *pair)
        scores = Banks([ps_scores[:, :, :]], [sem("scores_full")], [sem("scores_free")])

        stages = []
        stream = []
        given_back = {}
        ends = {"pe": 0, "act": 0, "dve": 0}
        chains = {}

        feeds = []

        def handed_out(f, weight):
            return f["first"] + int(weight * min((P - f["first"]) / max(f["weight"], 1.0), RATE))

        def point(us):
            f = feeds[-1] if feeds and feeds[-1]["open"] else None
            if f is None:
                return lambda name, e: None
            f["weight"] += us
            behind = f["weight"]
            f["cuts"].append(behind)

            def run(name, e):
                at = f["cuts"].index(behind)
                for i in range(handed_out(f, f["cuts"][at - 1] if at else 0), handed_out(f, behind)):
                    f[name](e, i)
            return run

        def stage(pe=None, act=None, dve=None, points=(), us=1.0):
            stages.append({"pe": pe, "act": act, "dve": dve, "points": points, "after": point(us)})

        def run_stages(name, eng):
            others = [n for n in ("pe", "act", "dve") if n != name]
            for k, s in enumerate(stages):
                if s[name] is not None:
                    s[name](eng)
                else:
                    for p in s["points"]:
                        p(name, eng)
                s["after"](name, eng)
                eng.drain().then_inc(done[name], 1)
                for n in others:
                    eng.wait_ge(done[n], k + 1)

        def weights(view, chunks, cols):
            stream.append((view, chunks, cols))
            return len(stream) - 1

        def slot_ap(n):
            _, chunks, cols = stream[n]
            return wring[:, n % SLOTS, 0:chunks * cols].rearrange("p (c n) -> p c n", c=chunks)

        def slot_wait(pe, n):
            pe.wait_ge(w_landed[n % SLOTS], 16 * (n // SLOTS + 1))

        def rows_of(w):
            return w.rearrange("(c p) n -> p c n", p=P)

        gains = []
        squares = [probs[:, i].rearrange("p a b -> p (a b)") for i in range(2)]

        def norm(src, dst, width, g, tiles=range(TILES)):
            gains.append((g, width))
            number = len(gains)
            g_value = gain_landed.plan(16)
            n = len(tiles)
            v_value, r_value = var_ready.plan(), root_ready.plan()
            gain_used.plan()
            var, root, y, t1 = (stat[:, 4 * i:4 * i + n] for i in range(4))
            p = point(4.0)

            def dve(e):
                link = chains["dve"]
                for i, t in enumerate(tiles):
                    link.add(e.tensor_tensor_reduce(squares[t][:, 0:width], src(t), src(t), 1.0 / width, 0.0, ALU.mult, ALU.add,
                                                    stat[:, i:i + 1]))
                link.wait()
                e.tensor_scalar(var, var, EPS, None, ALU.add).then_inc(var_ready.sem, 1)
                p("dve", e)
                e.wait_ge(root_ready.sem, r_value)
                link(e.reciprocal(y, root))
                link(e.tensor_tensor(t1, y, y, ALU.mult))
                link(e.tensor_tensor(t1, t1, var, ALU.mult))
                link(e.tensor_scalar(t1, t1, -0.5, 1.5, ALU.mult, ALU.add))
                link(e.tensor_tensor(y, y, t1, ALU.mult))
                e.wait_ge(gain_landed.sem, g_value)
                for i, t in enumerate(tiles):
                    last = e.scalar_tensor_tensor(dst(t), src(t), stat[:, 8 + i:9 + i], gain[:, 0:width],
                                                  ALU.mult, ALU.mult)
                last.then_inc(gain_used.sem, 1)

            def act(e):
                e.wait_ge(var_ready.sem, v_value)
                e.activation(root, var, ACT.Sqrt).then_inc(root_ready.sem, 1)
                p("act", e)
                if number < len(gains):
                    e.wait_ge(gain_used.sem, number)
                    load_gain(e, number)

            stage(act=act, dve=dve, points=[p], us=5.0)

        def load_gain(e, n):
            g, width = gains[n]
            e.dma_start(gain[:, 0:width], g.to_broadcast([P, width])).then_inc(gain_landed.sem, 16)

        def turn(blocks):
            plan = [(srcs, dst, turns.take()) for srcs, dst in blocks]
            points = [point(0.8) for _ in plan]

            def pe(e):
                for (srcs, dst, u), p in zip(plan, points):
                    w = dst.shape[0]
                    u.wait_free(e)
                    for i, s in enumerate(srcs):
                        last = e.transpose(u.ap[0:w, i * P:(i + 1) * P], s, ident[:, :])
                    last.then_inc(u.full, 1)
                    p("pe", e)

            def empty(e, b):
                for (srcs, dst, u), p in zip(plan, points):
                    if u.b == b:
                        u.wait_full(e)
                        w, n = dst.shape[0], len(srcs)
                        src = u.ap[0:w, 0:n * P].rearrange("p (n t) -> p n t", n=n)
                        copy = e.copy if b == 0 else e.tensor_copy
                        copy(dst, src).then_inc(u.free, 1)
                    p(("act", "dve")[b], e)

            stage(pe=pe, act=lambda e: empty(e, 0), dve=lambda e: empty(e, 1), points=points)

        def turn_wide(src, dst, chunks, tiles=range(TILES)):
            blocks = []
            for t in tiles:
                for c0 in range(0, chunks, 4):
                    n = min(4, chunks - c0)
                    blocks.append(([src(t)[:, c * P:(c + 1) * P] for c in range(c0, c0 + n)],
                                   dst[:, c0:c0 + n, t * P:(t + 1) * P]))
            turn(blocks)

        def project(xT, w, chunks, cols, empty, engine, tiles=range(TILES)):
            per = min(chunks, 4) if chunks != 6 else 3
            wide = SLOT // per // 512 * 512 if per < 4 else 512
            plan = []
            wv = rows_of(w)
            for n0 in range(0, cols, wide):
                wn = min(wide, cols - n0)
                slots = [(weights(wv[:, k:k + per, n0:n0 + wn], per, wn), k) for k in range(0, chunks, per)]
                blocks = range(0, wn, 512)
                for b0 in blocks:
                    bn = min(512, wn - b0)
                    units = [products.take() for _ in tiles]
                    plan.append((slots, b0, bn, n0 + b0, units, b0 == blocks[-1]))
                for s, k0 in slots:
                    last_use = units[-1].full_at() if k0 + per == chunks else (w_used.sem, w_used.plan())
                    given_back[s] = last_use
            points = [point(len(tiles) * chunks * 0.35) for _ in plan]

            def pe(e):
                for (slots, b0, bn, _, units, ends_slot), p in zip(plan, points):
                    for u in units:
                        u.wait_free(e)
                    for s, k0 in slots:
                        slot_wait(e, s)
                        sl = slot_ap(s)
                        for t, u in zip(tiles, units):
                            for k in range(per):
                                last = e.matmul(u.ap[:, 0:bn], xT[:, k0 + k, t * P:(t + 1) * P],
                                                sl[:, k, b0:b0 + bn], start=k0 + k == 0, stop=k0 + k == chunks - 1)
                            if k0 + per == chunks:
                                last.then_inc(u.full, 1)
                        if ends_slot and k0 + per < chunks:
                            last.then_inc(w_used.sem, 1)
                    p("pe", e)

            def other(e):
                for (_, _, bn, c0, units, _), p in zip(plan, points):
                    for t, u in zip(tiles, units):
                        u.wait_full(e)
                        empty(e, u.ap[:, 0:bn], t, c0, bn).then_inc(u.free, 1)
                    p(engine, e)

            stage(pe=pe, points=points, **{engine: other})

        def rotate(src, dst, heads, half, t, stride=1):
            c = cos[:, t, 0:32:stride].unsqueeze(1).to_broadcast([P, heads, half])
            s = sin[:, t, 0:32:stride].unsqueeze(1).to_broadcast([P, heads, half])
            x1, x2 = src[:, :, 0, :], src[:, :, 1, :]
            n = heads * half
            flat_probs = probs[:, :, :, :].rearrange("p a b c -> p (a b c)")
            tmp = [flat_probs[:, i * n:(i + 1) * n].rearrange("p (a b) -> p a b", a=heads) for i in range(4)]

            def dve(e):
                link = chains["dve"]
                link.add(e.tensor_tensor(tmp[0], x1, c, ALU.mult))
                link.add(e.tensor_tensor(tmp[1], x2, s, ALU.mult))
                link.add(e.tensor_tensor(tmp[2], x1, s, ALU.mult))
                link(e.tensor_tensor(tmp[3], x2, c, ALU.mult))
                link.add(e.tensor_tensor(dst[:, :, 0, :], tmp[0], tmp[1], ALU.subtract))
                link(e.tensor_tensor(dst[:, :, 1, :], tmp[2], tmp[3], ALU.add))
            return dve

        def dve_stage(steps):
            points = [point(3.0) for _ in steps]

            def dve(e):
                for s, p in zip(steps, points):
                    s(e)
                    p("dve", e)
            stage(dve=dve, points=points)

        def attend(groups):
            plan = []
            for g in groups:
                n_out = {"joint": 1, "diff": 2}.get(g["kind"], len(g["maps"]))
                n_turned = 2 if g["kind"] == "diff" else len(g["maps"])
                chunks = g["tile"] + 1
                value = {"s": scores.take(), "turns": [turns.take() for _ in range(chunks)], "out": products.take(),
                         "n_out": n_out, "n_turned": n_turned, "chunks": chunks, "w": P * chunks,
                         "m": maxes_ready.plan(), "p": probs_ready.plan()}
                if g["kind"] == "stick":
                    value["m2"] = maxes_ready.plan()
                    value["a1"] = from_act.plan()
                if g["kind"] == "diff":
                    value["a2"] = from_act.plan()
                plan.append(g | value | {"points": [point(6.0), point(6.0)]})

            def place(i):
                return (i % 2) * 2 + i // 2

            def places(g):
                n = len(g["maps"])
                return [place(i) for i in range(n)] if g["kind"] != "joint" else list(range(n))

            def pe(e):
                def score(g):
                    g["s"].wait_free(e)
                    for i, (q, k) in enumerate(g["maps"]):
                        last = e.matmul(g["s"].ap[:, places(g)[i], 0:g["w"]], q, k, start=True, stop=True)
                    last.then_inc(g["s"].full, 1)

                def apply(n, g):
                    e.wait_ge(probs_ready.sem, g["p"])
                    for c, u in enumerate(g["turns"]):
                        u.wait_free(e)
                        for i in range(g["n_turned"]):
                            at = i if g["kind"] == "diff" else places(g)[i]
                            last = e.transpose(u.ap[:, i * P:(i + 1) * P], probs[:, n % 2, at, c * P:(c + 1) * P],
                                               ident[:, :])
                        last.then_inc(u.full, 1)
                    u = g["out"]
                    for turned_unit in g["turns"]:
                        turned_unit.wait_emptied(e)
                    u.wait_free(e)
                    for i in range(g["n_turned"]):
                        o = 0 if g["kind"] == "joint" else i
                        for c in range(g["chunks"]):
                            first = c == 0 and (i == 0 or g["kind"] != "joint")
                            final = c == g["chunks"] - 1 and (i == g["n_turned"] - 1 or g["kind"] != "joint")
                            last = e.matmul(u.ap[:, o * HD:(o + 1) * HD], probsT[:, n % 2, c, i, :], g["values"][i](c),
                                            start=first, stop=final)
                    last.then_inc(u.full, 1)

                for n, g in enumerate(plan):
                    score(g)
                    g["points"][0]("pe", e)
                    if n:
                        apply(n - 1, plan[n - 1])
                    g["points"][1]("pe", e)
                apply(len(plan) - 1, plan[-1])

            def empty_turns(e, b, n, g):
                for c, u in enumerate(g["turns"]):
                    if u.b == b:
                        u.wait_full(e)
                        k = g["n_turned"]
                        copy = e.copy if b == 0 else e.tensor_copy
                        copy(probsT[:, n % 2, c, 0:k, :], u.ap[:, 0:k * P].rearrange("p (n t) -> p n t", n=k)
                             ).then_inc(u.free, 1)

            def act(e):
                link = chains["act"]
                for n, g in enumerate(plan):
                    w, k = g["w"], len(g["maps"])
                    pr = probs[:, n % 2]
                    sums = stat[:, 16 + 8 * (n % 2):24 + 8 * (n % 2)]
                    neg = stat[:, 32 + 8 * (n % 2):40 + 8 * (n % 2)]
                    if g["kind"] == "stick":
                        az = stick_tmp[:, :, 0:w]
                        g["s"].wait_full(e)
                        link(e.activation(az, g["s"].ap[:, :, 0:w], ACT.Abs, scale=g["scale"]))
                        link(e.activation(az, az, ACT.Exp, scale=-1.0))
                        e.activation(az, az, ACT.Ln, bias=1.0).then_inc(from_act.sem, 1)
                        e.wait_ge(maxes_ready.sem, g["m2"])
                        e.activation(pr[:, :, 0:w], pr[:, :, 0:w], ACT.Exp).then_inc(probs_ready.sem, 1)
                    else:
                        e.wait_ge(maxes_ready.sem, g["m"])
                        if g["kind"] == "joint":
                            last = e.activation(pr[:, 0:k, 0:w], pr[:, 0:k, 0:w], ACT.Exp, bias=neg[:, 0:1],
                                                accum_out=sums[:, 0:1])
                        else:
                            for i in sorted(places(g)):
                                last = e.activation(pr[:, i, 0:w], pr[:, i, 0:w], ACT.Exp, bias=neg[:, i:i + 1],
                                                    accum_out=sums[:, i:i + 1])
                        last.then_inc(from_act.sem if g["kind"] == "diff" else probs_ready.sem, 1)
                    g["points"][0]("act", e)
                    if n:
                        empty_turns(e, 0, n - 1, plan[n - 1])
                    g["points"][1]("act", e)
                empty_turns(e, 0, len(plan) - 1, plan[-1])

            def dve(e):
                link = chains["dve"]

                def soften(n, g):
                    w, k = g["w"], len(g["maps"])
                    pr = probs[:, n % 2]
                    neg = stat[:, 32 + 8 * (n % 2):40 + 8 * (n % 2)]
                    sums = stat[:, 16 + 8 * (n % 2):24 + 8 * (n % 2)]
                    s = g["s"].ap
                    if g["kind"] == "stick":
                        e.wait_ge(from_act.sem, g["a1"])
                        az = stick_tmp[:, :, 0:w]
                        z = pr[:, :, 0:w]
                        e.tensor_scalar(z, s[:, :, 0:w], g["scale"], None, ALU.mult).then_inc(g["s"].free, 1)
                        e.wait_ge(g["s"].free, g["s"].use + 1)
                        link(e.scalar_tensor_tensor(az, z, 0.0, az, ALU.max, ALU.add))
                        link(e.tensor_tensor(az, az, g["strict"].unsqueeze(1).to_broadcast([P, 4, w]), ALU.mult))
                        for i in range(4):
                            link.add(e.tensor_tensor_scan(az[:, i, ::-1], zero[:, 0:w], az[:, i, ::-1], 0.0,
                                                          ALU.add, ALU.add))
                        link.wait()
                        link(e.tensor_tensor(z, z, az, ALU.subtract))
                        e.tensor_tensor(z, z, g["bias"].unsqueeze(1).to_broadcast([P, 4, w]), ALU.add
                                        ).then_inc(maxes_ready.sem, 2)
                        return
                    g["s"].wait_full(e)
                    if isinstance(g["bias"], list):
                        for i in range(k):
                            at = places(g)[i]
                            last = e.scalar_tensor_tensor(pr[:, at, 0:w], s[:, at, 0:w], g["scale"], g["bias"][i],
                                                          ALU.mult, ALU.add)
                    else:
                        last = e.scalar_tensor_tensor(pr[:, 0:k, 0:w], s[:, 0:k, 0:w], g["scale"],
                                                      g["bias"].unsqueeze(1).to_broadcast([P, k, w]), ALU.mult, ALU.add)
                    last.then_inc(g["s"].free, 1)
                    e.wait_ge(g["s"].free, g["s"].use + 1)
                    if g["kind"] == "joint":
                        link(e.tensor_reduce(neg[:, 0:1], pr[:, 0:k, 0:w], AX.XY, ALU.max))
                        k = 1
                    else:
                        link(e.tensor_reduce(neg[:, 0:k], pr[:, 0:k, 0:w], AX.X, ALU.max))
                    e.tensor_scalar(neg[:, 0:k], neg[:, 0:k], -1.0, None, ALU.mult).then_inc(maxes_ready.sem, 1)

                def combine(n, g):
                    w = g["w"]
                    pr = probs[:, n % 2]
                    sums = stat[:, 16 + 8 * (n % 2):24 + 8 * (n % 2)]
                    e.wait_ge(from_act.sem, g["a2"])
                    link(e.reciprocal(sums[:, 0:4], sums[:, 0:4]))
                    link(e.tensor_scalar(sums[:, 2:4], sums[:, 2:4], lam, None, ALU.mult))
                    for i in range(2):
                        link(e.tensor_scalar(pr[:, 2 + i, 0:w], pr[:, 2 + i, 0:w], sums[:, 2 + i:3 + i], None, ALU.mult))
                        last = e.scalar_tensor_tensor(pr[:, i, 0:w], pr[:, i, 0:w], sums[:, i:i + 1], pr[:, 2 + i, 0:w],
                                                      ALU.mult, ALU.subtract)
                        if i == 0:
                            link(last)
                    last.then_inc(probs_ready.sem, 1)

                def take_out(n, g):
                    sums = stat[:, 16 + 8 * (n % 2):24 + 8 * (n % 2)]
                    k = g["n_out"]
                    if g["kind"] in ("softmax", "joint"):
                        e.wait_ge(probs_ready.sem, g["p"])
                        link(e.reciprocal(sums[:, 0:max(k, 1)], sums[:, 0:max(k, 1)]))
                    g["out"].wait_full(e)
                    src = g["out"].ap[:, 0:k * HD].rearrange("p (n d) -> p n d", n=k)
                    if g["kind"] == "softmax":
                        for par in range(2):
                            r = sums[:, 2 * par:2 * par + 2].unsqueeze(2).to_broadcast([P, 2, HD])
                            last = e.tensor_tensor(g["out_ap"][:, par::2, :], src[:, par::2, :], r, ALU.mult)
                            if par == 0:
                                link(last)
                    elif g["kind"] == "joint":
                        last = e.tensor_scalar(g["out_ap"], src, sums[:, 0:1], None, ALU.mult)
                    else:
                        last = e.tensor_copy(g["out_ap"], src)
                    last.then_inc(g["out"].free, 1)

                for n, g in enumerate(plan):
                    if g.get("before"):
                        g["before"](e)
                    soften(n, g)
                    g["points"][0]("dve", e)
                    if n:
                        empty_turns(e, 1, n - 1, plan[n - 1])
                        take_out(n - 1, plan[n - 1])
                    if g["kind"] == "diff":
                        combine(n, g)
                    g["points"][1]("dve", e)
                empty_turns(e, 1, len(plan) - 1, plan[-1])
                take_out(len(plan) - 1, plan[-1])

            stage(pe=pe, act=act, dve=dve, points=[p for g in plan for p in g["points"]], us=5.0)

        raw = sb("raw", [P, 8])
        lam = small[:, 250:251]
        flat = rows[:, :, :].rearrange("p a b -> p (a b)")

        def carve(at, shape):
            n = int(np.prod(shape))
            v = flat[:, at:at + n]
            return v.rearrange("p (a b) -> p a b", a=shape[0]) if len(shape) == 2 else v

        stick_tmp = carve(0, (4, SEQ))
        dist = carve(1024, (TILES, SEQ))
        strict = carve(1536, (TILES, SEQ))
        strict_bias = carve(2048, (TILES, SEQ))
        zero = carve(2560, (SEQ,))
        dil_bias = [causal] + [carve(2816 + 512 * i, (TILES, SEQ)) for i in range(2)]
        window = carve(3840, (TILES, SEQ))
        head_bias = carve(4352, (4, SEQ))
        gates = carve(5376, (TILES, 512))
        upper = carve(6400, (TILES, SEQ))
        forget = carve(6912, (TILES, 4))
        cum_keys = carve(6920, (4, SEQ))

        inv = small[:, 0:32]
        ang = small[:, 32:96].rearrange("p (t f) -> p t f", t=TILES)
        turns_n = small[:, 96:160].rearrange("p (t f) -> p t f", t=TILES)
        pos = raw[:, 0:2]
        pos_i = raw[:, 2:4]
        ang_v, sin_v = to_act.plan(), from_act.plan()

        def angles_dve(e):
            link = chains["dve"]
            e.wait_ge(consts_landed, 32)
            link(e.tensor_copy(pos, pos_i.bitcast(I32)))
            for t in range(TILES):
                link.add(e.tensor_scalar(ang[:, t, :], inv, pos[:, t:t + 1], None, ALU.mult))
            link.wait()
            link(e.tensor_scalar(turns_n, ang, float(1 / TWO_PI), ROUND, ALU.mult, ALU.add))
            link(e.tensor_scalar(turns_n, turns_n, ROUND, None, ALU.subtract))
            for c in (C1, C2, C3):
                link(e.scalar_tensor_tensor(ang, turns_n, -c, ang, ALU.mult, ALU.add))
            link(e.tensor_scalar(ang, ang, 3.1415925, -3.1415925, ALU.min, ALU.max))
            link(e.scalar_tensor_tensor(turns_n, ang, -1.0, ang, ALU.mult, ALU.max))
            e.tensor_scalar(turns_n, turns_n, -1.0, float(np.pi / 2), ALU.mult, ALU.add).then_inc(to_act.sem, 1)

        def angles_act(e):
            e.wait_ge(to_act.sem, ang_v)
            e.activation(sin[:, :, :], ang, ACT.Sin)
            e.activation(cos[:, :, :], turns_n, ACT.Sin).then_inc(from_act.sem, 1)

        def wait_pool_pe(e):
            e.wait_ge(pool_made, 1)

        def wait_pool_dve(e):
            e.wait_ge(pool_made, 1)
            e.wait_ge(x_landed, 16)
            angles_dve(e)

        stage(pe=wait_pool_pe, act=angles_act, dve=wait_pool_dve)

        X = lambda t: x[:, t, :]
        H = lambda t: h[:, t, :]
        M = lambda t: mixed[:, t, 0:D]
        T = turned[:, :].rearrange("p (c s) -> p c s", s=SEQ)

        def add_residual(e, ps, t, c0, n):
            return e.tensor_tensor(x[:, t, c0:c0 + n], x[:, t, c0:c0 + n], ps, ALU.add)

        def copy_to(buf):
            return lambda e, ps, t, c0, n: e.copy(buf[:, t, c0:c0 + n], ps)

        norm(X, H, D, a["attn_norm"][0:1, :])
        turn_wide(H, hT, DC)
        proj = tok[:, 0:TILES * EVEN_COLS].rearrange("p (t n) -> p t n", t=TILES)
        project(hT, a["hyb_w_in"][0], DC, EVEN_COLS, copy_to(proj), "act")
        R_QA, R_KA, R_IQ, R_IK, R_QB, R_KB = 0, 512, 640, 1152, 1280, 1792
        rot = tok[:, TILES * EVEN_COLS:TILES * (EVEN_COLS + 2304)].rearrange("p (t n) -> p t n", t=TILES)
        steps = []
        for t in range(TILES):
            for src, dst, heads in ((QA, R_QA, 8), (KA, R_KA, 1), (KA, R_KA + HD, 1), (IQ, R_IQ, 8), (IK, R_IK, 1),
                                    (IK, R_IK + HD, 1), (QB, R_QB, 16)):
                sv, dv = (b[:, t, o:o + heads * HD].rearrange("p (a b c) -> p a b c", a=heads, b=2)
                          for b, o in ((proj, src), (rot, dst)))
                steps.append(rotate(sv, dv, heads, HD // 2, t))
        dve_stage(steps)
        turn_wide(lambda t: rot[:, t, :], T, 18)

        def head_T(first, i, t, n=1, shared=False):
            c = first // P + (0 if shared else i // 2)
            r = (i % 2) * HD
            return T[r:r + HD, c, t * P:t * P + n * P]

        keep_bias = carve(0, (TILES, SEQ))
        rank = carve(512, (TILES, SEQ))
        relu = carve(1024, (4, SEQ))
        iws = stat[:, 56:64]

        def index(t):
            w = P * (t + 1)
            w_scale = 8 ** -0.5 * 64 ** -0.5
            units = [scores.take() for _ in range(2)]
            used_values = [relu_used.plan() for _ in range(2)]
            rk = rank[:, t, 0:w]

            def pe(e):
                for j, u in enumerate(units):
                    u.wait_free(e)
                    for i in range(4):
                        last = e.matmul(u.ap[:, (i % 2) * 2 + i // 2, 0:w], head_T(R_IQ, 4 * j + i, t),
                                        head_T(R_IK, i, 0, t + 1, True), start=True, stop=True)
                    last.then_inc(u.full, 1)

            def act(e):
                for u, used in zip(units, used_values):
                    u.wait_full(e)
                    if used > 1:
                        e.wait_ge(relu_used.sem, used - 1)
                    e.activation(relu[:, :, 0:w], u.ap[:, :, 0:w], ACT.Relu).then_inc(u.free, 1)

            def dve(e):
                link = chains["dve"]
                link(e.tensor_scalar(iws, proj[:, t, IW:IW + 8], w_scale, None, ALU.mult))
                for j, (u, used) in enumerate(zip(units, used_values)):
                    u.wait_emptied(e)
                    for i in range(4):
                        src = relu[:, (i % 2) * 2 + i // 2, 0:w]
                        s = iws[:, 4 * j + i:4 * j + i + 1]
                        if j == 0 and i == 0:
                            link(e.tensor_scalar(rk, src, s, None, ALU.mult))
                        elif i < 3:
                            link(e.scalar_tensor_tensor(rk, src, s, rk, ALU.mult, ALU.add))
                        else:
                            e.scalar_tensor_tensor(rk, src, s, rk, ALU.mult, ALU.add).then_inc(relu_used.sem, 1)
                            e.wait_ge(relu_used.sem, used)
                link(e.tensor_tensor(rk, rk, causal[:, t, 0:w], ALU.add))
                m8 = stat[:, 48:56]
                for _ in range(DSA_KEEP // 8):
                    link(e.max(m8, rk))
                    link(e.match_replace(rk, m8, rk, TAKEN))
                kb = keep_bias[:, t, 0:w]
                link(e.tensor_scalar(kb, rk, TAKEN / 2, NEG, ALU.is_gt, ALU.mult))
                link(e.tensor_tensor(kb, kb, causal[:, t, 0:w], ALU.add))

            stage(pe=pe, act=act, dve=dve)

        for t in range(TILES):
            index(t)

        groups = []
        for t in range(TILES):
            for j in range(2):
                hs = range(4 * j, 4 * j + 4)
                groups.append(dict(
                    kind="softmax", tile=t, scale=HD ** -0.5, bias=keep_bias[:, t, 0:P * (t + 1)],
                    maps=[(head_T(R_QA, i, t), head_T(R_KA, i, 0, t + 1, True)) for i in hs],
                    values=[lambda c: proj[:, c, VA:VA + HD]] * 4,
                    out_ap=mixed[:, t, 256 * j:256 * j + 256].rearrange("p (n d) -> p n d", d=HD)))
            for j in range(2):
                hs = range(4 * j, 4 * j + 4)
                groups.append(dict(
                    kind="softmax", tile=t, scale=HD ** -0.5, bias=causal[:, t, 0:P * (t + 1)],
                    maps=[(head_T(R_QB, i, t), head_T(R_KB, i, 0, t + 1)) for i in hs],
                    values=[(lambda c, i=i: proj[:, c, VB + i * HD:VB + (i + 1) * HD]) for i in hs],
                    out_ap=mixed[:, t, 512 + 256 * j:768 + 256 * j].rearrange("p (n d) -> p n d", d=HD)))
        attend(groups)
        turn_wide(M, T, DC)
        project(T, a["hyb_w_out"][0], DC, D, add_residual, "dve")

        qT = turned[:, 16 * SEQ:16 * SEQ + 16 * P].rearrange("p (n t) -> p n t", n=16)
        key_scores = turned[:, 16 * SEQ + 16 * P:32 * SEQ].rearrange("p (n k) -> p n k", n=16)
        spare = tok[:, MLA_HEADS * P * TILES:]
        onehot = spare[:, 0:2048]
        best = spare[:, 2048:2304].rearrange("p (n k) -> p n k", n=16)
        best_at = spare[:, 2304:2560].rearrange("p (n k) -> p n k", n=16)
        best_f = spare[:, 2560:2816].rearrange("p (n k) -> p n k", n=16)
        top = spare[:, 2816:2944].rearrange("p (n k) -> p n k", n=EH)
        top_at = spare[:, 2944:3072].rearrange("p (n k) -> p n k", n=EH)
        hi = spare[:, 3072:3200]
        lo = spare[:, 3200:3328]
        pick = [spare[:, 3328:3456], spare[:, 3456:3584]]
        iota16 = sb("iota16", [P, TOP])

        routed = {}

        def route(layer, t):
            wq = rows_of(a["peer_w_q"][layer])
            plan = []
            for b in range(4):
                slots = [(weights(wq[:, k:k + 4, b * 512:(b + 1) * 512], 4, 512), k) for k in (0, 4)]
                plan.append((slots, products.take()))
                for s, _ in slots:
                    given_back[s] = plan[-1][1].full_at()
            keys = weights(a["peer_keys"][layer].rearrange("(o p) n -> p o n", o=1), 1, SLOT)
            key_units = [products.take() for _ in range(4)]
            given_back[keys] = key_units[-1].full_at()
            e_in, e_out = to_act.plan(), from_act.plan()
            routed[layer, t] = experts_ready.plan()
            made = [point(5.0) for _ in range(4)] + [point(3.0)]
            ranked = [point(5.0) for _ in range(12)]

            def pe(e):
                for b, (slots, u) in enumerate(plan):
                    u.wait_free(e)
                    for s, _ in slots:
                        slot_wait(e, s)
                    for j in range(4):
                        for s, k0 in slots:
                            for k in range(4):
                                last = e.matmul(u.ap[:, j * P:(j + 1) * P], slot_ap(s)[:, k, j * P:(j + 1) * P],
                                                hT[:, k0 + k, t * P:(t + 1) * P], start=k0 + k == 0,
                                                stop=k0 + k == DC - 1)
                    last.then_inc(u.full, 1)
                    made[b]("pe", e)
                slot_wait(e, keys)
                for b, u in enumerate(key_units):
                    plan[b][1].wait_emptied(e)
                    u.wait_free(e)
                    for j in range(4 * b, 4 * b + 4):
                        last = e.matmul(u.ap[:, (j % 4) * P:(j % 4 + 1) * P], qT[:, j, :],
                                        slot_ap(keys)[:, 0, j * P:(j + 1) * P], start=True, stop=True)
                    last.then_inc(u.full, 1)
                for p in made[4:] + ranked:
                    p("pe", e)

            def act(e):
                for b, (_, u) in enumerate(plan):
                    u.wait_full(e)
                    e.copy(qT[:, 4 * b:4 * b + 4, :], u.ap.rearrange("p (n t) -> p n t", n=4)).then_inc(u.free, 1)
                    made[b]("act", e)
                for b, u in enumerate(key_units):
                    u.wait_full(e)
                    e.copy(key_scores[:, 4 * b:4 * b + 4, :], u.ap.rearrange("p (n t) -> p n t", n=4)
                           ).then_inc(u.free, 1)
                for p in made[4:] + ranked:
                    p("act", e)
                e.wait_ge(to_act.sem, e_in)
                e.activation(share[:, t, :], share[:, t, :], ACT.Exp).then_inc(from_act.sem, 1)

            def dve(e):
                link = chains["dve"]
                for p in made:
                    p("dve", e)
                halves = [(key_scores[:, j, :], best[:, j, :], best_at[:, j, :].bitcast(U32)) for j in range(16)]

                rest = list(ranked)

                def top16(items, ready):
                    for j, (v, m, at) in enumerate(items):
                        if ready:
                            key_units[j // 4].wait_emptied(e)
                        link.add(e.max(m[:, 0:8], v))
                    link.wait()
                    rest.pop(0)("dve", e)
                    for v, m, at in items:
                        link.add(e.max_index(at[:, 0:8], m[:, 0:8], v))
                    link.wait()
                    rest.pop(0)("dve", e)
                    for v, m, at in items:
                        link.add(e.match_replace(v, m[:, 0:8], v, TAKEN))
                    link.wait()
                    rest.pop(0)("dve", e)
                    for v, m, at in items:
                        link.add(e.max(m[:, 8:16], v))
                    link.wait()
                    rest.pop(0)("dve", e)
                    for v, m, at in items:
                        link.add(e.max_index(at[:, 8:16], m[:, 8:16], v))
                    link.wait()
                    rest.pop(0)("dve", e)

                top16(halves, True)
                link(e.tensor_copy(best_f, best_at.bitcast(U32)))
                cand = key_scores.rearrange("p n k -> p (n k)").rearrange("p (h i j) -> p h i j", h=EH, i=TOP)
                b4 = best.rearrange("p (h s) k -> p h s k", s=2)
                link(e.tensor_tensor(cand, b4[:, :, 0, :].unsqueeze(3).to_broadcast([P, EH, TOP, TOP]),
                                     b4[:, :, 1, :].unsqueeze(2).to_broadcast([P, EH, TOP, TOP]), ALU.add))
                cf = key_scores.rearrange("p n k -> p (n k)").rearrange("p (h m) -> p h m", h=EH)
                top16([(cf[:, j, :], top[:, j, :], top_at[:, j, :].bitcast(U32)) for j in range(EH)], False)
                rest.pop(0)("dve", e)
                at = top_at.rearrange("p n k -> p (n k)").bitcast(I32)
                link.add(e.tensor_scalar(pick[0].bitcast(I32), at, 4, None, ALU.arith_shift_right))
                link(e.tensor_scalar(pick[1].bitcast(I32), at, 15, None, ALU.bitwise_and))
                link.add(e.tensor_copy(hi, pick[0].bitcast(I32)))
                link(e.tensor_copy(lo, pick[1].bitcast(I32)))
                f4 = best_f.rearrange("p (h s) k -> p h s k", s=2)
                oh3 = onehot.rearrange("p (a i) -> p a i", i=TOP)
                oh4 = onehot.rearrange("p (h k i) -> p h k i", h=EH, k=TOP)
                for s, where in enumerate((hi, lo)):
                    link(e.tensor_tensor(oh3, where.unsqueeze(2).to_broadcast([P, P, TOP]),
                                         iota16[:, :].unsqueeze(1).to_broadcast([P, P, TOP]), ALU.is_equal))
                    link(e.tensor_tensor(oh4, oh4, f4[:, :, s, :].unsqueeze(2).to_broadcast([P, EH, TOP, TOP]),
                                         ALU.mult))
                    link(e.tensor_reduce(pick[s], oh3, AX.X, ALU.add))
                for p in rest:
                    p("dve", e)
                if layer:
                    link(e.tensor_scalar(pick[1], pick[1], float(layer * NK * NK), None, ALU.add))
                e.scalar_tensor_tensor(expert[:, t, :], pick[0], float(NK), pick[1], ALU.mult, ALU.add
                                       ).then_inc(experts_ready.sem, 1)
                sh = share[:, t, :].rearrange("p (h k) -> p h k", h=EH)
                e.tensor_tensor(sh, top, top[:, :, 0:1].to_broadcast([P, EH, TOP]), ALU.subtract
                                ).then_inc(to_act.sem, 1)
                e.wait_ge(from_act.sem, e_out)
                link(e.tensor_reduce(small[:, 240:248], sh, AX.X, ALU.add))
                link(e.reciprocal(small[:, 240:248], small[:, 240:248]))
                link(e.tensor_tensor(sh, sh, small[:, 240:248].unsqueeze(2).to_broadcast([P, EH, TOP]), ALU.mult))

            stage(pe=pe, act=act, dve=dve, points=made + ranked)

        gathers = []

        def start_experts(layer, t):
            n0 = len(gathers) * P
            gathers.append((layer, t, routed[layer, t]))
            gelu_v = [gelu_ready.plan() for _ in range(EH)]
            weights_v = [weights_ready.plan() for _ in range(EH)]

            def dve(e, i):
                if i < P:
                    n = n0 + i
                    e.wait_ge(u_landed[n % U_SLOTS], 16 * (n // U_SLOTS + 1))
                    r = rows[:, n % U_SLOTS, :]
                    e.tensor_tensor_reduce(r, r, h[:, t, :], 1.0, 0.0, ALU.mult, ALU.add,
                                           dots[:, i:i + 1]).then_inc(u_used.sem, 1)
                j = i // TOP - 1
                if i % TOP == 1 and 0 <= j < EH:
                    e.wait_ge(gelu_ready.sem, gelu_v[j])
                    e.tensor_tensor(weight[:, j * TOP:(j + 1) * TOP], gelu[:, j % 2, :],
                                    share[:, t, j * TOP:(j + 1) * TOP], ALU.mult).then_inc(weights_ready.sem, 1)

            def act(e, i):
                j = i // TOP - 1
                if i % TOP == 0 and 0 <= j < EH:
                    e.wait_ge(u_used.sem, n0 + (j + 1) * TOP)
                    e.activation(gelu[:, j % 2, :], dots[:, j * TOP:(j + 1) * TOP], ACT.Gelu
                                 ).then_inc(gelu_ready.sem, 1)
                k = i - LAG
                if k >= 0:
                    n = n0 + k
                    if k % TOP == 0:
                        e.wait_ge(weights_ready.sem, weights_v[k // TOP])
                    if n >= DIAGS:
                        e.wait_ge(v_used.sem, n - DIAGS + 1)
                    e.activation(diag[:, n % DIAGS, :], ident[:, :], ACT.Copy,
                                 scale=weight[:, k:k + 1]).then_inc(diag_ready.sem, 1)

            def pe(e, i):
                k = i - LAG
                if k >= 0:
                    n = n0 + k
                    e.wait_ge(v_landed[n % V_SLOTS], 16 * (n // V_SLOTS + 1))
                    e.wait_ge(diag_ready.sem, n + 1)
                    for b in range(2):
                        last = e.matmul(ps_acc[:, b * 512:(b + 1) * 512], diag[:, n % DIAGS, :],
                                        rows[:, U_SLOTS + n % V_SLOTS, b * 512:(b + 1) * 512],
                                        start=k == 0, stop=k == P - 1)
                    last.then_inc(v_used.sem, 1)

            feeds.append({"open": True, "first": 0, "weight": 0.0, "cuts": [], "pe": pe, "act": act, "dve": dve})

        def finish_experts(t, behind=None):
            f = feeds[-1]
            f["open"] = False
            items = range(handed_out(f, f["weight"]), ITEMS)
            total = len(gathers) * P
            if behind:
                start_experts(*behind)
                feeds[-1]["first"] = LAG
            then = feeds[-1] if behind else None

            def part(name):
                def run(e):
                    for i in items:
                        f[name](e, i)
                        if then and i >= P:
                            then[name](e, i - P)
                return run

            def dve(e):
                link = chains["dve"]
                part("dve")(e)
                e.wait_ge(v_used.sem, total)
                for b in range(2):
                    link.add(e.tensor_tensor(x[:, t, b * 512:(b + 1) * 512], x[:, t, b * 512:(b + 1) * 512],
                                             ps_acc[:, b * 512:(b + 1) * 512], ALU.add))
                link.wait()

            stage(pe=part("pe"), act=part("act"), dve=dve)

        def feed_forward(layer, tiles):
            norm(X, H, D, a["ffn_norm"][layer:layer + 1, :], tiles)
            turn_wide(H, hT, DC, tiles)
            for t in tiles:
                route(layer, t)

        feed_forward(0, [0])
        start_experts(0, 0)
        feed_forward(0, [1])
        finish_experts(0, (0, 1))

        n_q, n_kv = MLA_HEADS * MLA_D, MLA_HEADS * P
        kv_tok = tok[:, 0:TILES * n_kv].rearrange("p (t n) -> p t n", t=TILES)
        q_tok = spare[:, 0:n_q]
        k_tok = spare[:, n_q:2 * n_q]
        kh = turned[:, 0:16 * SEQ].rearrange("p (n s) -> p n s", s=SEQ)
        qh = turned[:, 16 * SEQ:16 * SEQ + 16 * P].rearrange("p (n s) -> p n s", s=P)
        mixedT = turned[:, 16 * SEQ + 16 * P:32 * SEQ].rearrange("p (c s) -> p c s", s=SEQ)

        def latent(t):
            tiles = [t]
            norm(X, H, D, a["attn_norm"][1:2, :], tiles)
            turn_wide(H, hT, DC, tiles)
            project(hT, a["mla_w_in"][0], DC, Q_RANK + KV_RANK + ROPE, copy_to(mixed), "act", tiles)
            norm(lambda t: mixed[:, t, 0:Q_RANK], lambda t: h[:, t, 0:Q_RANK], Q_RANK, a["mla_q_norm"], tiles)
            norm(lambda t: mixed[:, t, Q_RANK:D], lambda t: h[:, t, Q_RANK:D], KV_RANK, a["mla_kv_norm"], tiles)
            turn_wide(H, hT, DC, tiles)
            project(hT[:, 0:6, :], a["mla_w_uq"][0], 6, n_q,
                    lambda e, ps, t, c0, n: e.copy(q_tok[:, c0:c0 + n], ps), "act", tiles)
            project(hT[:, 6:8, :], a["mla_w_ukv"][0], 2, n_kv, copy_to(kv_tok), "act", tiles)
            q3 = q_tok.rearrange("p (n d) -> p n d", n=MLA_HEADS)
            k3 = k_tok.rearrange("p (n d) -> p n d", n=MLA_HEADS)
            kv3 = kv_tok[:, t, :].rearrange("p (n d) -> p n d", n=MLA_HEADS)
            qr = q3[:, :, NOPE:MLA_D].rearrange("p n (b c) -> p n b c", b=2)
            kr = mixed[:, t, D:D + ROPE].rearrange("p (n b c) -> p n b c", n=1, b=2)

            def keys(e):
                chains["dve"].add(e.tensor_copy(k3[:, :, 0:NOPE], kv3[:, :, 0:NOPE]))
                chains["dve"].add(e.tensor_copy(k3[:, :, NOPE:MLA_D], mixed[:, t, D:D + ROPE].unsqueeze(1)
                                                .to_broadcast([P, MLA_HEADS, ROPE])))

            dve_stage([rotate(qr, qr, MLA_HEADS, ROPE // 2, t, 2), rotate(kr, kr, 1, ROPE // 2, t, 2), keys])
            blocks = []
            for src, dst in ((q_tok, qh), (k_tok, kh[:, :, t * P:(t + 1) * P])):
                for n0 in range(0, MLA_HEADS, 4):
                    blocks.append(([src[:, n * MLA_D:(n + 1) * MLA_D] for n in range(n0, n0 + 4)],
                                   dst[0:MLA_D, n0:n0 + 4, :]))
            turn(blocks)
            attend([dict(
                kind="softmax", tile=t, scale=MLA_D ** -0.5, bias=causal[:, t, 0:P * (t + 1)],
                maps=[(qh[0:MLA_D, n, :], kh[0:MLA_D, n, 0:P * (t + 1)]) for n in range(n0, n0 + 4)],
                values=[(lambda c, n=n: kv_tok[:, c, n * P + NOPE:(n + 1) * P]) for n in range(n0, n0 + 4)],
                out_ap=mixed[:, t, n0 * HD:(n0 + 4) * HD].rearrange("p (n d) -> p n d", d=HD))
                for n0 in range(0, MLA_HEADS, 4)])
            turn_wide(M, mixedT, DC, tiles)
            project(mixedT, a["mla_w_out"][0], DC, D, add_residual, "dve", tiles)

        latent(0)
        feed_forward(1, [0])
        finish_experts(1, (1, 0))
        latent(1)
        feed_forward(1, [1])
        finish_experts(0, (1, 1))
        finish_experts(1)

        norm(X, M, D, a["final_norm"])
        dve_stage([lambda e, t=t: e.tensor_copy(X(t), M(t)) for t in range(TILES)])

        norm(X, H, D, a["mix_norm_g_2"])
        turn_wide(H, hT, DC)
        mix = tok[:, 0:TILES * MIX].rearrange("p (t n) -> p t n", t=TILES)
        project(hT, a["w_in_2"][0][:, 0:MIX], DC, MIX, copy_to(mix), "act")
        (S_Q, S_K, S_V, D_Q, D_K, D_V, F_Q, F_K, F_V, F_F, E_Q, E_K, E_V) = (
            int(c) for c in np.cumsum([0, 256, 256, 256, 768, 768, 768, 256, 256, 256, 4, 256, 256]))
        T_SQ, T_SK, T_DQ, T_DK, T_FQ, T_FK, T_EQ, T_EK = 0, 2, 4, 10, 16, 18, 20, 24
        blocks = []
        for t in range(TILES):
            for col, first, n in ((S_Q, T_SQ, 4), (D_Q, T_DQ, 4), (D_Q + 512, T_DQ + 4, 4), (D_K + 256, T_DK + 2, 4),
                                  (F_Q, T_FQ, 4)):
                blocks.append(([mix[:, t, col + c * P:col + (c + 1) * P] for c in range(n)],
                               T[:, first:first + n, t * P:(t + 1) * P]))
            for col, first in ((E_Q, T_EQ), (E_K, T_EK)):
                blocks.append(([mix[:, t, col + c * HD:col + (c + 1) * HD] for c in range(4)],
                               T[0:HD, first:first + 4, t * P:(t + 1) * P]))
        turn(blocks)

        fl_in, fl_out = to_act.plan(), from_act.plan()
        l_in, l_out = to_act.plan(), from_act.plan()
        col_unit = products.take()
        key_units = [products.take() for _ in range(2)]
        bf = small[:, 0:4]
        lams = small[:, 8:136].rearrange("p (n d) -> p n d", n=4)
        lf_b = stick_tmp[:, :, :].rearrange("p a b -> p (a b)").rearrange("p (r h q) -> p r h q", r=TILES, h=4)
        cum_q = small[:, 140:148].rearrange("p (t h) -> p t h", t=TILES)
        cum_pe = var_ready.plan()
        causal_in = [causal[:, t, 0:P * (t + 1)] for t in range(TILES)]
        diff_gain = small[:, 150:214]
        last_landed = sem("last_landed")
        masks_made = sem("masks_made")

        def masks_dve(e):
            link = chains["dve"]
            e.wait_ge(masks_made, 1)
            e.wait_ge(last_landed, 48)
            fv = mix[:, :, F_F:F_F + 4]
            f0 = forget[:, :, :]
            f1 = stat[:, 0:8].rearrange("p (t h) -> p t h", t=TILES)
            link(e.tensor_tensor(f0, fv, bf.unsqueeze(1).to_broadcast([P, TILES, 4]), ALU.add))
            link(e.scalar_tensor_tensor(f1, f0, -1.0, f0, ALU.mult, ALU.max))
            e.tensor_scalar(f1, f1, -1.0, None, ALU.mult).then_inc(to_act.sem, 1)
            e.wait_ge(from_act.sem, fl_out)
            link(e.scalar_tensor_tensor(f0, f0, 0.0, f1, ALU.min, ALU.subtract))
            for r in range(TILES):
                last = e.tensor_copy(lf_b[:, r], f0[:, r, :].unsqueeze(2).to_broadcast([P, 4, P]))
            last.then_inc(var_ready.sem, 1)
            for i in range(2):
                last = e.tensor_tensor_reduce(lams[:, 2 * i, :], lams[:, 2 * i, :], lams[:, 2 * i + 1, :], 1.0, 0.0,
                                              ALU.mult, ALU.add, stat[:, 8 + i:9 + i])
            last.then_inc(to_act.sem, 1)
            e.wait_ge(from_act.sem, l_out)
            link(e.tensor_tensor(lam, stat[:, 8:9], stat[:, 9:10], ALU.subtract))
            link(e.tensor_scalar(lam, lam, LAMBDA_INIT, None, ALU.add))
            link(e.tensor_scalar(diff_gain, diff_gain, 1.0 - LAMBDA_INIT, None, ALU.mult))
            link.add(e.memset(zero, 0.0))
            link.add(e.tensor_scalar(strict, dist, 0.0, None, ALU.is_gt))
            link.add(e.tensor_scalar(strict_bias, dist, 0.0, NEG, ALU.is_le, ALU.mult))
            di = window.bitcast(I32)
            for g in (1, 2):
                link(e.tensor_copy(di, dist))
                link(e.tensor_scalar(di, di, DIL[g][1] - 1, None, ALU.bitwise_and))
                link(e.tensor_copy(dil_bias[g], di))
                link(e.tensor_scalar(dil_bias[g], dil_bias[g], 0.0, NEG, ALU.not_equal, ALU.mult))
                link(e.tensor_tensor(dil_bias[g], dil_bias[g], causal[:, :, :], ALU.add))
            link(e.tensor_scalar(window, dist, float(DIL[0][0]), NEG, ALU.is_gt, ALU.mult))
            link(e.tensor_tensor(window, window, causal[:, :, :], ALU.add))
            col_unit.wait_full(e)
            e.tensor_copy(cum_q, col_unit.ap[:, 0:8].rearrange("p (t h) -> p t h", t=TILES)
                          ).then_inc(col_unit.free, 1)
            for j, u in enumerate(key_units):
                u.wait_full(e)
                e.tensor_copy(cum_keys[:, 2 * j:2 * j + 2, :], u.ap.rearrange("p (n s) -> p n s", n=2)
                              ).then_inc(u.free, 1)

        def masks_act(e):
            link = chains["act"]
            f1 = stat[:, 0:8]
            e.wait_ge(to_act.sem, fl_in)
            link(e.activation(f1, f1, ACT.Exp))
            e.activation(f1, f1, ACT.Ln, bias=1.0).then_inc(from_act.sem, 1)
            e.wait_ge(to_act.sem, l_in)
            e.activation(stat[:, 8:10], stat[:, 8:10], ACT.Exp).then_inc(from_act.sem, 1)

        def masks_pe(e):
            e.wait_ge(masks_made, 1)
            e.wait_ge(var_ready.sem, cum_pe)
            col_unit.wait_free(e)
            for t in range(TILES):
                for r in range(t + 1):
                    last = e.matmul(col_unit.ap[:, 4 * t:4 * t + 4], upper[:, r, t * P:(t + 1) * P], forget[:, r, :],
                                    start=r == 0, stop=r == t)
            last.then_inc(col_unit.full, 1)
            for j, u in enumerate(key_units):
                u.wait_free(e)
                for i in range(2):
                    for r in range(TILES):
                        last = e.matmul(u.ap[:, i * SEQ:(i + 1) * SEQ], lf_b[:, r, 2 * j + i, :], upper[:, r, :],
                                        start=r == 0, stop=r == TILES - 1)
                last.then_inc(u.full, 1)

        masks_stage = len(stages)
        stage(pe=masks_pe, act=masks_act, dve=masks_dve)

        def bias_of(t, make):
            def before(e):
                for i in range(4):
                    make(e, i)
                chains["dve"].wait()
            return before

        def masked_slope(t, masks, slopes):
            w = P * (t + 1)

            def before(e):
                link = chains["dve"]
                link.wait()
                for i, (m, s) in enumerate(zip(masks, slopes)):
                    link.add(e.scalar_tensor_tensor(head_bias[:, i, 0:w], dist[:, t, 0:w], -s, m[:, t, 0:w],
                                                    ALU.mult, ALU.add))
                link.wait()
            return before

        def forget_bias(t):
            w = P * (t + 1)

            def before(e):
                link = chains["dve"]
                for i in range(4):
                    link.add(e.scalar_tensor_tensor(head_bias[:, i, 0:w], causal[:, t, 0:w], cum_q[:, t, i:i + 1],
                                                    cum_keys[:, i, 0:w], ALU.add, ALU.subtract))
                link.wait()
            return before

        def two_T(first, i, t, n=1):
            return T[(i % 2) * HD:(i % 2) * HD + HD, first + i // 2, t * P:t * P + n * P]

        groups = []
        for t in range(TILES):
            w = P * (t + 1)
            groups.append(dict(
                kind="stick", tile=t, scale=HD ** -0.5, bias=strict_bias[:, t, 0:w], strict=strict[:, t, 0:w],
                maps=[(two_T(T_SQ, i, t), two_T(T_SK, i, 0, t + 1)) for i in range(4)],
                values=[(lambda c, i=i: mix[:, c, S_V + i * HD:S_V + (i + 1) * HD]) for i in range(4)],
                out_ap=mixed[:, t, 0:256].rearrange("p (n d) -> p n d", d=HD)))
            for i in range(4):
                groups.append(dict(
                    kind="joint", tile=t, scale=HD ** -0.5, bias=[head_bias[:, g, 0:w] for g in range(3)],
                    before=masked_slope(t, [window] + dil_bias[1:], [SLOPES_DIL[g][i] for g in range(3)]),
                    maps=[(two_T(T_DQ, 4 * g + i, t), two_T(T_DK, 4 * g + i, 0, t + 1)) for g in range(3)],
                    values=[(lambda c, n=4 * g + i: mix[:, c, D_V + n * HD:D_V + (n + 1) * HD]) for g in range(3)],
                    out_ap=mixed[:, t, 256 + i * HD:256 + (i + 1) * HD].rearrange("p (n d) -> p n d", n=1)))
            groups.append(dict(
                kind="softmax", tile=t, scale=HD ** -0.5, bias=[head_bias[:, i, 0:w] for i in range(4)],
                before=forget_bias(t),
                maps=[(two_T(T_FQ, i, t), two_T(T_FK, i, 0, t + 1)) for i in range(4)],
                values=[(lambda c, i=i: mix[:, c, F_V + i * HD:F_V + (i + 1) * HD]) for i in range(4)],
                out_ap=mixed[:, t, 512:768].rearrange("p (n d) -> p n d", d=HD)))
            for j in range(2):
                hs = (2 * j, 2 * j + 1)
                order = [(n, c) for n in hs for c in range(2)]
                groups.append(dict(
                    kind="diff", tile=t, scale=32 ** -0.5, bias=[head_bias[:, i // 2, 0:w] for i in range(4)],
                    before=masked_slope(t, [causal, causal], [SLOPES_DIFF[n] for n in hs]),
                    maps=[(T[32 * c:32 * c + 32, T_EQ + n, t * P:(t + 1) * P], T[32 * c:32 * c + 32, T_EK + n, 0:w])
                          for n, c in order],
                    values=[(lambda c, n=n: mix[:, c, E_V + n * HD:E_V + (n + 1) * HD]) for n in hs],
                    out_ap=mixed[:, t, 768 + 128 * j:896 + 128 * j].rearrange("p (n d) -> p n d", d=HD)))
        attend(groups)

        heads = mixed[:, :, 768:1024].rearrange("p t (n d) -> p t n d", d=HD)
        v_value, r_value = var_ready.plan(), root_ready.plan()

        def diff_norm_dve(e):
            link = chains["dve"]
            sq = probs[:, 0, :, :].rearrange("p a b -> p (a b)")[:, 0:512].rearrange("p (t n d) -> p t n d", t=TILES, n=4)
            var, root, y, t1 = (stat[:, 8 * i:8 * i + 8] for i in range(4))
            for t in range(TILES):
                link.add(e.tensor_tensor(sq[:, t], heads[:, t], heads[:, t], ALU.mult))
            link.wait()
            link(e.tensor_reduce(var, sq.rearrange("p t n d -> p (t n) d"), AX.X, ALU.add))
            e.tensor_scalar(var, var, 1.0 / HD, EPS, ALU.mult, ALU.add).then_inc(var_ready.sem, 1)
            e.wait_ge(root_ready.sem, r_value)
            link(e.reciprocal(y, root))
            link(e.tensor_tensor(t1, y, y, ALU.mult))
            link(e.tensor_tensor(t1, t1, var, ALU.mult))
            link(e.tensor_scalar(t1, t1, -0.5, 1.5, ALU.mult, ALU.add))
            link(e.tensor_tensor(y, y, t1, ALU.mult))
            for t in range(TILES):
                link(e.tensor_tensor(heads[:, t], heads[:, t],
                                     y[:, 4 * t:4 * t + 4].unsqueeze(2).to_broadcast([P, 4, HD]), ALU.mult))
                link(e.tensor_tensor(heads[:, t], heads[:, t],
                                     diff_gain.unsqueeze(1).to_broadcast([P, 4, HD]), ALU.mult))

        def diff_norm_act(e):
            e.wait_ge(var_ready.sem, v_value)
            e.activation(stat[:, 8:16], stat[:, 0:8], ACT.Sqrt).then_inc(root_ready.sem, 1)

        stage(act=diff_norm_act, dve=diff_norm_dve)
        turn_wide(M, T, DC)

        w_in = rows_of(a["w_in_2"][0])
        w_branch = a["w_branch_2"][0]
        plan = []
        for n in range(4):
            branch = None
            for half in range(2):
                c0 = MIX + n * D + half * 512
                slots = [(weights(w_in[:, k:k + 4, c0:c0 + 512], 4, 512), k) for k in (0, 4)]
                if half == 0:
                    branch = weights(rows_of(w_branch[n]), 2, D)
                for t in range(TILES):
                    plan.append((n, half, t, slots, branch, products.take(), products.take(),
                                 relu_used.plan() if n else None))
                for s, _ in slots:
                    given_back[s] = plan[-1][5].full_at()
                given_back[branch] = plan[-1][6].full_at()
        gated = mixed

        def gate_pe(e):
            for n, half, t, slots, branch, ug, ub, _ in plan:
                for s, _ in slots:
                    slot_wait(e, s)
                ug.wait_free(e)
                for s, k0 in slots:
                    for k in range(4):
                        last = e.matmul(ug.ap, hT[:, k0 + k, t * P:(t + 1) * P], slot_ap(s)[:, k, :],
                                        start=k0 + k == 0, stop=k0 + k == DC - 1)
                last.then_inc(ug.full, 1)
                slot_wait(e, branch)
                ub.wait_free(e)
                for k in range(2):
                    last = e.matmul(ub.ap, T[:, 2 * n + k, t * P:(t + 1) * P],
                                    slot_ap(branch)[:, k, half * 512:half * 512 + 512], start=k == 0, stop=k == 1)
                last.then_inc(ub.full, 1)

        def gate_act(e):
            for i, (_, _, _, _, _, ug, _, _) in enumerate(plan):
                if i >= 2:
                    before, used = plan[i - 2][6], plan[i - 2][7]
                    if used is None:
                        before.wait_emptied(e)
                    else:
                        e.wait_ge(relu_used.sem, used)
                ug.wait_full(e)
                e.activation(gates[:, i % 2, :], ug.ap, ACT.Sigmoid).then_inc(ug.free, 1)

        def gate_dve(e):
            link = chains["dve"]
            for i, (n, half, t, _, _, ug, ub, _) in enumerate(plan):
                ug.wait_emptied(e)
                ub.wait_full(e)
                g = gates[:, i % 2, :]
                y = gated[:, t, half * 512:half * 512 + 512]
                if n == 0:
                    e.tensor_tensor(y, g, ub.ap, ALU.mult).then_inc(ub.free, 1)
                else:
                    e.tensor_tensor(g, g, ub.ap, ALU.mult).then_inc(ub.free, 1)
                    e.wait_ge(ub.free, ub.use + 1)
                    e.tensor_tensor(y, y, g, ALU.add).then_inc(relu_used.sem, 1)

        stage(pe=gate_pe, act=gate_act, dve=gate_dve)
        turn_wide(M, hT, DC)
        project(hT, a["w_out_2"][0], DC, D, add_residual, "dve")

        norm(X, H, D, a["mlp_norm_g_2"])
        turn_wide(H, hT, DC)
        w_up = rows_of(a["w_up_2"][0])
        up_plan = []
        for b in range(8):
            slots = [(weights(w_up[:, k:k + 4, b * 512:(b + 1) * 512], 4, 512), k) for k in (0, 4)]
            up_plan.append((b, slots, [products.take() for _ in range(2)]))
            for s, _ in slots:
                given_back[s] = up_plan[-1][2][-1].full_at()

        def up_pe(e):
            for b, slots, units in up_plan:
                for s, _ in slots:
                    slot_wait(e, s)
                for j, u in enumerate(units):
                    u.wait_free(e)
                    for i in range(2):
                        f = (2 * j + i) * P
                        for s, k0 in slots:
                            for k in range(4):
                                last = e.matmul(u.ap[:, i * SEQ:(i + 1) * SEQ], slot_ap(s)[:, k, f:f + P],
                                                hT[:, k0 + k, :], start=k0 + k == 0, stop=k0 + k == DC - 1)
                    last.then_inc(u.full, 1)

        def up_act(e):
            for b, _, units in up_plan:
                for j, u in enumerate(units):
                    u.wait_full(e)
                    e.activation(T[:, 4 * b + 2 * j:4 * b + 2 * j + 2, :], u.ap.rearrange("p (n s) -> p n s", n=2),
                                 ACT.Relu).then_inc(u.free, 1)

        def up_dve(e):
            for b, _, units in up_plan:
                for j, u in enumerate(units):
                    u.wait_emptied(e)
                    v = T[:, 4 * b + 2 * j:4 * b + 2 * j + 2, :]
                    e.tensor_tensor(v, v, v, ALU.mult)

        stage(pe=up_pe, act=up_act, dve=up_dve)
        project(T, a["w_down_2"][0], 32, D, add_residual, "dve")
        norm(X, H, D, a["final_norm_g_2"])

        block = ctx.enter_context(nc.Block())

        @block.sync
        def _(sp):
            sp.dma_start(raw[:, 2:4].bitcast(I32), a["positions"]).then_inc(consts_landed, 16)
            sp.dma_start(small[:, 0:32], a["inv_freq"].to_broadcast([P, 32])).then_inc(consts_landed, 16)
            load_gain(sp, 0)
            sp.dma_start(x[:, :, :], a["x"].rearrange("(t p) d -> p t d", p=P)).then_inc(x_landed, 16)
            for n, (view, chunks, cols) in enumerate(stream):
                if n >= SLOTS:
                    sp.wait_ge(*given_back[n - SLOTS])
                sp.dma_start(slot_ap(n), view).then_inc(w_landed[n % SLOTS], 16)
            for t in range(TILES):
                sp.wait_ge(done["dve"], len(stages))
                sp.dma_start(out.rearrange("(t p) d -> p t d", p=P)[:, t, :], h[:, t, :]).then_inc(out_landed, 16)
            sp.wait_ge(out_landed, 16 * TILES)

        @block.gpsimd
        def _(pool):
            step = Chain(pool, pool_step)
            step.add(pool.memset(ident[:, :], 0.0))
            step(pool.memset(causal[:, :, :], 0.0))
            step.add(pool.affine_select(ident[:, :], ident[:, :], pattern=[[-1, P]], compare_op=ALU.not_equal,
                                        fill=1.0, base=0, channel_multiplier=1))
            step.add(pool.affine_select(causal[:, :, :], causal[:, :, :], pattern=[[P, TILES], [-1, SEQ]],
                                        compare_op=ALU.is_ge, fill=NEG, base=0, channel_multiplier=1))
            step(pool.iota(iota16[:, :], pattern=[[1, TOP]], base=0, channel_multiplier=0,
                           allow_small_or_imprecise_dtypes=True))
            pool.drain().then_inc(pool_made, 1)
            for n in range(len(gathers) * P + TOP):
                if n < len(gathers) * P:
                    _, t, ready = gathers[n // P]
                    if n % P == 0:
                        pool.wait_ge(experts_ready.sem, ready)
                    if n >= U_SLOTS:
                        pool.wait_ge(u_used.sem, n - U_SLOTS + 1)
                    pool.indirect_dma_start(
                        rows[:, n % U_SLOTS, :], None, a["peer_u"],
                        bass.IndirectOffsetOnAxis(ap=expert[:, t, n % P:n % P + 1], axis=0)
                    ).then_inc(u_landed[n % U_SLOTS], 16)
                m = n - TOP
                if m >= 0:
                    t = gathers[m // P][1]
                    if m >= V_SLOTS:
                        pool.wait_ge(v_used.sem, m - V_SLOTS + 1)
                    pool.indirect_dma_start(
                        rows[:, U_SLOTS + m % V_SLOTS, :], None, a["peer_v"],
                        bass.IndirectOffsetOnAxis(ap=expert[:, t, m % P:m % P + 1], axis=0)
                    ).then_inc(v_landed[m % V_SLOTS], 16)
            for e in ("dve", "act", "pe"):
                pool.wait_ge(done[e], masks_stage)
            step.add(pool.iota(dist, pattern=[[P, TILES], [-1, SEQ]], base=0, channel_multiplier=1,
                               allow_small_or_imprecise_dtypes=True))
            step(pool.memset(upper, 1.0))
            step(pool.affine_select(upper, upper, pattern=[[-P, TILES], [1, SEQ]], compare_op=ALU.is_ge, fill=0.0,
                                    base=0, channel_multiplier=-1))
            pool.dma_start(small[:, 0:4], a["b_forget_2"].to_broadcast([P, 4])).then_inc(last_landed, 16)
            pool.dma_start(small[:, 8:136], a["lambdas"].to_broadcast([P, 128])).then_inc(last_landed, 16)
            pool.dma_start(diff_gain, a["diff_norm_g_2"].to_broadcast([P, HD])).then_inc(last_landed, 16)
            pool.drain().then_inc(masks_made, 1)

        @block.scalar
        def _(act):
            chains["act"] = Chain(act, act_step)
            run_stages("act", act)

        @block.vector
        def _(dve):
            chains["dve"] = Chain(dve, dve_step)
            run_stages("dve", dve)

        @block.tensor
        def _(pe):
            run_stages("pe", pe)


INPUTS = ["x", "positions", "attn_norm", "ffn_norm", "final_norm", "hyb_w_in", "hyb_w_out", "mla_w_in", "mla_q_norm",
          "mla_kv_norm", "mla_w_uq", "mla_w_ukv", "mla_w_out", "peer_w_q", "peer_keys", "peer_u", "peer_v",
          "mix_norm_g_2", "w_in_2", "b_forget_2", "lambdas", "diff_norm_g_2", "w_branch_2", "w_out_2",
          "mlp_norm_g_2", "w_up_2", "w_down_2", "final_norm_g_2", "inv_freq"]


def kernel(**inputs):
    import concourse.bacc as bacc
    from concourse.bass_utils import run_bass_kernel_spmd

    got = {k: np.asarray(v) for k, v in inputs.items()}
    lambdas = [got.pop(f"lambda_{n}_2") for n in ("q1", "k1", "q2", "k2")]
    keys = got.pop("peer_sub_keys")
    layers = keys.shape[0]
    laid = got | {
        "x": got["x"].reshape(SEQ, D),
        "positions": got["positions"].reshape(TILES, P).T,
        "final_norm": got["final_norm"].reshape(1, D),
        "final_norm_g_2": got["final_norm_g_2"].reshape(1, D),
        "peer_u": got["peer_u"].reshape(-1, D),
        "peer_v": got["peer_v"].reshape(-1, D),
        "peer_keys": keys.transpose(0, 4, 1, 2, 3).reshape(layers, P, EH * 2 * NK),
        "lambdas": np.concatenate(lambdas, axis=1),
        "inv_freq": (1.0 / 10000.0 ** (np.arange(0, HD, 2, dtype=np.float32) / HD)).astype(np.float32).reshape(1, 32),
    }
    nc = bacc.Bacc("TRN2", target_bir_lowering=False, num_devices=1)
    arrays, a = {}, {}
    for name in INPUTS:
        v = np.ascontiguousarray(laid[name])
        arrays[f"in_{name}"] = v
        a[name] = nc.dram_tensor(f"in_{name}", v.shape, mybir.dt.from_np(v.dtype), kind="ExternalInput").ap()
    out = nc.dram_tensor("out_0", (SEQ, D), F32, kind="ExternalOutput").ap()
    build(nc, a, out)
    r = run_bass_kernel_spmd(nc, [arrays], core_ids=[0])
    return r.results[0]["out_0"].reshape(1, SEQ, D)
```

```python
from contextlib import ExitStack

import numpy as np

import concourse.bass as bass
from concourse import mybir

ALU = mybir.AluOpType
ACT = mybir.ActivationFunctionType
F32R = mybir.dt.float32r
F32 = mybir.dt.float32
I32 = mybir.dt.int32
U32 = mybir.dt.uint32
AX = mybir.AxisListType

P = 128
SEQ = 256
TILES = SEQ // P
D = 1024
DC = D // P
EPS = 1e-6
NEG = -1.0e30
TAKEN = -3.0e38
SLOT = 2048
SLOTS = 5
U_SLOTS = 4
V_SLOTS = 4
DIAGS = 4

HD = 64
QA, KA, VA, IQ, IK, IW, QB, KB, VB = (int(c) for c in np.cumsum([0, 512, 64, 64, 512, 64, 8, 512, 512]))
EVEN_COLS = VB + 512
DSA_KEEP = 64
KV_RANK, Q_RANK, ROPE = 256, 768, 32
MLA_HEADS, NOPE = 16, 64
MLA_D = NOPE + ROPE
EH, NK, TOP = 8, 128, 16
LAG = TOP + 2
ITEMS = EH * TOP + LAG
RATE = 0.6
MIX = 4612
SLOPES = [float(np.float32(2.0 ** (-8.0 * n / 16))) for n in range(1, 17)]
DIL = ((128, 1), (512, 4), (2048, 16))
SLOPES_DIL = [SLOPES[0:4], SLOPES[8:12], SLOPES[12:16]]
SLOPES_DIFF = SLOPES[4:8]
LAMBDA_INIT = 0.2
TWO_PI = 2 * np.pi
C1 = 6.28125
C2 = float(np.float32(np.round((TWO_PI - C1) * 2 ** 21) / 2 ** 21))
C3 = float(TWO_PI - C1 - C2)
ROUND = 12582912.0


class Banks:

    def __init__(self, views, full, free):
        self.views, self.full, self.free, self.n = views, full, free, 0

    def take(self):
        b, use = self.n % len(self.views), self.n // len(self.views)
        self.n += 1
        return Unit(self, b, use)


class Unit:

    def __init__(self, banks, b, use):
        self.ap, self.b, self.use = banks.views[b], b, use
        self.full, self.free = banks.full[b], banks.free[b]

    def wait_free(self, pe):
        if self.use:
            pe.wait_ge(self.free, self.use)

    def wait_full(self, eng):
        eng.wait_ge(self.full, self.use + 1)

    def wait_emptied(self, eng):
        eng.wait_ge(self.free, self.use + 1)

    def full_at(self):
        return self.full, self.use + 1


class Signal:

    def __init__(self, sem):
        self.sem, self.n = sem, 0

    def plan(self, k=1):
        self.n += k
        return self.n


class Chain:

    def __init__(self, eng, sem):
        self.eng, self.sem, self.n = eng, sem, 0

    def __call__(self, ins):
        self.n += 1
        ins.then_inc(self.sem, 1)
        self.eng.wait_ge(self.sem, self.n)

    def add(self, ins):
        self.n += 1
        ins.then_inc(self.sem, 1)

    def wait(self):
        self.eng.wait_ge(self.sem, self.n)


def build(nc, a, out):
    with ExitStack() as ctx:
        def sb(name, shape, dt=F32):
            return ctx.enter_context(nc.sbuf_tensor("sb_" + name, shape, dt))

        def sem(name):
            return ctx.enter_context(nc.semaphore(name))

        psum = [ctx.enter_context(nc.psum_tensor(f"bank{i}", [P, 512], F32)) for i in range(2)]
        ps_scores = ctx.enter_context(nc.psum_tensor("ps_scores", [P, 4, SEQ], F32))
        ps_turn = [ctx.enter_context(nc.psum_tensor(f"ps_turn{i}", [P, 512], F32)) for i in range(2)]
        ps_acc = ctx.enter_context(nc.psum_tensor("ps_acc", [P, D], F32))

        x = sb("x", [P, TILES, D])
        h = sb("h", [P, TILES, D])
        mixed = sb("mixed", [P, TILES, 1056])
        probs = sb("probs", [P, 2, 4, SEQ])
        probsT = sb("probsT", [P, 2, 2, 4, P])
        wring = sb("wring", [P, SLOTS, SLOT])
        with ExitStack() as first_use:
            hT, rows, tok, turned = (first_use.enter_context(nc.sbuf_tensor("sb_" + name, [P, n], F32))
                                     for name, n in (("hT", DC * SEQ), ("rows", (U_SLOTS + V_SLOTS) * D),
                                                     ("tok", 10496), ("turned", 32 * SEQ)))
        hT_r, rows_r, tok_r, turned_r = (sb(name, [P, n], F32R) for name, n in (
            ("hT_r", DC * SEQ), ("rows_r", (U_SLOTS + V_SLOTS) * D), ("tok_r", 10496), ("turned_r", 32 * SEQ)))
        hT = hT[:, :].rearrange("p (c s) -> p c s", c=DC)
        rows = rows[:, :].rearrange("p (n d) -> p n d", d=D)
        gain = sb("gain", [P, D])
        ident = sb("ident", [P, P])
        causal = sb("causal", [P, TILES, SEQ])
        cos = sb("cos", [P, TILES, 32])
        sin = sb("sin", [P, TILES, 32])
        small = sb("small", [P, 256])
        stat = sb("stat", [P, 64])
        expert = sb("expert", [P, TILES, P], I32)
        share = sb("share", [P, TILES, P])
        dots = sb("dots", [P, P])
        gelu = sb("gelu", [P, 2, TOP])
        weight = sb("weight", [P, P])
        diag = sb("diag", [P, DIAGS, P])

        w_landed = [sem(f"w_landed{i}") for i in range(SLOTS)]
        w_used = Signal(sem("w_used"))
        gain_landed = Signal(sem("gain_landed"))
        gain_used = Signal(sem("gain_used"))
        x_landed = sem("x_landed")
        consts_landed = sem("consts_landed")
        pool_made = sem("pool_made")
        pool_step = sem("pool_step")
        dve_step = sem("dve_step")
        act_step = sem("act_step")
        done = {e: sem(f"stage_done_{e}") for e in ("pe", "act", "dve")}
        var_ready = Signal(sem("var_ready"))
        root_ready = Signal(sem("root_ready"))
        maxes_ready = Signal(sem("maxes_ready"))
        probs_ready = Signal(sem("probs_ready"))
        relu_used = Signal(sem("relu_used"))
        to_act = Signal(sem("to_act"))
        from_act = Signal(sem("from_act"))
        experts_ready = Signal(sem("experts_ready"))
        u_landed = [sem(f"u_landed{i}") for i in range(U_SLOTS)]
        v_landed = [sem(f"v_landed{i}") for i in range(V_SLOTS)]
        u_used = Signal(sem("u_used"))
        v_used = Signal(sem("v_used"))
        gelu_ready = Signal(sem("gelu_ready"))
        weights_ready = Signal(sem("weights_ready"))
        diag_ready = Signal(sem("diag_ready"))
        hi_made = Signal(sem("hi_made"))
        lo_made = Signal(sem("lo_made"))
        turned_hi = Signal(sem("turned_hi"))
        squared = Signal(sem("squared"))
        out_landed = sem("out_landed")

        pair = [sem(f"product_full{i}") for i in range(2)], [sem(f"product_free{i}") for i in range(2)]
        products = Banks([b[:, :] for b in psum], *pair)
        pair = [sem(f"turn_full{i}") for i in range(2)], [sem(f"turn_free{i}") for i in range(2)]
        turns = Banks([b[:, :] for b in ps_turn], *pair)
        pair = [sem(f"spare_full{i}") for i in range(2)], [sem(f"spare_free{i}") for i in range(2)]
        spare_banks = Banks([ps_acc[:, 0:512], ps_acc[:, 512:1024]], *pair)
        scores = Banks([ps_scores[:, :, :]], [sem("scores_full")], [sem("scores_free")])

        pair = [sem(f"two_scores_full{i}") for i in range(2)], [sem(f"two_scores_free{i}") for i in range(2)]
        two_scores = Banks([ps_scores[:, :, :], ps_acc[:, :].rearrange("p (n s) -> p n s", n=4)], *pair)

        stages = []
        stream = []
        given_back = {}
        ends = {"pe": 0, "act": 0, "dve": 0}
        chains = {}

        feeds = []

        def handed_out(f, weight):
            return f["first"] + int(weight * min((P - f["first"]) / max(f["weight"], 1.0), RATE))

        def point(us):
            f = feeds[-1] if feeds and feeds[-1]["open"] else None
            if f is None:
                return lambda name, e: None
            f["weight"] += us
            behind = f["weight"]
            f["cuts"].append(behind)

            def run(name, e):
                at = f["cuts"].index(behind)
                for i in range(handed_out(f, f["cuts"][at - 1] if at else 0), handed_out(f, behind)):
                    f[name](e, i)
            return run

        def stage(pe=None, act=None, dve=None, points=(), us=1.0):
            stages.append({"pe": pe, "act": act, "dve": dve, "points": points, "after": point(us)})

        def run_stages(name, eng):
            others = [n for n in ("pe", "act", "dve") if n != name]
            for k, s in enumerate(stages):
                if s[name] is not None:
                    s[name](eng)
                else:
                    for p in s["points"]:
                        p(name, eng)
                s["after"](name, eng)
                eng.drain().then_inc(done[name], 1)
                for n in others:
                    eng.wait_ge(done[n], k + 1)

        def weights(view, chunks, cols):
            stream.append((view, chunks, cols))
            return len(stream) - 1

        def slot_ap(n):
            _, chunks, cols = stream[n]
            return wring[:, n % SLOTS, 0:chunks * cols].rearrange("p (c n) -> p c n", c=chunks)

        def slot_wait(pe, n):
            pe.wait_ge(w_landed[n % SLOTS], 16 * (n // SLOTS + 1))

        def rows_of(w):
            return w.rearrange("(c p) n -> p c n", p=P)

        gains = []
        squares = [probs[:, i].rearrange("p a b -> p (a b)") for i in range(2)]

        def norm(src, dst, width, g, tiles=range(TILES)):
            gains.append((g, width))
            number = len(gains)
            g_value = gain_landed.plan(16)
            n = len(tiles)
            v_value, r_value = var_ready.plan(), root_ready.plan()
            gain_used.plan()
            var, root, y, t1 = (stat[:, 4 * i:4 * i + n] for i in range(4))
            p = point(4.0)

            def dve(e):
                link = chains["dve"]
                for i, t in enumerate(tiles):
                    link.add(e.tensor_tensor_reduce(squares[t][:, 0:width], src(t), src(t), 1.0 / width, 0.0, ALU.mult, ALU.add,
                                                    stat[:, i:i + 1]))
                link.wait()
                e.tensor_scalar(var, var, EPS, None, ALU.add).then_inc(var_ready.sem, 1)
                p("dve", e)
                e.wait_ge(root_ready.sem, r_value)
                link(e.reciprocal(y, root))
                link(e.tensor_tensor(t1, y, y, ALU.mult))
                link(e.tensor_tensor(t1, t1, var, ALU.mult))
                link(e.tensor_scalar(t1, t1, -0.5, 1.5, ALU.mult, ALU.add))
                link(e.tensor_tensor(y, y, t1, ALU.mult))
                e.wait_ge(gain_landed.sem, g_value)
                for i, t in enumerate(tiles):
                    last = e.scalar_tensor_tensor(dst(t), src(t), stat[:, 8 + i:9 + i], gain[:, 0:width],
                                                  ALU.mult, ALU.mult)
                last.then_inc(gain_used.sem, 1)

            def act(e):
                e.wait_ge(var_ready.sem, v_value)
                e.activation(root, var, ACT.Sqrt).then_inc(root_ready.sem, 1)
                p("act", e)
                if number < len(gains):
                    e.wait_ge(gain_used.sem, number)
                    load_gain(e, number)

            stage(act=act, dve=dve, points=[p], us=5.0)

        def load_gain(e, n):
            g, width = gains[n]
            e.dma_start(gain[:, 0:width], g.to_broadcast([P, width])).then_inc(gain_landed.sem, 16)

        def turn(blocks):
            plan = [(srcs, dst, turns.take()) for srcs, dst in blocks]
            points = [point(0.8) for _ in plan]

            def pe(e):
                for (srcs, dst, u), p in zip(plan, points):
                    w = dst.shape[0]
                    u.wait_free(e)
                    for i, s in enumerate(srcs):
                        last = e.transpose(u.ap[0:w, i * P:(i + 1) * P], s, ident[:, :])
                    last.then_inc(u.full, 1)
                    p("pe", e)

            def empty(e, b):
                for (srcs, dst, u), p in zip(plan, points):
                    if u.b == b:
                        u.wait_full(e)
                        w, n = dst.shape[0], len(srcs)
                        src = u.ap[0:w, 0:n * P].rearrange("p (n t) -> p n t", n=n)
                        copy = e.copy if b == 0 else e.tensor_copy
                        copy(dst, src).then_inc(u.free, 1)
                    p(("act", "dve")[b], e)

            stage(pe=pe, act=lambda e: empty(e, 0), dve=lambda e: empty(e, 1), points=points)

        def turn_wide(src, dst, chunks, tiles=range(TILES)):
            blocks = []
            for t in tiles:
                for c0 in range(0, chunks, 4):
                    n = min(4, chunks - c0)
                    blocks.append(([src(t)[:, c * P:(c + 1) * P] for c in range(c0, c0 + n)],
                                   dst[:, c0:c0 + n, t * P:(t + 1) * P]))
            turn(blocks)

        def project(xT, w, chunks, cols, empty, engine, tiles=range(TILES)):
            per = min(chunks, 4) if chunks != 6 else 3
            wide = SLOT // per // 512 * 512 if per < 4 else 512
            plan = []
            wv = rows_of(w)
            for n0 in range(0, cols, wide):
                wn = min(wide, cols - n0)
                slots = [(weights(wv[:, k:k + per, n0:n0 + wn], per, wn), k) for k in range(0, chunks, per)]
                blocks = range(0, wn, 512)
                for b0 in blocks:
                    bn = min(512, wn - b0)
                    units = [products.take() for _ in tiles]
                    plan.append((slots, b0, bn, n0 + b0, units, b0 == blocks[-1]))
                for s, k0 in slots:
                    last_use = units[-1].full_at() if k0 + per == chunks else (w_used.sem, w_used.plan())
                    given_back[s] = last_use
            points = [point(len(tiles) * chunks * 0.35) for _ in plan]

            def pe(e):
                for (slots, b0, bn, _, units, ends_slot), p in zip(plan, points):
                    for u in units:
                        u.wait_free(e)
                    for s, k0 in slots:
                        slot_wait(e, s)
                        sl = slot_ap(s)
                        for t, u in zip(tiles, units):
                            for k in range(per):
                                last = e.matmul(u.ap[:, 0:bn], xT[:, k0 + k, t * P:(t + 1) * P],
                                                sl[:, k, b0:b0 + bn], start=k0 + k == 0, stop=k0 + k == chunks - 1)
                            if k0 + per == chunks:
                                last.then_inc(u.full, 1)
                        if ends_slot and k0 + per < chunks:
                            last.then_inc(w_used.sem, 1)
                    p("pe", e)

            def other(e):
                for (_, _, bn, c0, units, _), p in zip(plan, points):
                    for t, u in zip(tiles, units):
                        u.wait_full(e)
                        empty(e, u.ap[:, 0:bn], t, c0, bn).then_inc(u.free, 1)
                    p(engine, e)

            stage(pe=pe, points=points, **{engine: other})

        places = [rows_r[:, 0:2 * SLOT], rows_r[:, 2 * SLOT:4 * SLOT],
                  tok_r[:, 0:2 * SLOT], tok_r[:, 2 * SLOT:4 * SLOT]]
        splits = []
        split_back = {}
        place_user = {}

        def plan_split(s, chunks, c0, c1, place):
            m = len(splits)
            splits.append((s, chunks, c0, c1, place, place_user.get(place)))
            place_user[place] = m
            hi_made.plan()
            given_back[s] = (lo_made.sem, lo_made.plan())
            return m

        def halves_of(m):
            _, chunks, c0, c1, place, _ = splits[m]
            n = chunks * (c1 - c0)
            return [places[place][:, i * SLOT:i * SLOT + n].rearrange("p (c n) -> p c n", c=chunks)
                    for i in range(2)]

        def split_act(e, m):
            s, _, c0, c1, _, before = splits[m]
            slot_wait(e, s)
            if before is not None:
                e.wait_ge(*split_back[before])
            e.copy(halves_of(m)[0], slot_ap(s)[:, :, c0:c1]).then_inc(hi_made.sem, 1)

        def split_dve(e, m):
            s, _, c0, c1, _, _ = splits[m]
            e.wait_ge(hi_made.sem, m + 1)
            high, low = halves_of(m)
            e.tensor_tensor(low, slot_ap(s)[:, :, c0:c1], high, ALU.subtract).then_inc(lo_made.sem, 1)

        def split_wait(pe, m):
            pe.wait_ge(lo_made.sem, m + 1)

        def product(pe, ps, left, right, start, stop):
            pe.matmul(ps, left[0], right[0], start=start, stop=False)
            pe.matmul(ps, left[0], right[1], start=False, stop=False)
            return pe.matmul(ps, left[1], right[0], start=False, stop=stop)

        def quads(v):
            return [v[:, c:c + 4 * SEQ].rearrange("p (c s) -> p c s", c=4) for c in range(0, v.shape[1], 4 * SEQ)]

        def chunk_of(pair, k, t=None):
            cols = slice(0, SEQ) if t is None else slice(t * P, (t + 1) * P)
            return [q[k // 4][:, k % 4, cols] for q in pair]

        def turn_split(src, pair):
            plan = [(t, q, turns.take(), turned_hi.plan()) for t in range(TILES) for q in range(2)]

            def pe(e):
                for t, q, u, _ in plan:
                    u.wait_free(e)
                    for i in range(4):
                        last = e.transpose(u.ap[:, i * P:(i + 1) * P], src(t)[:, (4 * q + i) * P:(4 * q + i + 1) * P],
                                           ident[:, :])
                    last.then_inc(u.full, 1)

            def act(e):
                for t, q, u, _ in plan:
                    u.wait_full(e)
                    e.copy(pair[0][q][:, :, t * P:(t + 1) * P], u.ap.rearrange("p (n t) -> p n t", n=4)
                           ).then_inc(turned_hi.sem, 1)

            def dve(e):
                for t, q, u, made in plan:
                    e.wait_ge(turned_hi.sem, made)
                    e.tensor_tensor(pair[1][q][:, :, t * P:(t + 1) * P], u.ap.rearrange("p (n t) -> p n t", n=4),
                                    pair[0][q][:, :, t * P:(t + 1) * P], ALU.subtract).then_inc(u.free, 1)

            stage(pe=pe, act=act, dve=dve)

        def project_split(pair, w, chunks, cols, empty, engine, ring):
            wv = rows_of(w)
            plan, order, waiting, n_splits = [], [], None, 0
            for b, c0 in enumerate(range(0, cols, 512)):
                n = min(512, cols - c0)
                ms = []
                for k0 in range(0, chunks, 4):
                    s = weights(wv[:, k0:k0 + 4, c0:c0 + n], 4, n)
                    ms.append(plan_split(s, 4, 0, n, ring[n_splits % len(ring)]))
                    n_splits += 1
                    order.append(("split", ms[-1]))
                    if waiting is not None:
                        order.append(("empty", waiting))
                        waiting = None
                units = [(products, spare_banks)[b % 2].take() for _ in range(TILES)]
                for m in ms[:-1]:
                    split_back[m] = w_used.sem, w_used.plan()
                split_back[ms[-1]] = units[-1].full_at()
                plan.append((c0, n, ms, units))
                waiting = b
            order.append(("empty", waiting))

            def pe(e):
                for c0, n, ms, units in plan:
                    for u in units:
                        u.wait_free(e)
                    for i, m in enumerate(ms):
                        split_wait(e, m)
                        right = halves_of(m)
                        for t, u in enumerate(units):
                            for k in range(4):
                                last = product(e, u.ap[:, 0:n], chunk_of(pair, 4 * i + k, t),
                                               [r[:, k, :] for r in right], 4 * i + k == 0, 4 * i + k == chunks - 1)
                            if m == ms[-1]:
                                last.then_inc(u.full, 1)
                        if m != ms[-1]:
                            last.then_inc(w_used.sem, 1)

            def other(name):
                def run(e):
                    for what, i in order:
                        if what == "split":
                            (split_act if name == "act" else split_dve)(e, i)
                        elif name == engine:
                            c0, n, _, units = plan[i]
                            for t, u in enumerate(units):
                                u.wait_full(e)
                                empty(e, u.ap[:, 0:n], t, c0, n).then_inc(u.free, 1)
                return run

            stage(pe=pe, act=other("act"), dve=other("dve"))

        def rotate(src, dst, heads, half, t, stride=1):
            c = cos[:, t, 0:32:stride].unsqueeze(1).to_broadcast([P, heads, half])
            s = sin[:, t, 0:32:stride].unsqueeze(1).to_broadcast([P, heads, half])
            x1, x2 = src[:, :, 0, :], src[:, :, 1, :]
            n = heads * half
            flat_probs = probs[:, :, :, :].rearrange("p a b c -> p (a b c)")
            tmp = [flat_probs[:, i * n:(i + 1) * n].rearrange("p (a b) -> p a b", a=heads) for i in range(4)]

            def dve(e):
                link = chains["dve"]
                link.add(e.tensor_tensor(tmp[0], x1, c, ALU.mult))
                link.add(e.tensor_tensor(tmp[1], x2, s, ALU.mult))
                link.add(e.tensor_tensor(tmp[2], x1, s, ALU.mult))
                link(e.tensor_tensor(tmp[3], x2, c, ALU.mult))
                link.add(e.tensor_tensor(dst[:, :, 0, :], tmp[0], tmp[1], ALU.subtract))
                link(e.tensor_tensor(dst[:, :, 1, :], tmp[2], tmp[3], ALU.add))
            return dve

        def dve_stage(steps):
            points = [point(3.0) for _ in steps]

            def dve(e):
                for s, p in zip(steps, points):
                    s(e)
                    p("dve", e)
            stage(dve=dve, points=points)

        def attend(groups, maps_in=scores):
            plan = []
            ahead = len(maps_in.views) - 1
            for g in groups:
                n_out = {"joint": 1, "diff": 2}.get(g["kind"], len(g["maps"]))
                n_turned = 2 if g["kind"] == "diff" else len(g["maps"])
                chunks = g["tile"] + 1
                value = {"s": maps_in.take(), "turns": [turns.take() for _ in range(chunks)], "out": products.take(),
                         "n_out": n_out, "n_turned": n_turned, "chunks": chunks, "w": P * chunks,
                         "m": maxes_ready.plan(), "p": probs_ready.plan()}
                if g["kind"] == "stick":
                    value["m2"] = maxes_ready.plan()
                    value["a1"] = from_act.plan()
                if g["kind"] == "diff":
                    value["a2"] = from_act.plan()
                plan.append(g | value | {"points": [point(6.0), point(6.0)]})

            def sums_of(n):
                at = (16, 24, 48)[n % 3]
                return stat[:, at:at + 8]

            def place(i):
                return (i % 2) * 2 + i // 2

            def places(g):
                n = len(g["maps"])
                return [place(i) for i in range(n)] if g["kind"] != "joint" else list(range(n))

            def pe(e):
                def score(g):
                    g["s"].wait_free(e)
                    for i, (q, k) in enumerate(g["maps"]):
                        last = e.matmul(g["s"].ap[:, places(g)[i], 0:g["w"]], q, k, start=True, stop=True)
                    last.then_inc(g["s"].full, 1)

                def turn_probs(n, g):
                    e.wait_ge(probs_ready.sem, g["p"])
                    for c, u in enumerate(g["turns"]):
                        u.wait_free(e)
                        for i in range(g["n_turned"]):
                            at = i if g["kind"] == "diff" else places(g)[i]
                            last = e.transpose(u.ap[:, i * P:(i + 1) * P], probs[:, n % 2, at, c * P:(c + 1) * P],
                                               ident[:, :])
                        last.then_inc(u.full, 1)

                def sum_values(n, g):
                    u = g["out"]
                    for turned_unit in g["turns"]:
                        turned_unit.wait_emptied(e)
                    u.wait_free(e)
                    for i in range(g["n_turned"]):
                        o = 0 if g["kind"] == "joint" else i
                        for c in range(g["chunks"]):
                            first = c == 0 and (i == 0 or g["kind"] != "joint")
                            final = c == g["chunks"] - 1 and (i == g["n_turned"] - 1 or g["kind"] != "joint")
                            last = e.matmul(u.ap[:, o * HD:(o + 1) * HD], probsT[:, n % 2, c, i, :], g["values"][i](c),
                                            start=first, stop=final)
                    last.then_inc(u.full, 1)

                for g in plan[:ahead]:
                    score(g)
                for n, g in enumerate(plan):
                    if n and ahead:
                        turn_probs(n - 1, plan[n - 1])
                    if n + ahead < len(plan):
                        score(plan[n + ahead])
                    g["points"][0]("pe", e)
                    if n and not ahead:
                        turn_probs(n - 1, plan[n - 1])
                    if n:
                        sum_values(n - 1, plan[n - 1])
                    g["points"][1]("pe", e)
                turn_probs(len(plan) - 1, plan[-1])
                sum_values(len(plan) - 1, plan[-1])

            def empty_turns(e, n, g):
                for c, u in enumerate(g["turns"]):
                    u.wait_full(e)
                    k = g["n_turned"]
                    e.copy(probsT[:, n % 2, c, 0:k, :], u.ap[:, 0:k * P].rearrange("p (n t) -> p n t", n=k)
                           ).then_inc(u.free, 1)

            def act(e):
                link = chains["act"]
                for n, g in enumerate(plan):
                    g["points"][0]("act", e)
                    w, k = g["w"], len(g["maps"])
                    pr = probs[:, n % 2]
                    sums = sums_of(n)
                    neg = stat[:, 32 + 8 * (n % 2):40 + 8 * (n % 2)]
                    if g["kind"] == "stick":
                        az = stick_tmp[:, :, 0:w]
                        g["s"].wait_full(e)
                        link(e.activation(az, g["s"].ap[:, :, 0:w], ACT.Abs, scale=g["scale"]))
                        link(e.activation(az, az, ACT.Exp, scale=-1.0))
                        e.activation(az, az, ACT.Ln, bias=1.0).then_inc(from_act.sem, 1)
                        e.wait_ge(maxes_ready.sem, g["m2"])
                        e.activation(pr[:, :, 0:w], pr[:, :, 0:w], ACT.Exp).then_inc(probs_ready.sem, 1)
                    else:
                        e.wait_ge(maxes_ready.sem, g["m"])
                        if g["kind"] == "joint":
                            last = e.activation(pr[:, 0:k, 0:w], pr[:, 0:k, 0:w], ACT.Exp, bias=neg[:, 0:1],
                                                accum_out=sums[:, 0:1])
                        else:
                            for i in sorted(places(g)):
                                last = e.activation(pr[:, i, 0:w], pr[:, i, 0:w], ACT.Exp, bias=neg[:, i:i + 1],
                                                    accum_out=sums[:, i:i + 1])
                        last.then_inc(from_act.sem if g["kind"] == "diff" else probs_ready.sem, 1)
                    if n:
                        empty_turns(e, n - 1, plan[n - 1])
                    g["points"][1]("act", e)
                empty_turns(e, len(plan) - 1, plan[-1])

            def dve(e):
                link = chains["dve"]

                def soften(n, g):
                    w, k = g["w"], len(g["maps"])
                    pr = probs[:, n % 2]
                    neg = stat[:, 32 + 8 * (n % 2):40 + 8 * (n % 2)]
                    sums = sums_of(n)
                    s = g["s"].ap
                    if g["kind"] == "stick":
                        e.wait_ge(from_act.sem, g["a1"])
                        az = stick_tmp[:, :, 0:w]
                        z = pr[:, :, 0:w]
                        e.tensor_scalar(z, s[:, :, 0:w], g["scale"], None, ALU.mult).then_inc(g["s"].free, 1)
                        e.wait_ge(g["s"].free, g["s"].use + 1)
                        link(e.scalar_tensor_tensor(az, z, 0.0, az, ALU.max, ALU.add))
                        link(e.tensor_tensor(az, az, g["strict"].unsqueeze(1).to_broadcast([P, 4, w]), ALU.mult))
                        for i in range(4):
                            link.add(e.tensor_tensor_scan(az[:, i, ::-1], zero[:, 0:w], az[:, i, ::-1], 0.0,
                                                          ALU.add, ALU.add))
                        link.wait()
                        link(e.tensor_tensor(z, z, az, ALU.subtract))
                        e.tensor_tensor(z, z, g["bias"].unsqueeze(1).to_broadcast([P, 4, w]), ALU.add
                                        ).then_inc(maxes_ready.sem, 2)
                        return
                    g["s"].wait_full(e)
                    if isinstance(g["bias"], list):
                        for i in range(k):
                            at = places(g)[i]
                            last = e.scalar_tensor_tensor(pr[:, at, 0:w], s[:, at, 0:w], g["scale"], g["bias"][i],
                                                          ALU.mult, ALU.add)
                    else:
                        last = e.scalar_tensor_tensor(pr[:, 0:k, 0:w], s[:, 0:k, 0:w], g["scale"],
                                                      g["bias"].unsqueeze(1).to_broadcast([P, k, w]), ALU.mult, ALU.add)
                    last.then_inc(g["s"].free, 1)
                    e.wait_ge(g["s"].free, g["s"].use + 1)
                    if g["kind"] == "joint":
                        link(e.tensor_reduce(neg[:, 0:1], pr[:, 0:k, 0:w], AX.XY, ALU.max))
                        k = 1
                    else:
                        link(e.tensor_reduce(neg[:, 0:k], pr[:, 0:k, 0:w], AX.X, ALU.max))
                    e.tensor_scalar(neg[:, 0:k], neg[:, 0:k], -1.0, None, ALU.mult).then_inc(maxes_ready.sem, 1)

                def combine(n, g):
                    w = g["w"]
                    pr = probs[:, n % 2]
                    sums = sums_of(n)
                    e.wait_ge(from_act.sem, g["a2"])
                    link(e.reciprocal(sums[:, 0:4], sums[:, 0:4]))
                    link(e.tensor_scalar(sums[:, 2:4], sums[:, 2:4], lam, None, ALU.mult))
                    for i in range(2):
                        link(e.tensor_scalar(pr[:, 2 + i, 0:w], pr[:, 2 + i, 0:w], sums[:, 2 + i:3 + i], None, ALU.mult))
                        last = e.scalar_tensor_tensor(pr[:, i, 0:w], pr[:, i, 0:w], sums[:, i:i + 1], pr[:, 2 + i, 0:w],
                                                      ALU.mult, ALU.subtract)
                        if i == 0:
                            link(last)
                    last.then_inc(probs_ready.sem, 1)

                def take_out(n, g):
                    sums = sums_of(n)
                    k = g["n_out"]
                    if g["kind"] in ("softmax", "joint"):
                        e.wait_ge(probs_ready.sem, g["p"])
                        link(e.reciprocal(sums[:, 0:max(k, 1)], sums[:, 0:max(k, 1)]))
                    g["out"].wait_full(e)
                    src = g["out"].ap[:, 0:k * HD].rearrange("p (n d) -> p n d", n=k)
                    if g["kind"] == "softmax":
                        for par in range(2):
                            r = sums[:, 2 * par:2 * par + 2].unsqueeze(2).to_broadcast([P, 2, HD])
                            last = e.tensor_tensor(g["out_ap"][:, par::2, :], src[:, par::2, :], r, ALU.mult)
                            if par == 0:
                                link(last)
                    elif g["kind"] == "joint":
                        last = e.tensor_scalar(g["out_ap"], src, sums[:, 0:1], None, ALU.mult)
                    else:
                        last = e.tensor_copy(g["out_ap"], src)
                    last.then_inc(g["out"].free, 1)

                for n, g in enumerate(plan):
                    if g.get("before"):
                        g["before"](e)
                    if n >= 2:
                        for u in plan[n - 2]["turns"]:
                            u.wait_full(e)
                    soften(n, g)
                    g["points"][0]("dve", e)
                    if n >= 2:
                        take_out(n - 2, plan[n - 2])
                    if g["kind"] == "diff":
                        combine(n, g)
                    g["points"][1]("dve", e)
                for n in range(len(plan) - 2, len(plan)):
                    take_out(n, plan[n])

            stage(pe=pe, act=act, dve=dve, points=[p for g in plan for p in g["points"]], us=5.0)

        raw = sb("raw", [P, 8])
        lam = small[:, 250:251]
        flat = rows[:, :, :].rearrange("p a b -> p (a b)")

        def carve(at, shape):
            n = int(np.prod(shape))
            v = flat[:, at:at + n]
            return v.rearrange("p (a b) -> p a b", a=shape[0]) if len(shape) == 2 else v

        stick_tmp = carve(0, (4, SEQ))
        dist = carve(1024, (TILES, SEQ))
        strict = carve(1536, (TILES, SEQ))
        strict_bias = carve(2048, (TILES, SEQ))
        zero = carve(2560, (SEQ,))
        dil_bias = [causal] + [carve(2816 + 512 * i, (TILES, SEQ)) for i in range(2)]
        window = carve(3840, (TILES, SEQ))
        head_bias = carve(4352, (4, SEQ))
        gates = probs[:, 0].rearrange("p a b -> p (a b)").rearrange("p (t n) -> p t n", t=TILES)
        upper = carve(6400, (TILES, SEQ))
        forget = carve(6912, (TILES, 4))
        cum_keys = carve(6920, (4, SEQ))

        inv = small[:, 0:32]
        ang = small[:, 32:96].rearrange("p (t f) -> p t f", t=TILES)
        turns_n = small[:, 96:160].rearrange("p (t f) -> p t f", t=TILES)
        pos = raw[:, 0:2]
        pos_i = raw[:, 2:4]
        ang_v, sin_v = to_act.plan(), from_act.plan()

        def angles_dve(e):
            link = chains["dve"]
            e.wait_ge(consts_landed, 32)
            link(e.tensor_copy(pos, pos_i.bitcast(I32)))
            for t in range(TILES):
                link.add(e.tensor_scalar(ang[:, t, :], inv, pos[:, t:t + 1], None, ALU.mult))
            link.wait()
            link(e.tensor_scalar(turns_n, ang, float(1 / TWO_PI), ROUND, ALU.mult, ALU.add))
            link(e.tensor_scalar(turns_n, turns_n, ROUND, None, ALU.subtract))
            for c in (C1, C2, C3):
                link(e.scalar_tensor_tensor(ang, turns_n, -c, ang, ALU.mult, ALU.add))
            link(e.tensor_scalar(ang, ang, 3.1415925, -3.1415925, ALU.min, ALU.max))
            link(e.scalar_tensor_tensor(turns_n, ang, -1.0, ang, ALU.mult, ALU.max))
            e.tensor_scalar(turns_n, turns_n, -1.0, float(np.pi / 2), ALU.mult, ALU.add).then_inc(to_act.sem, 1)

        def angles_act(e):
            e.wait_ge(to_act.sem, ang_v)
            e.activation(sin[:, :, :], ang, ACT.Sin)
            e.activation(cos[:, :, :], turns_n, ACT.Sin).then_inc(from_act.sem, 1)

        def wait_pool_pe(e):
            e.wait_ge(pool_made, 1)

        def wait_pool_dve(e):
            e.wait_ge(pool_made, 1)
            e.wait_ge(x_landed, 16)
            angles_dve(e)

        stage(pe=wait_pool_pe, act=angles_act, dve=wait_pool_dve)

        X = lambda t: x[:, t, :]
        H = lambda t: h[:, t, :]
        M = lambda t: mixed[:, t, 0:D]
        T = turned[:, :].rearrange("p (c s) -> p c s", s=SEQ)

        def add_residual(e, ps, t, c0, n):
            return e.tensor_tensor(x[:, t, c0:c0 + n], x[:, t, c0:c0 + n], ps, ALU.add)

        def copy_to(buf):
            return lambda e, ps, t, c0, n: e.copy(buf[:, t, c0:c0 + n], ps)

        norm(X, H, D, a["attn_norm"][0:1, :])
        T_quads = quads(turned_r[:, :])
        x_pair = quads(hT_r[:, :]), T_quads[0:2]
        turn_split(H, x_pair)
        proj = tok[:, 0:TILES * EVEN_COLS].rearrange("p (t n) -> p t n", t=TILES)
        project_split(x_pair, a["hyb_w_in"][0], DC, EVEN_COLS, copy_to(proj), "act", (0, 1))
        R_QA, R_KA, R_IQ, R_IK, R_QB, R_KB = 0, 512, 640, 1152, 1280, 1792
        rot = tok[:, TILES * EVEN_COLS:TILES * (EVEN_COLS + 2304)].rearrange("p (t n) -> p t n", t=TILES)
        steps = []
        for t in range(TILES):
            for src, dst, heads in ((QA, R_QA, 8), (KA, R_KA, 1), (KA, R_KA + HD, 1), (IQ, R_IQ, 8), (IK, R_IK, 1),
                                    (IK, R_IK + HD, 1), (QB, R_QB, 16)):
                sv, dv = (b[:, t, o:o + heads * HD].rearrange("p (a b c) -> p a b c", a=heads, b=2)
                          for b, o in ((proj, src), (rot, dst)))
                steps.append(rotate(sv, dv, heads, HD // 2, t))
        dve_stage(steps)
        turn_wide(lambda t: rot[:, t, :], T, 18)

        def head_T(first, i, t, n=1, shared=False):
            c = first // P + (0 if shared else i // 2)
            r = (i % 2) * HD
            return T[r:r + HD, c, t * P:t * P + n * P]

        keep_bias = carve(0, (TILES, SEQ))
        rank = carve(512, (TILES, SEQ))
        relu = carve(1024, (4, SEQ))
        iws = stat[:, 56:64]

        def index(t):
            w = P * (t + 1)
            w_scale = 8 ** -0.5 * 64 ** -0.5
            units = [scores.take() for _ in range(2)]
            used_values = [relu_used.plan() for _ in range(2)]
            rk = rank[:, t, 0:w]

            def pe(e):
                for j, u in enumerate(units):
                    u.wait_free(e)
                    for i in range(4):
                        last = e.matmul(u.ap[:, (i % 2) * 2 + i // 2, 0:w], head_T(R_IQ, 4 * j + i, t),
                                        head_T(R_IK, i, 0, t + 1, True), start=True, stop=True)
                    last.then_inc(u.full, 1)

            def act(e):
                for u, used in zip(units, used_values):
                    u.wait_full(e)
                    if used > 1:
                        e.wait_ge(relu_used.sem, used - 1)
                    e.activation(relu[:, :, 0:w], u.ap[:, :, 0:w], ACT.Relu).then_inc(u.free, 1)

            def dve(e):
                link = chains["dve"]
                link(e.tensor_scalar(iws, proj[:, t, IW:IW + 8], w_scale, None, ALU.mult))
                for j, (u, used) in enumerate(zip(units, used_values)):
                    u.wait_emptied(e)
                    for i in range(4):
                        src = relu[:, (i % 2) * 2 + i // 2, 0:w]
                        s = iws[:, 4 * j + i:4 * j + i + 1]
                        if j == 0 and i == 0:
                            link(e.tensor_scalar(rk, src, s, None, ALU.mult))
                        elif i < 3:
                            link(e.scalar_tensor_tensor(rk, src, s, rk, ALU.mult, ALU.add))
                        else:
                            e.scalar_tensor_tensor(rk, src, s, rk, ALU.mult, ALU.add).then_inc(relu_used.sem, 1)
                            e.wait_ge(relu_used.sem, used)
                link(e.tensor_tensor(rk, rk, causal[:, t, 0:w], ALU.add))
                m8 = stat[:, 48:56]
                for _ in range(DSA_KEEP // 8):
                    link(e.max(m8, rk))
                    link(e.match_replace(rk, m8, rk, TAKEN))
                kb = keep_bias[:, t, 0:w]
                link(e.tensor_scalar(kb, rk, TAKEN / 2, NEG, ALU.is_gt, ALU.mult))
                link(e.tensor_tensor(kb, kb, causal[:, t, 0:w], ALU.add))

            stage(pe=pe, act=act, dve=dve)

        for t in range(TILES):
            index(t)

        groups = []
        for t in range(TILES):
            for j in range(2):
                hs = range(4 * j, 4 * j + 4)
                groups.append(dict(
                    kind="softmax", tile=t, scale=HD ** -0.5, bias=keep_bias[:, t, 0:P * (t + 1)],
                    maps=[(head_T(R_QA, i, t), head_T(R_KA, i, 0, t + 1, True)) for i in hs],
                    values=[lambda c: proj[:, c, VA:VA + HD]] * 4,
                    out_ap=mixed[:, t, 256 * j:256 * j + 256].rearrange("p (n d) -> p n d", d=HD)))
            for j in range(2):
                hs = range(4 * j, 4 * j + 4)
                groups.append(dict(
                    kind="softmax", tile=t, scale=HD ** -0.5, bias=causal[:, t, 0:P * (t + 1)],
                    maps=[(head_T(R_QB, i, t), head_T(R_KB, i, 0, t + 1)) for i in hs],
                    values=[(lambda c, i=i: proj[:, c, VB + i * HD:VB + (i + 1) * HD]) for i in hs],
                    out_ap=mixed[:, t, 512 + 256 * j:768 + 256 * j].rearrange("p (n d) -> p n d", d=HD)))
        attend(groups, two_scores)
        turn_split(M, (T_quads[0:2], T_quads[2:4]))
        project_split((T_quads[0:2], T_quads[2:4]), a["hyb_w_out"][0], DC, D, add_residual, "dve", (0, 1))

        qT = turned[:, 16 * SEQ:16 * SEQ + 16 * P].rearrange("p (n t) -> p n t", n=16)
        key_scores = turned[:, 16 * SEQ + 16 * P:32 * SEQ].rearrange("p (n k) -> p n k", n=16)
        spare = tok[:, MLA_HEADS * P * TILES:]
        onehot = spare[:, 0:2048]
        best = spare[:, 2048:2304].rearrange("p (n k) -> p n k", n=16)
        best_at = spare[:, 2304:2560].rearrange("p (n k) -> p n k", n=16)
        best_f = spare[:, 2560:2816].rearrange("p (n k) -> p n k", n=16)
        top = spare[:, 2816:2944].rearrange("p (n k) -> p n k", n=EH)
        top_at = spare[:, 2944:3072].rearrange("p (n k) -> p n k", n=EH)
        hi = spare[:, 3072:3200]
        lo = spare[:, 3200:3328]
        pick = [spare[:, 3328:3456], spare[:, 3456:3584]]
        iota16 = sb("iota16", [P, TOP])

        routed = {}

        def route(layer, t):
            wq = rows_of(a["peer_w_q"][layer])
            plan = []
            for b in range(4):
                slots = [(weights(wq[:, k:k + 4, b * 512:(b + 1) * 512], 4, 512), k) for k in (0, 4)]
                plan.append((slots, products.take()))
                for s, _ in slots:
                    given_back[s] = plan[-1][1].full_at()
            keys = weights(a["peer_keys"][layer].rearrange("(o p) n -> p o n", o=1), 1, SLOT)
            key_units = [products.take() for _ in range(4)]
            given_back[keys] = key_units[-1].full_at()
            e_in, e_out = to_act.plan(), from_act.plan()
            routed[layer, t] = experts_ready.plan()
            made = [point(5.0) for _ in range(4)] + [point(3.0)]
            ranked = [point(5.0) for _ in range(12)]

            def pe(e):
                for b, (slots, u) in enumerate(plan):
                    u.wait_free(e)
                    for s, _ in slots:
                        slot_wait(e, s)
                    for j in range(4):
                        for s, k0 in slots:
                            for k in range(4):
                                last = e.matmul(u.ap[:, j * P:(j + 1) * P], slot_ap(s)[:, k, j * P:(j + 1) * P],
                                                hT[:, k0 + k, t * P:(t + 1) * P], start=k0 + k == 0,
                                                stop=k0 + k == DC - 1)
                    last.then_inc(u.full, 1)
                    made[b]("pe", e)
                slot_wait(e, keys)
                for b, u in enumerate(key_units):
                    plan[b][1].wait_emptied(e)
                    u.wait_free(e)
                    for j in range(4 * b, 4 * b + 4):
                        last = e.matmul(u.ap[:, (j % 4) * P:(j % 4 + 1) * P], qT[:, j, :],
                                        slot_ap(keys)[:, 0, j * P:(j + 1) * P], start=True, stop=True)
                    last.then_inc(u.full, 1)
                for p in made[4:] + ranked:
                    p("pe", e)

            def act(e):
                for b, (_, u) in enumerate(plan):
                    u.wait_full(e)
                    e.copy(qT[:, 4 * b:4 * b + 4, :], u.ap.rearrange("p (n t) -> p n t", n=4)).then_inc(u.free, 1)
                    made[b]("act", e)
                for b, u in enumerate(key_units):
                    u.wait_full(e)
                    e.copy(key_scores[:, 4 * b:4 * b + 4, :], u.ap.rearrange("p (n t) -> p n t", n=4)
                           ).then_inc(u.free, 1)
                for p in made[4:] + ranked:
                    p("act", e)
                e.wait_ge(to_act.sem, e_in)
                e.activation(share[:, t, :], share[:, t, :], ACT.Exp).then_inc(from_act.sem, 1)

            def dve(e):
                link = chains["dve"]
                for p in made:
                    p("dve", e)
                halves = [(key_scores[:, j, :], best[:, j, :], best_at[:, j, :].bitcast(U32)) for j in range(16)]

                rest = list(ranked)

                def top16(items, ready):
                    for j, (v, m, at) in enumerate(items):
                        if ready:
                            key_units[j // 4].wait_emptied(e)
                        link.add(e.max(m[:, 0:8], v))
                    link.wait()
                    rest.pop(0)("dve", e)
                    for v, m, at in items:
                        link.add(e.max_index(at[:, 0:8], m[:, 0:8], v))
                    link.wait()
                    rest.pop(0)("dve", e)
                    for v, m, at in items:
                        link.add(e.match_replace(v, m[:, 0:8], v, TAKEN))
                    link.wait()
                    rest.pop(0)("dve", e)
                    for v, m, at in items:
                        link.add(e.max(m[:, 8:16], v))
                    link.wait()
                    rest.pop(0)("dve", e)
                    for v, m, at in items:
                        link.add(e.max_index(at[:, 8:16], m[:, 8:16], v))
                    link.wait()
                    rest.pop(0)("dve", e)

                top16(halves, True)
                link(e.tensor_copy(best_f, best_at.bitcast(U32)))
                cand = key_scores.rearrange("p n k -> p (n k)").rearrange("p (h i j) -> p h i j", h=EH, i=TOP)
                b4 = best.rearrange("p (h s) k -> p h s k", s=2)
                link(e.tensor_tensor(cand, b4[:, :, 0, :].unsqueeze(3).to_broadcast([P, EH, TOP, TOP]),
                                     b4[:, :, 1, :].unsqueeze(2).to_broadcast([P, EH, TOP, TOP]), ALU.add))
                cf = key_scores.rearrange("p n k -> p (n k)").rearrange("p (h m) -> p h m", h=EH)
                top16([(cf[:, j, :], top[:, j, :], top_at[:, j, :].bitcast(U32)) for j in range(EH)], False)
                rest.pop(0)("dve", e)
                at = top_at.rearrange("p n k -> p (n k)").bitcast(I32)
                link.add(e.tensor_scalar(pick[0].bitcast(I32), at, 4, None, ALU.arith_shift_right))
                link(e.tensor_scalar(pick[1].bitcast(I32), at, 15, None, ALU.bitwise_and))
                link.add(e.tensor_copy(hi, pick[0].bitcast(I32)))
                link(e.tensor_copy(lo, pick[1].bitcast(I32)))
                f4 = best_f.rearrange("p (h s) k -> p h s k", s=2)
                oh3 = onehot.rearrange("p (a i) -> p a i", i=TOP)
                oh4 = onehot.rearrange("p (h k i) -> p h k i", h=EH, k=TOP)
                for s, where in enumerate((hi, lo)):
                    link(e.tensor_tensor(oh3, where.unsqueeze(2).to_broadcast([P, P, TOP]),
                                         iota16[:, :].unsqueeze(1).to_broadcast([P, P, TOP]), ALU.is_equal))
                    link(e.tensor_tensor(oh4, oh4, f4[:, :, s, :].unsqueeze(2).to_broadcast([P, EH, TOP, TOP]),
                                         ALU.mult))
                    link(e.tensor_reduce(pick[s], oh3, AX.X, ALU.add))
                for p in rest:
                    p("dve", e)
                if layer:
                    link(e.tensor_scalar(pick[1], pick[1], float(layer * NK * NK), None, ALU.add))
                e.scalar_tensor_tensor(expert[:, t, :], pick[0], float(NK), pick[1], ALU.mult, ALU.add
                                       ).then_inc(experts_ready.sem, 1)
                sh = share[:, t, :].rearrange("p (h k) -> p h k", h=EH)
                e.tensor_tensor(sh, top, top[:, :, 0:1].to_broadcast([P, EH, TOP]), ALU.subtract
                                ).then_inc(to_act.sem, 1)
                e.wait_ge(from_act.sem, e_out)
                link(e.tensor_reduce(small[:, 240:248], sh, AX.X, ALU.add))
                link(e.reciprocal(small[:, 240:248], small[:, 240:248]))
                link(e.tensor_tensor(sh, sh, small[:, 240:248].unsqueeze(2).to_broadcast([P, EH, TOP]), ALU.mult))

            stage(pe=pe, act=act, dve=dve, points=made + ranked)

        gathers = []

        def start_experts(layer, t):
            n0 = len(gathers) * P
            gathers.append((layer, t, routed[layer, t]))
            gelu_v = [gelu_ready.plan() for _ in range(EH)]
            weights_v = [weights_ready.plan() for _ in range(EH)]

            def dve(e, i):
                if i < P:
                    n = n0 + i
                    e.wait_ge(u_landed[n % U_SLOTS], 16 * (n // U_SLOTS + 1))
                    r = rows[:, n % U_SLOTS, :]
                    e.tensor_tensor_reduce(r, r, h[:, t, :], 1.0, 0.0, ALU.mult, ALU.add,
                                           dots[:, i:i + 1]).then_inc(u_used.sem, 1)
                j = i // TOP - 1
                if i % TOP == 1 and 0 <= j < EH:
                    e.wait_ge(gelu_ready.sem, gelu_v[j])
                    e.tensor_tensor(weight[:, j * TOP:(j + 1) * TOP], gelu[:, j % 2, :],
                                    share[:, t, j * TOP:(j + 1) * TOP], ALU.mult).then_inc(weights_ready.sem, 1)

            def act(e, i):
                j = i // TOP - 1
                if i % TOP == 0 and 0 <= j < EH:
                    e.wait_ge(u_used.sem, n0 + (j + 1) * TOP)
                    e.activation(gelu[:, j % 2, :], dots[:, j * TOP:(j + 1) * TOP], ACT.Gelu
                                 ).then_inc(gelu_ready.sem, 1)
                k = i - LAG
                if k >= 0:
                    n = n0 + k
                    if k % TOP == 0:
                        e.wait_ge(weights_ready.sem, weights_v[k // TOP])
                    if n >= DIAGS:
                        e.wait_ge(v_used.sem, n - DIAGS + 1)
                    e.activation(diag[:, n % DIAGS, :], ident[:, :], ACT.Copy,
                                 scale=weight[:, k:k + 1]).then_inc(diag_ready.sem, 1)

            def pe(e, i):
                k = i - LAG
                if k >= 0:
                    n = n0 + k
                    e.wait_ge(v_landed[n % V_SLOTS], 16 * (n // V_SLOTS + 1))
                    e.wait_ge(diag_ready.sem, n + 1)
                    for b in range(2):
                        last = e.matmul(ps_acc[:, b * 512:(b + 1) * 512], diag[:, n % DIAGS, :],
                                        rows[:, U_SLOTS + n % V_SLOTS, b * 512:(b + 1) * 512],
                                        start=k == 0, stop=k == P - 1)
                    last.then_inc(v_used.sem, 1)

            feeds.append({"open": True, "first": 0, "weight": 0.0, "cuts": [], "pe": pe, "act": act, "dve": dve})

        def finish_experts(t, behind=None):
            f = feeds[-1]
            f["open"] = False
            items = range(handed_out(f, f["weight"]), ITEMS)
            total = len(gathers) * P
            if behind:
                start_experts(*behind)
                feeds[-1]["first"] = LAG
            then = feeds[-1] if behind else None

            def part(name):
                def run(e):
                    for i in items:
                        f[name](e, i)
                        if then and i >= P:
                            then[name](e, i - P)
                return run

            def dve(e):
                link = chains["dve"]
                part("dve")(e)
                e.wait_ge(v_used.sem, total)
                for b in range(2):
                    link.add(e.tensor_tensor(x[:, t, b * 512:(b + 1) * 512], x[:, t, b * 512:(b + 1) * 512],
                                             ps_acc[:, b * 512:(b + 1) * 512], ALU.add))
                link.wait()

            stage(pe=part("pe"), act=part("act"), dve=dve)

        def feed_forward(layer, tiles):
            norm(X, H, D, a["ffn_norm"][layer:layer + 1, :], tiles)
            turn_wide(H, hT, DC, tiles)
            for t in tiles:
                route(layer, t)

        feed_forward(0, [0])
        start_experts(0, 0)
        feed_forward(0, [1])
        finish_experts(0, (0, 1))

        n_q, n_kv = MLA_HEADS * MLA_D, MLA_HEADS * P
        kv_tok = tok[:, 0:TILES * n_kv].rearrange("p (t n) -> p t n", t=TILES)
        q_tok = spare[:, 0:n_q]
        k_tok = spare[:, n_q:2 * n_q]
        kh = turned[:, 0:16 * SEQ].rearrange("p (n s) -> p n s", s=SEQ)
        qh = turned[:, 16 * SEQ:16 * SEQ + 16 * P].rearrange("p (n s) -> p n s", s=P)
        mixedT = turned[:, 16 * SEQ + 16 * P:32 * SEQ].rearrange("p (c s) -> p c s", s=SEQ)

        def latent(t):
            tiles = [t]
            norm(X, H, D, a["attn_norm"][1:2, :], tiles)
            turn_wide(H, hT, DC, tiles)
            project(hT, a["mla_w_in"][0], DC, Q_RANK + KV_RANK + ROPE, copy_to(mixed), "act", tiles)
            norm(lambda t: mixed[:, t, 0:Q_RANK], lambda t: h[:, t, 0:Q_RANK], Q_RANK, a["mla_q_norm"], tiles)
            norm(lambda t: mixed[:, t, Q_RANK:D], lambda t: h[:, t, Q_RANK:D], KV_RANK, a["mla_kv_norm"], tiles)
            turn_wide(H, hT, DC, tiles)
            project(hT[:, 0:6, :], a["mla_w_uq"][0], 6, n_q,
                    lambda e, ps, t, c0, n: e.copy(q_tok[:, c0:c0 + n], ps), "act", tiles)
            project(hT[:, 6:8, :], a["mla_w_ukv"][0], 2, n_kv, copy_to(kv_tok), "act", tiles)
            q3 = q_tok.rearrange("p (n d) -> p n d", n=MLA_HEADS)
            k3 = k_tok.rearrange("p (n d) -> p n d", n=MLA_HEADS)
            kv3 = kv_tok[:, t, :].rearrange("p (n d) -> p n d", n=MLA_HEADS)
            qr = q3[:, :, NOPE:MLA_D].rearrange("p n (b c) -> p n b c", b=2)
            kr = mixed[:, t, D:D + ROPE].rearrange("p (n b c) -> p n b c", n=1, b=2)

            def keys(e):
                chains["dve"].add(e.tensor_copy(k3[:, :, 0:NOPE], kv3[:, :, 0:NOPE]))
                chains["dve"].add(e.tensor_copy(k3[:, :, NOPE:MLA_D], mixed[:, t, D:D + ROPE].unsqueeze(1)
                                                .to_broadcast([P, MLA_HEADS, ROPE])))

            dve_stage([rotate(qr, qr, MLA_HEADS, ROPE // 2, t, 2), rotate(kr, kr, 1, ROPE // 2, t, 2), keys])
            blocks = []
            for src, dst in ((q_tok, qh), (k_tok, kh[:, :, t * P:(t + 1) * P])):
                for n0 in range(0, MLA_HEADS, 4):
                    blocks.append(([src[:, n * MLA_D:(n + 1) * MLA_D] for n in range(n0, n0 + 4)],
                                   dst[0:MLA_D, n0:n0 + 4, :]))
            turn(blocks)
            attend([dict(
                kind="softmax", tile=t, scale=MLA_D ** -0.5, bias=causal[:, t, 0:P * (t + 1)],
                maps=[(qh[0:MLA_D, n, :], kh[0:MLA_D, n, 0:P * (t + 1)]) for n in range(n0, n0 + 4)],
                values=[(lambda c, n=n: kv_tok[:, c, n * P + NOPE:(n + 1) * P]) for n in range(n0, n0 + 4)],
                out_ap=mixed[:, t, n0 * HD:(n0 + 4) * HD].rearrange("p (n d) -> p n d", d=HD))
                for n0 in range(0, MLA_HEADS, 4)])
            turn_wide(M, mixedT, DC, tiles)
            project(mixedT, a["mla_w_out"][0], DC, D, add_residual, "dve", tiles)

        latent(0)
        feed_forward(1, [0])
        finish_experts(1, (1, 0))
        latent(1)
        feed_forward(1, [1])
        finish_experts(0, (1, 1))
        finish_experts(1)

        norm(X, M, D, a["final_norm"])
        dve_stage([lambda e, t=t: e.tensor_copy(X(t), M(t)) for t in range(TILES)])

        norm(X, H, D, a["mix_norm_g_2"])
        mix = tok[:, 0:TILES * MIX].rearrange("p (t n) -> p t n", t=TILES)
        low = tok_r[:, TILES * MIX:TILES * MIX + 4 * SEQ]
        x_pair = quads(hT_r[:, :]), [T_quads[7]] + quads(low)
        turn_split(H, x_pair)
        project_split(x_pair, a["w_in_2"][0][:, 0:MIX], DC, MIX, copy_to(mix), "act", (0, 1))
        (S_Q, S_K, S_V, D_Q, D_K, D_V, F_Q, F_K, F_V, F_F, E_Q, E_K, E_V) = (
            int(c) for c in np.cumsum([0, 256, 256, 256, 768, 768, 768, 256, 256, 256, 4, 256, 256]))
        T_SQ, T_SK, T_DQ, T_DK, T_FQ, T_FK, T_EQ, T_EK = 0, 2, 4, 10, 16, 18, 20, 24
        blocks = []
        for t in range(TILES):
            for col, first, n in ((S_Q, T_SQ, 4), (D_Q, T_DQ, 4), (D_Q + 512, T_DQ + 4, 4), (D_K + 256, T_DK + 2, 4),
                                  (F_Q, T_FQ, 4)):
                blocks.append(([mix[:, t, col + c * P:col + (c + 1) * P] for c in range(n)],
                               T[:, first:first + n, t * P:(t + 1) * P]))
            for col, first in ((E_Q, T_EQ), (E_K, T_EK)):
                blocks.append(([mix[:, t, col + c * HD:col + (c + 1) * HD] for c in range(4)],
                               T[0:HD, first:first + 4, t * P:(t + 1) * P]))
        turn(blocks)

        fl_in, fl_out = to_act.plan(), from_act.plan()
        l_in, l_out = to_act.plan(), from_act.plan()
        col_unit = products.take()
        key_units = [products.take() for _ in range(2)]
        bf = small[:, 0:4]
        lams = small[:, 8:136].rearrange("p (n d) -> p n d", n=4)
        lf_b = stick_tmp[:, :, :].rearrange("p a b -> p (a b)").rearrange("p (r h q) -> p r h q", r=TILES, h=4)
        cum_q = small[:, 140:148].rearrange("p (t h) -> p t h", t=TILES)
        cum_pe = var_ready.plan()
        causal_in = [causal[:, t, 0:P * (t + 1)] for t in range(TILES)]
        diff_gain = small[:, 150:214]
        last_landed = sem("last_landed")
        masks_made = sem("masks_made")

        def masks_dve(e):
            link = chains["dve"]
            e.wait_ge(masks_made, 1)
            e.wait_ge(last_landed, 48)
            fv = mix[:, :, F_F:F_F + 4]
            f0 = forget[:, :, :]
            f1 = stat[:, 0:8].rearrange("p (t h) -> p t h", t=TILES)
            link(e.tensor_tensor(f0, fv, bf.unsqueeze(1).to_broadcast([P, TILES, 4]), ALU.add))
            link(e.scalar_tensor_tensor(f1, f0, -1.0, f0, ALU.mult, ALU.max))
            e.tensor_scalar(f1, f1, -1.0, None, ALU.mult).then_inc(to_act.sem, 1)
            e.wait_ge(from_act.sem, fl_out)
            link(e.scalar_tensor_tensor(f0, f0, 0.0, f1, ALU.min, ALU.subtract))
            for r in range(TILES):
                last = e.tensor_copy(lf_b[:, r], f0[:, r, :].unsqueeze(2).to_broadcast([P, 4, P]))
            last.then_inc(var_ready.sem, 1)
            for i in range(2):
                last = e.tensor_tensor_reduce(lams[:, 2 * i, :], lams[:, 2 * i, :], lams[:, 2 * i + 1, :], 1.0, 0.0,
                                              ALU.mult, ALU.add, stat[:, 8 + i:9 + i])
            last.then_inc(to_act.sem, 1)
            e.wait_ge(from_act.sem, l_out)
            link(e.tensor_tensor(lam, stat[:, 8:9], stat[:, 9:10], ALU.subtract))
            link(e.tensor_scalar(lam, lam, LAMBDA_INIT, None, ALU.add))
            link(e.tensor_scalar(diff_gain, diff_gain, 1.0 - LAMBDA_INIT, None, ALU.mult))
            link.add(e.memset(zero, 0.0))
            link.add(e.tensor_scalar(strict, dist, 0.0, None, ALU.is_gt))
            link.add(e.tensor_scalar(strict_bias, dist, 0.0, NEG, ALU.is_le, ALU.mult))
            di = window.bitcast(I32)
            for g in (1, 2):
                link(e.tensor_copy(di, dist))
                link(e.tensor_scalar(di, di, DIL[g][1] - 1, None, ALU.bitwise_and))
                link(e.tensor_copy(dil_bias[g], di))
                link(e.tensor_scalar(dil_bias[g], dil_bias[g], 0.0, NEG, ALU.not_equal, ALU.mult))
                link(e.tensor_tensor(dil_bias[g], dil_bias[g], causal[:, :, :], ALU.add))
            link(e.tensor_scalar(window, dist, float(DIL[0][0]), NEG, ALU.is_gt, ALU.mult))
            link(e.tensor_tensor(window, window, causal[:, :, :], ALU.add))
            col_unit.wait_full(e)
            e.tensor_copy(cum_q, col_unit.ap[:, 0:8].rearrange("p (t h) -> p t h", t=TILES)
                          ).then_inc(col_unit.free, 1)
            for j, u in enumerate(key_units):
                u.wait_full(e)
                e.tensor_copy(cum_keys[:, 2 * j:2 * j + 2, :], u.ap.rearrange("p (n s) -> p n s", n=2)
                              ).then_inc(u.free, 1)

        def masks_act(e):
            link = chains["act"]
            f1 = stat[:, 0:8]
            e.wait_ge(to_act.sem, fl_in)
            link(e.activation(f1, f1, ACT.Exp))
            e.activation(f1, f1, ACT.Ln, bias=1.0).then_inc(from_act.sem, 1)
            e.wait_ge(to_act.sem, l_in)
            e.activation(stat[:, 8:10], stat[:, 8:10], ACT.Exp).then_inc(from_act.sem, 1)

        def masks_pe(e):
            e.wait_ge(masks_made, 1)
            e.wait_ge(var_ready.sem, cum_pe)
            col_unit.wait_free(e)
            for t in range(TILES):
                for r in range(t + 1):
                    last = e.matmul(col_unit.ap[:, 4 * t:4 * t + 4], upper[:, r, t * P:(t + 1) * P], forget[:, r, :],
                                    start=r == 0, stop=r == t)
            last.then_inc(col_unit.full, 1)
            for j, u in enumerate(key_units):
                u.wait_free(e)
                for i in range(2):
                    for r in range(TILES):
                        last = e.matmul(u.ap[:, i * SEQ:(i + 1) * SEQ], lf_b[:, r, 2 * j + i, :], upper[:, r, :],
                                        start=r == 0, stop=r == TILES - 1)
                last.then_inc(u.full, 1)

        masks_stage = len(stages)
        stage(pe=masks_pe, act=masks_act, dve=masks_dve)

        def bias_of(t, make):
            def before(e):
                for i in range(4):
                    make(e, i)
                chains["dve"].wait()
            return before

        def masked_slope(t, masks, slopes):
            w = P * (t + 1)

            def before(e):
                link = chains["dve"]
                link.wait()
                for i, (m, s) in enumerate(zip(masks, slopes)):
                    link.add(e.scalar_tensor_tensor(head_bias[:, i, 0:w], dist[:, t, 0:w], -s, m[:, t, 0:w],
                                                    ALU.mult, ALU.add))
                link.wait()
            return before

        def forget_bias(t):
            w = P * (t + 1)

            def before(e):
                link = chains["dve"]
                for i in range(4):
                    link.add(e.scalar_tensor_tensor(head_bias[:, i, 0:w], causal[:, t, 0:w], cum_q[:, t, i:i + 1],
                                                    cum_keys[:, i, 0:w], ALU.add, ALU.subtract))
                link.wait()
            return before

        def two_T(first, i, t, n=1):
            return T[(i % 2) * HD:(i % 2) * HD + HD, first + i // 2, t * P:t * P + n * P]

        groups = []
        for t in range(TILES):
            w = P * (t + 1)
            groups.append(dict(
                kind="stick", tile=t, scale=HD ** -0.5, bias=strict_bias[:, t, 0:w], strict=strict[:, t, 0:w],
                maps=[(two_T(T_SQ, i, t), two_T(T_SK, i, 0, t + 1)) for i in range(4)],
                values=[(lambda c, i=i: mix[:, c, S_V + i * HD:S_V + (i + 1) * HD]) for i in range(4)],
                out_ap=mixed[:, t, 0:256].rearrange("p (n d) -> p n d", d=HD)))
            for i in range(4):
                groups.append(dict(
                    kind="joint", tile=t, scale=HD ** -0.5, bias=[head_bias[:, g, 0:w] for g in range(3)],
                    before=masked_slope(t, [window] + dil_bias[1:], [SLOPES_DIL[g][i] for g in range(3)]),
                    maps=[(two_T(T_DQ, 4 * g + i, t), two_T(T_DK, 4 * g + i, 0, t + 1)) for g in range(3)],
                    values=[(lambda c, n=4 * g + i: mix[:, c, D_V + n * HD:D_V + (n + 1) * HD]) for g in range(3)],
                    out_ap=mixed[:, t, 256 + i * HD:256 + (i + 1) * HD].rearrange("p (n d) -> p n d", n=1)))
            groups.append(dict(
                kind="softmax", tile=t, scale=HD ** -0.5, bias=[head_bias[:, i, 0:w] for i in range(4)],
                before=forget_bias(t),
                maps=[(two_T(T_FQ, i, t), two_T(T_FK, i, 0, t + 1)) for i in range(4)],
                values=[(lambda c, i=i: mix[:, c, F_V + i * HD:F_V + (i + 1) * HD]) for i in range(4)],
                out_ap=mixed[:, t, 512:768].rearrange("p (n d) -> p n d", d=HD)))
            for j in range(2):
                hs = (2 * j, 2 * j + 1)
                order = [(n, c) for n in hs for c in range(2)]
                groups.append(dict(
                    kind="diff", tile=t, scale=32 ** -0.5, bias=[head_bias[:, i // 2, 0:w] for i in range(4)],
                    before=masked_slope(t, [causal, causal], [SLOPES_DIFF[n] for n in hs]),
                    maps=[(T[32 * c:32 * c + 32, T_EQ + n, t * P:(t + 1) * P], T[32 * c:32 * c + 32, T_EK + n, 0:w])
                          for n, c in order],
                    values=[(lambda c, n=n: mix[:, c, E_V + n * HD:E_V + (n + 1) * HD]) for n in hs],
                    out_ap=mixed[:, t, 768 + 128 * j:896 + 128 * j].rearrange("p (n d) -> p n d", d=HD)))
        attend(groups, two_scores)

        heads = mixed[:, :, 768:1024].rearrange("p t (n d) -> p t n d", d=HD)
        v_value, r_value = var_ready.plan(), root_ready.plan()

        def diff_norm_dve(e):
            link = chains["dve"]
            sq = probs[:, 0, :, :].rearrange("p a b -> p (a b)")[:, 0:512].rearrange("p (t n d) -> p t n d", t=TILES, n=4)
            var, root, y, t1 = (stat[:, 8 * i:8 * i + 8] for i in range(4))
            for t in range(TILES):
                link.add(e.tensor_tensor(sq[:, t], heads[:, t], heads[:, t], ALU.mult))
            link.wait()
            link(e.tensor_reduce(var, sq.rearrange("p t n d -> p (t n) d"), AX.X, ALU.add))
            e.tensor_scalar(var, var, 1.0 / HD, EPS, ALU.mult, ALU.add).then_inc(var_ready.sem, 1)
            e.wait_ge(root_ready.sem, r_value)
            link(e.reciprocal(y, root))
            link(e.tensor_tensor(t1, y, y, ALU.mult))
            link(e.tensor_tensor(t1, t1, var, ALU.mult))
            link(e.tensor_scalar(t1, t1, -0.5, 1.5, ALU.mult, ALU.add))
            link(e.tensor_tensor(y, y, t1, ALU.mult))
            for t in range(TILES):
                link(e.tensor_tensor(heads[:, t], heads[:, t],
                                     y[:, 4 * t:4 * t + 4].unsqueeze(2).to_broadcast([P, 4, HD]), ALU.mult))
                link(e.tensor_tensor(heads[:, t], heads[:, t],
                                     diff_gain.unsqueeze(1).to_broadcast([P, 4, HD]), ALU.mult))

        def diff_norm_act(e):
            e.wait_ge(var_ready.sem, v_value)
            e.activation(stat[:, 8:16], stat[:, 0:8], ACT.Sqrt).then_inc(root_ready.sem, 1)

        stage(act=diff_norm_act, dve=diff_norm_dve)
        m_pair = T_quads[0:2], T_quads[2:4]
        turn_split(M, m_pair)

        w_in = rows_of(a["w_in_2"][0])
        w_branch = a["w_branch_2"][0]
        plan = []
        for n in range(4):
            for half in range(2):
                c0 = MIX + n * D + half * 512
                slots = [weights(w_in[:, k:k + 4, c0:c0 + 512], 4, 512) for k in (0, 4)]
                if half == 0:
                    branch = weights(rows_of(w_branch[n]), 2, D)
                at = 3 * len(plan)
                ms = [plan_split(s, 4, 0, 512, (at + i) % 4) for i, s in enumerate(slots)]
                ms.append(plan_split(branch, 2, half * 512, half * 512 + 512, (at + 2) % 4))
                ug = [products.take() for _ in range(TILES)]
                ub = [spare_banks.take() for _ in range(TILES)]
                split_back[ms[0]] = w_used.sem, w_used.plan()
                split_back[ms[1]], split_back[ms[2]] = ug[-1].full_at(), ub[-1].full_at()
                plan.append((n, half, ms, ug, ub, [relu_used.plan() if n else None for _ in range(TILES)]))
        gated = mixed

        def gate_pe(e):
            for n, half, ms, ug, ub, _ in plan:
                for i in range(2):
                    split_wait(e, ms[i])
                    right = halves_of(ms[i])
                    for t, u in enumerate(ug):
                        if i == 0:
                            u.wait_free(e)
                        for k in range(4):
                            last = product(e, u.ap, chunk_of(x_pair, 4 * i + k, t), [r[:, k, :] for r in right],
                                           4 * i + k == 0, 4 * i + k == DC - 1)
                        if i == 1:
                            last.then_inc(u.full, 1)
                    if i == 0:
                        last.then_inc(w_used.sem, 1)
                split_wait(e, ms[2])
                right = halves_of(ms[2])
                for t, u in enumerate(ub):
                    u.wait_free(e)
                    for k in range(2):
                        last = product(e, u.ap, chunk_of(m_pair, 2 * n + k, t), [r[:, k, :] for r in right],
                                       k == 0, k == 1)
                    last.then_inc(u.full, 1)

        def gate_splits(e, split, q, first):
            if q < len(plan):
                for m in (plan[q][2][0:1] if first else plan[q][2][1:]):
                    split(e, m)

        def gate_act(e):
            gate_splits(e, split_act, 0, True)
            gate_splits(e, split_act, 0, False)
            for q, (_, _, _, ug, _, _) in enumerate(plan):
                gate_splits(e, split_act, q + 1, True)
                for t, u in enumerate(ug):
                    if q:
                        ub, used = plan[q - 1][4][t], plan[q - 1][5][t]
                        if used is None:
                            ub.wait_emptied(e)
                        else:
                            e.wait_ge(relu_used.sem, used)
                    u.wait_full(e)
                    e.activation(gates[:, t, :], u.ap, ACT.Sigmoid).then_inc(u.free, 1)
                gate_splits(e, split_act, q + 1, False)

        def gate_dve(e):
            gate_splits(e, split_dve, 0, True)
            gate_splits(e, split_dve, 0, False)
            for q, (n, half, _, ug, ub, _) in enumerate(plan):
                gate_splits(e, split_dve, q + 1, True)
                for t in range(TILES):
                    ug[t].wait_emptied(e)
                    ub[t].wait_full(e)
                    g = gates[:, t, :]
                    y = gated[:, t, half * 512:half * 512 + 512]
                    if n == 0:
                        e.tensor_tensor(y, g, ub[t].ap, ALU.mult).then_inc(ub[t].free, 1)
                    else:
                        e.tensor_tensor(g, g, ub[t].ap, ALU.mult).then_inc(ub[t].free, 1)
                        ub[t].wait_emptied(e)
                        e.tensor_tensor(y, y, g, ALU.add).then_inc(relu_used.sem, 1)
                gate_splits(e, split_dve, q + 1, False)

        stage(pe=gate_pe, act=gate_act, dve=gate_dve)
        turn_split(M, x_pair)
        project_split(x_pair, a["w_out_2"][0], DC, D, add_residual, "dve", (0, 1, 2, 3))

        norm(X, H, D, a["mlp_norm_g_2"])
        hidden = T_quads, quads(tok_r[:, 0:32 * SEQ])
        low = tok_r[:, 32 * SEQ:40 * SEQ]
        mlp_pair = quads(hT_r[:, :]), quads(low)
        turn_split(H, mlp_pair)
        w_up = rows_of(a["w_up_2"][0])
        up_plan = []
        for b in range(8):
            slots = [weights(w_up[:, k:k + 4, b * 512:(b + 1) * 512], 4, 512) for k in (0, 4)]
            ms = [plan_split(s, 4, 0, 512, i) for i, s in enumerate(slots)]
            units = [products.take(), products.take(), spare_banks.take(), spare_banks.take()]
            split_back[ms[0]] = w_used.sem, w_used.plan()
            split_back[ms[1]] = units[-1].full_at()
            up_plan.append((ms, units, [squared.plan() for _ in units],
                            [turned_hi.plan() for _ in units]))
        units_2 = h[:, :, :].rearrange("p a b -> p (a b)").rearrange("p (n s) -> p n s", s=SEQ)

        def up_pe(e):
            for b, (ms, units, _, _) in enumerate(up_plan):
                for i, m in enumerate(ms):
                    split_wait(e, m)
                    left = halves_of(m)
                    for j, u in enumerate(units):
                        if i == 0:
                            u.wait_free(e)
                        for k in range(4):
                            last = product(e, u.ap[:, 0:SEQ], [w[:, k, j * P:(j + 1) * P] for w in left],
                                           chunk_of(mlp_pair, 4 * i + k), 4 * i + k == 0, 4 * i + k == DC - 1)
                        if i == 1:
                            last.then_inc(u.full, 1)
                    if i == 0:
                        last.then_inc(w_used.sem, 1)

        def up_act(e):
            split_act(e, up_plan[0][0][0])
            split_act(e, up_plan[0][0][1])
            for b, (_, units, sq_v, _) in enumerate(up_plan):
                if b + 1 < len(up_plan):
                    split_act(e, up_plan[b + 1][0][0])
                for j, u in enumerate(units):
                    u.wait_full(e)
                    e.activation(units_2[:, (4 * b + j) % 8, :], u.ap[:, 0:SEQ], ACT.Relu).then_inc(u.free, 1)
                for j in range(4):
                    e.wait_ge(squared.sem, sq_v[j])
                    e.copy(hidden[0][b][:, j, :], units_2[:, (4 * b + j) % 8, :]).then_inc(turned_hi.sem, 1)
                if b + 1 < len(up_plan):
                    split_act(e, up_plan[b + 1][0][1])

        def up_dve(e):
            split_dve(e, up_plan[0][0][0])
            split_dve(e, up_plan[0][0][1])
            for b, (_, units, _, hi_v) in enumerate(up_plan):
                if b + 1 < len(up_plan):
                    split_dve(e, up_plan[b + 1][0][0])
                for j, u in enumerate(units):
                    u.wait_emptied(e)
                    v = units_2[:, (4 * b + j) % 8, :]
                    e.tensor_tensor(v, v, v, ALU.mult).then_inc(squared.sem, 1)
                if b + 1 < len(up_plan):
                    split_dve(e, up_plan[b + 1][0][1])
                for j in range(4):
                    e.wait_ge(turned_hi.sem, hi_v[j])
                    e.tensor_tensor(hidden[1][b][:, j, :], units_2[:, (4 * b + j) % 8, :], hidden[0][b][:, j, :],
                                    ALU.subtract)

        stage(pe=up_pe, act=up_act, dve=up_dve)
        project_split(hidden, a["w_down_2"][0], 32, D, add_residual, "dve", (0, 1))
        norm(X, H, D, a["final_norm_g_2"])

        block = ctx.enter_context(nc.Block())

        @block.sync
        def _(sp):
            sp.dma_start(raw[:, 2:4].bitcast(I32), a["positions"]).then_inc(consts_landed, 16)
            sp.dma_start(small[:, 0:32], a["inv_freq"].to_broadcast([P, 32])).then_inc(consts_landed, 16)
            load_gain(sp, 0)
            sp.dma_start(x[:, :, :], a["x"].rearrange("(t p) d -> p t d", p=P)).then_inc(x_landed, 16)
            for n, (view, chunks, cols) in enumerate(stream):
                if n >= SLOTS:
                    sp.wait_ge(*given_back[n - SLOTS])
                sp.dma_start(slot_ap(n), view).then_inc(w_landed[n % SLOTS], 16)
            for t in range(TILES):
                sp.wait_ge(done["dve"], len(stages))
                sp.dma_start(out.rearrange("(t p) d -> p t d", p=P)[:, t, :], h[:, t, :]).then_inc(out_landed, 16)
            sp.wait_ge(out_landed, 16 * TILES)

        @block.gpsimd
        def _(pool):
            step = Chain(pool, pool_step)
            step.add(pool.memset(ident[:, :], 0.0))
            step(pool.memset(causal[:, :, :], 0.0))
            step.add(pool.affine_select(ident[:, :], ident[:, :], pattern=[[-1, P]], compare_op=ALU.not_equal,
                                        fill=1.0, base=0, channel_multiplier=1))
            step.add(pool.affine_select(causal[:, :, :], causal[:, :, :], pattern=[[P, TILES], [-1, SEQ]],
                                        compare_op=ALU.is_ge, fill=NEG, base=0, channel_multiplier=1))
            step(pool.iota(iota16[:, :], pattern=[[1, TOP]], base=0, channel_multiplier=0,
                           allow_small_or_imprecise_dtypes=True))
            pool.drain().then_inc(pool_made, 1)
            for n in range(len(gathers) * P + TOP):
                if n < len(gathers) * P:
                    _, t, ready = gathers[n // P]
                    if n % P == 0:
                        pool.wait_ge(experts_ready.sem, ready)
                    if n >= U_SLOTS:
                        pool.wait_ge(u_used.sem, n - U_SLOTS + 1)
                    pool.indirect_dma_start(
                        rows[:, n % U_SLOTS, :], None, a["peer_u"],
                        bass.IndirectOffsetOnAxis(ap=expert[:, t, n % P:n % P + 1], axis=0)
                    ).then_inc(u_landed[n % U_SLOTS], 16)
                m = n - TOP
                if m >= 0:
                    t = gathers[m // P][1]
                    if m >= V_SLOTS:
                        pool.wait_ge(v_used.sem, m - V_SLOTS + 1)
                    pool.indirect_dma_start(
                        rows[:, U_SLOTS + m % V_SLOTS, :], None, a["peer_v"],
                        bass.IndirectOffsetOnAxis(ap=expert[:, t, m % P:m % P + 1], axis=0)
                    ).then_inc(v_landed[m % V_SLOTS], 16)
            for e in ("dve", "act", "pe"):
                pool.wait_ge(done[e], masks_stage)
            step.add(pool.iota(dist, pattern=[[P, TILES], [-1, SEQ]], base=0, channel_multiplier=1,
                               allow_small_or_imprecise_dtypes=True))
            step(pool.memset(upper, 1.0))
            step(pool.affine_select(upper, upper, pattern=[[-P, TILES], [1, SEQ]], compare_op=ALU.is_ge, fill=0.0,
                                    base=0, channel_multiplier=-1))
            pool.dma_start(small[:, 0:4], a["b_forget_2"].to_broadcast([P, 4])).then_inc(last_landed, 16)
            pool.dma_start(small[:, 8:136], a["lambdas"].to_broadcast([P, 128])).then_inc(last_landed, 16)
            pool.dma_start(diff_gain, a["diff_norm_g_2"].to_broadcast([P, HD])).then_inc(last_landed, 16)
            pool.drain().then_inc(masks_made, 1)

        @block.scalar
        def _(act):
            chains["act"] = Chain(act, act_step)
            run_stages("act", act)

        @block.vector
        def _(dve):
            chains["dve"] = Chain(dve, dve_step)
            run_stages("dve", dve)

        @block.tensor
        def _(pe):
            run_stages("pe", pe)


INPUTS = ["x", "positions", "attn_norm", "ffn_norm", "final_norm", "hyb_w_in", "hyb_w_out", "mla_w_in", "mla_q_norm",
          "mla_kv_norm", "mla_w_uq", "mla_w_ukv", "mla_w_out", "peer_w_q", "peer_keys", "peer_u", "peer_v",
          "mix_norm_g_2", "w_in_2", "b_forget_2", "lambdas", "diff_norm_g_2", "w_branch_2", "w_out_2",
          "mlp_norm_g_2", "w_up_2", "w_down_2", "final_norm_g_2", "inv_freq"]


def kernel(**inputs):
    import concourse.bacc as bacc
    from concourse.bass_utils import run_bass_kernel_spmd

    got = {k: np.asarray(v) for k, v in inputs.items()}
    lambdas = [got.pop(f"lambda_{n}_2") for n in ("q1", "k1", "q2", "k2")]
    keys = got.pop("peer_sub_keys")
    layers = keys.shape[0]
    laid = got | {
        "x": got["x"].reshape(SEQ, D),
        "positions": got["positions"].reshape(TILES, P).T,
        "final_norm": got["final_norm"].reshape(1, D),
        "final_norm_g_2": got["final_norm_g_2"].reshape(1, D),
        "peer_u": got["peer_u"].reshape(-1, D),
        "peer_v": got["peer_v"].reshape(-1, D),
        "peer_keys": keys.transpose(0, 4, 1, 2, 3).reshape(layers, P, EH * 2 * NK),
        "lambdas": np.concatenate(lambdas, axis=1),
        "inv_freq": (1.0 / 10000.0 ** (np.arange(0, HD, 2, dtype=np.float32) / HD)).astype(np.float32).reshape(1, 32),
    }
    nc = bacc.Bacc("TRN2", target_bir_lowering=False, num_devices=1)
    arrays, a = {}, {}
    for name in INPUTS:
        v = np.ascontiguousarray(laid[name])
        arrays[f"in_{name}"] = v
        a[name] = nc.dram_tensor(f"in_{name}", v.shape, mybir.dt.from_np(v.dtype), kind="ExternalInput").ap()
    out = nc.dram_tensor("out_0", (SEQ, D), F32, kind="ExternalOutput").ap()
    build(nc, a, out)
    r = run_bass_kernel_spmd(nc, [arrays], core_ids=[0])
    return r.results[0]["out_0"].reshape(1, SEQ, D)
```
